# Optimizing a Trainium2 kernel written in Bass

```python
import math
import jax, jax.numpy as jnp
from jax import lax
import numpy as np

D_MODEL = 1024
BATCH = 1
SEQ = 256
DEPTH = 1

CHUNK = 64
Q_BLOCK = 128
EPS = 1e-6

FOX_HEADS = 4
FOX_DIM = 128
GDN_HEADS = 4
GDN_DK = 128
GDN_DV = 128
GDN_CONV = 4
SB_HEADS = 4
SB_DIM = 128
MEM_TOKENS = 256
MEM_HEADS = 4
MEM_DIM = 128
D_FF = 2816
FFN_CONV = 3
N_BRANCH = 3

FOX_W = FOX_HEADS * FOX_DIM
GDN_KW = GDN_HEADS * GDN_DK
GDN_VW = GDN_HEADS * GDN_DV
SB_W = SB_HEADS * SB_DIM
MEM_W = MEM_HEADS * MEM_DIM

IN_SPLITS = (
    FOX_W, FOX_W, FOX_W, FOX_HEADS,
    GDN_KW, GDN_KW, GDN_VW, GDN_HEADS, GDN_HEADS, GDN_VW,
    SB_W, SB_W, SB_W,
    N_BRANCH * D_MODEL,
)
N_IN = sum(IN_SPLITS)


def rmsnorm(x, g):
    xf = x.astype(jnp.float32)
    y = xf * lax.rsqrt(jnp.mean(xf * xf, axis=-1, keepdims=True) + EPS)
    return (y * g.astype(jnp.float32)).astype(x.dtype)

def l2norm(x):
    xf = x.astype(jnp.float32)
    return xf * lax.rsqrt(jnp.sum(xf * xf, axis=-1, keepdims=True) + EPS)

def heads(x, n):
    return x.reshape(x.shape[:-1] + (n, -1))

def causal_dwconv(x, w):
    width, ch = w.shape
    return lax.conv_general_dilated(
        x, w[:, None, :].astype(x.dtype), window_strides=(1,), padding=[(width - 1, 0)],
        dimension_numbers=("NWC", "WIO", "NWC"), feature_group_count=ch)

def split_projection(p):
    points = [int(s) for s in np.cumsum(IN_SPLITS)[:-1]]
    return jnp.split(p, points, axis=-1)

def fox_attention(q, k, v, logf):
    B, S, H, dh = q.shape
    c = jnp.cumsum(logf, axis=1).transpose(0, 2, 1)
    qh = q.transpose(0, 2, 1, 3)
    kh = k.transpose(0, 2, 1, 3)
    vh = v.transpose(0, 2, 1, 3)
    scale = dh ** -0.5
    outs = []
    for i in range(S // Q_BLOCK):
        lo, hi = i * Q_BLOCK, (i + 1) * Q_BLOCK
        s = (jnp.einsum("bhqd,bhkd->bhqk", qh[:, :, lo:hi], kh[:, :, :hi]).astype(jnp.float32) * scale
             + (c[:, :, lo:hi, None] - c[:, :, None, :hi]))
        mask = jnp.arange(hi)[None, :] <= jnp.arange(lo, hi)[:, None]
        p = jax.nn.softmax(jnp.where(mask, s, -jnp.inf), axis=-1).astype(vh.dtype)
        outs.append(jnp.einsum("bhqk,bhkd->bhqd", p, vh[:, :, :hi]))
    o = jnp.concatenate(outs, axis=2)
    return o.transpose(0, 2, 1, 3).reshape(B, S, H * dh)

def stick_breaking_attention(q, k, v):
    B, S, H, dh = q.shape
    qh = q.transpose(0, 2, 1, 3)
    kh = k.transpose(0, 2, 1, 3)
    vh = v.transpose(0, 2, 1, 3)
    scale = dh ** -0.5
    idx = jnp.arange(Q_BLOCK)
    tri_in = (idx[:, None] >= idx[None, :]).astype(jnp.float32)
    outs = []
    for i in range(S // Q_BLOCK):
        lo, hi = i * Q_BLOCK, (i + 1) * Q_BLOCK
        nk = i + 1
        z = jnp.einsum("bhqd,bhkd->bhqk", qh[:, :, lo:hi], kh[:, :, :hi]).astype(jnp.float32) * scale
        mask = jnp.arange(hi)[None, :] < jnp.arange(lo, hi)[:, None]
        log_keep = jnp.where(mask, -jax.nn.softplus(z), 0.0)
        lk = log_keep.reshape(B, H, Q_BLOCK, nk, Q_BLOCK)
        within = jnp.einsum("bhqnj,jk->bhqnk", lk, tri_in)
        tot = jnp.sum(lk, axis=-1)
        blk = jnp.arange(nk)
        tri_blk = (blk[:, None] > blk[None, :]).astype(jnp.float32)
        after = jnp.einsum("bhqm,mn->bhqn", tot, tri_blk)
        rc = (within + after[..., None]).reshape(B, H, Q_BLOCK, hi)
        a = jnp.exp(jnp.where(mask, z + rc, -jnp.inf)).astype(vh.dtype)
        outs.append(jnp.einsum("bhqk,bhkd->bhqd", a, vh[:, :, :hi]))
    o = jnp.concatenate(outs, axis=2)
    return o.transpose(0, 2, 1, 3).reshape(B, S, H * dh)

def gated_delta_rule(q, k, v, g, beta):
    B, T, H, dk = q.shape
    dv = v.shape[-1]
    N = T // CHUNK
    f32 = jnp.float32

    def chunks(a):
        a = a.astype(f32).reshape((B, N, CHUNK, H) + a.shape[3:])
        return jnp.moveaxis(a, (1, 3), (0, 2))

    qc = chunks(q) * dk ** -0.5
    kc = chunks(k)
    vc = chunks(v)
    bc = chunks(beta)
    gc = jnp.cumsum(chunks(g), axis=-1)
    idx = jnp.arange(CHUNK)
    causal = idx[:, None] >= idx[None, :]
    strict = idx[:, None] > idx[None, :]
    decay = jnp.exp(jnp.where(causal, gc[..., :, None] - gc[..., None, :], -jnp.inf))
    kk = jnp.einsum("nbhcd,nbhed->nbhce", kc, kc)
    a_mat = jnp.where(strict, bc[..., :, None] * kk * decay, 0.0) + jnp.eye(CHUNK, dtype=f32)
    rhs = jnp.concatenate([vc * bc[..., None], kc * (bc * jnp.exp(gc))[..., None]], axis=-1)
    sol = lax.linalg.triangular_solve(a_mat, rhs, left_side=True, lower=True)
    u, w = sol[..., :dv], sol[..., dv:]
    attn = jnp.where(causal, jnp.einsum("nbhcd,nbhed->nbhce", qc, kc) * decay, 0.0)
    g_last = gc[..., -1]
    k_tail = kc * jnp.exp(g_last[..., None] - gc)[..., None]

    def step(state, xs):
        q_n, u_n, w_n, g_n, attn_n, kt_n, gl_n = xs
        v_new = u_n - jnp.einsum("bhck,bhkv->bhcv", w_n, state)
        o = (jnp.einsum("bhck,bhkv->bhcv", q_n * jnp.exp(g_n)[..., None], state)
             + jnp.einsum("bhce,bhev->bhcv", attn_n, v_new))
        state = state * jnp.exp(gl_n)[..., None, None] + jnp.einsum("bhck,bhcv->bhkv", kt_n, v_new)
        return state, o

    s0 = jnp.zeros((B, H, dk, dv), f32)
    _, o = lax.scan(step, s0, (qc, u, w, gc, attn, k_tail, g_last))
    return jnp.moveaxis(o, (0, 2), (1, 3)).reshape(B, T, H, dv)

def memory_cross_attention(h, m, w_q, w_kv, q_g, k_g, w_o):
    B, S, _ = h.shape
    q = rmsnorm(heads(h @ w_q, MEM_HEADS), q_g)
    k, v = jnp.split(m @ w_kv, 2, axis=-1)
    k = rmsnorm(heads(k, MEM_HEADS), k_g)
    v = heads(v, MEM_HEADS)
    s = jnp.einsum("bqhd,bkhd->bhqk", q, k).astype(jnp.float32) * MEM_DIM ** -0.5
    p = jax.nn.softmax(s, axis=-1).astype(v.dtype)
    o = jnp.einsum("bhqk,bkhd->bqhd", p, v).reshape(B, S, MEM_W)
    return o @ w_o

def conv_ffn(h, w_up, conv_w, conv_b, w_down):
    u = causal_dwconv(h @ w_up, conv_w) + conv_b
    a, b = jnp.split(u, 2, axis=-1)
    return (jax.nn.silu(a) * b) @ w_down

def first_inputs(seed: int = 0) -> dict:
    key = jax.random.key(seed)
    ks = iter(jax.random.split(key, 40))
    L, D = DEPTH, D_MODEL
    f32 = jnp.float32

    def nrm(shape, scale):
        return jax.random.normal(next(ks), shape, f32) * scale

    def gain(shape):
        return 1.0 + 0.02 * jax.random.normal(next(ks), shape, f32)

    x = nrm((BATCH, SEQ, D), 1.0)
    mem = nrm((BATCH, MEM_TOKENS, D), 1.0)
    norm_mix = gain((L, D))
    w_in = nrm((L, D, N_IN), D ** -0.5)
    fox_fbias = jax.random.uniform(next(ks), (L, FOX_HEADS), f32, minval=1.0, maxval=5.0)
    fox_qnorm = gain((L, FOX_DIM))
    fox_knorm = gain((L, FOX_DIM))
    gdn_conv = nrm((L, GDN_CONV, 2 * GDN_KW + GDN_VW), GDN_CONV ** -0.5)
    gdn_a_log = jnp.log(jax.random.uniform(next(ks), (L, GDN_HEADS), f32, minval=1.0, maxval=16.0))
    dt = jnp.exp(jax.random.uniform(next(ks), (L, GDN_HEADS), f32,
                                    minval=math.log(1e-3), maxval=math.log(1e-1)))
    gdn_dt_bias = dt + jnp.log(-jnp.expm1(-dt))
    gdn_onorm = gain((L, GDN_DV))
    gate_bias = nrm((L, N_BRANCH * D), 0.01)
    w_oa = nrm((L, FOX_W, D), FOX_W ** -0.5)
    w_ob = nrm((L, GDN_VW, D), GDN_VW ** -0.5)
    w_oc = nrm((L, SB_W, D), SB_W ** -0.5)
    w_out = nrm((L, D, D), D ** -0.5)
    norm_xq = gain((L, D))
    norm_mem = gain((L, D))
    w_mq = nrm((L, D, MEM_W), D ** -0.5)
    w_mkv = nrm((L, D, 2 * MEM_W), D ** -0.5)
    mq_norm = gain((L, MEM_DIM))
    mk_norm = gain((L, MEM_DIM))
    w_mo = nrm((L, MEM_W, D), MEM_W ** -0.5)
    norm_ffn = gain((L, D))
    w_up = nrm((L, D, 2 * D_FF), D ** -0.5)
    ffn_conv = nrm((L, FFN_CONV, 2 * D_FF), FFN_CONV ** -0.5)
    ffn_conv_b = nrm((L, 2 * D_FF), 0.01)
    w_down = nrm((L, D_FF, D), D_FF ** -0.5)
    return {
        "x": x, "mem": mem, "norm_mix": norm_mix, "w_in": w_in,
        "fox_fbias": fox_fbias, "fox_qnorm": fox_qnorm, "fox_knorm": fox_knorm,
        "gdn_conv": gdn_conv, "gdn_a_log": gdn_a_log, "gdn_dt_bias": gdn_dt_bias,
        "gdn_onorm": gdn_onorm, "gate_bias": gate_bias,
        "w_oa": w_oa, "w_ob": w_ob, "w_oc": w_oc, "w_out": w_out,
        "norm_xq": norm_xq, "norm_mem": norm_mem, "w_mq": w_mq, "w_mkv": w_mkv,
        "mq_norm": mq_norm, "mk_norm": mk_norm, "w_mo": w_mo,
        "norm_ffn": norm_ffn, "w_up": w_up, "ffn_conv": ffn_conv,
        "ffn_conv_b": ffn_conv_b, "w_down": w_down,
    }

def first_block(x, mem, norm_mix, w_in, fox_fbias, fox_qnorm, fox_knorm, gdn_conv, gdn_a_log,
              gdn_dt_bias, gdn_onorm, gate_bias, w_oa, w_ob, w_oc, w_out, norm_xq, norm_mem,
              w_mq, w_mkv, mq_norm, mk_norm, w_mo, norm_ffn, w_up, ffn_conv, ffn_conv_b, w_down):
    B, S, D = x.shape
    f32 = jnp.float32
    for l in range(DEPTH):
        h = rmsnorm(x, norm_mix[l])
        (fq, fk, fv, ff, gq, gk, gv, gb, ga, gz, sq, sk, sv, gates) = split_projection(h @ w_in[l])

        fq = rmsnorm(heads(fq, FOX_HEADS), fox_qnorm[l])
        fk = rmsnorm(heads(fk, FOX_HEADS), fox_knorm[l])
        logf = jax.nn.log_sigmoid((ff + fox_fbias[l]).astype(f32))
        ya = fox_attention(fq, fk, heads(fv, FOX_HEADS), logf)

        qkv = jax.nn.silu(causal_dwconv(jnp.concatenate([gq, gk, gv], axis=-1), gdn_conv[l]))
        cq, ck, cv = jnp.split(qkv, [GDN_KW, 2 * GDN_KW], axis=-1)
        beta = jax.nn.sigmoid(gb.astype(f32))
        g_log = -jnp.exp(gdn_a_log[l].astype(f32)) * jax.nn.softplus((ga + gdn_dt_bias[l]).astype(f32))
        o = gated_delta_rule(l2norm(heads(cq, GDN_HEADS)), l2norm(heads(ck, GDN_HEADS)),
                             heads(cv, GDN_HEADS), g_log, beta)
        yb = (rmsnorm(o, gdn_onorm[l]) * jax.nn.silu(heads(gz, GDN_HEADS).astype(f32)))
        yb = yb.astype(x.dtype).reshape(B, S, GDN_VW)

        yc = stick_breaking_attention(heads(sq, SB_HEADS), heads(sk, SB_HEADS), heads(sv, SB_HEADS))

        g = jax.nn.sigmoid((gates + gate_bias[l]).astype(f32)).astype(x.dtype).reshape(B, S, N_BRANCH, D)
        mixed = (g[..., 0, :] * (ya @ w_oa[l]) + g[..., 1, :] * (yb @ w_ob[l])
                 + g[..., 2, :] * (yc @ w_oc[l]))
        x = x + mixed @ w_out[l]

        x = x + memory_cross_attention(rmsnorm(x, norm_xq[l]), rmsnorm(mem, norm_mem[l]),
                                       w_mq[l], w_mkv[l], mq_norm[l], mk_norm[l], w_mo[l])

        x = x + conv_ffn(rmsnorm(x, norm_ffn[l]), w_up[l], ffn_conv[l], ffn_conv_b[l], w_down[l])
    return x


D_PLE = 256
D_GMLP = D_MODEL
N_SGU_GROUPS = 4
CHUNK_2 = 128
D_POOL = D_MODEL
POOL_WINDOWS = (2, 4, 8, 16)
N_POOL_GROUPS = len(POOL_WINDOWS)
D_IN = 2 * D_GMLP + D_POOL + 2 * D_MODEL


def _rmsnorm(x, g):
    xf = x.astype(jnp.float32)
    y = xf * lax.rsqrt(jnp.mean(xf * xf, axis=-1, keepdims=True) + EPS)
    return (y * g.astype(jnp.float32)).astype(x.dtype)

def _layernorm(x, g):
    xf = x.astype(jnp.float32)
    mu = jnp.mean(xf, axis=-1, keepdims=True)
    xc = xf - mu
    y = xc * lax.rsqrt(jnp.mean(xc * xc, axis=-1, keepdims=True) + EPS)
    return (y * g.astype(jnp.float32)).astype(x.dtype)

def _swiglu(xn, w_gate, w_up, w_down):
    return (jax.nn.silu(xn @ w_gate) * (xn @ w_up)) @ w_down

def _spatial_gating(u, v, norm_g, w_s, b_s):
    B, S, _ = v.shape
    dg = D_GMLP // N_SGU_GROUPS
    v = _layernorm(v, norm_g)
    vc = v.reshape(B, S // CHUNK_2, CHUNK_2, N_SGU_GROUPS, dg)
    causal = jnp.tril(jnp.ones((CHUNK_2, CHUNK_2), dtype=bool))
    ws = jnp.where(causal[None], w_s, 0.0).astype(v.dtype)
    sv = jnp.einsum('gts,bcsgd->bctgd', ws, vc) + b_s.T[:, :, None].astype(v.dtype)
    return u * sv.reshape(B, S, D_GMLP)

def _pool_mixer(c, pool_w, pool_scale):
    B, S, _ = c.shape
    dg = D_POOL // N_POOL_GROUPS
    cf = c.astype(jnp.float32)
    cs = jnp.concatenate([jnp.zeros((B, 1, D_POOL), jnp.float32), jnp.cumsum(cf, axis=1)], axis=1)
    t = jnp.arange(S)
    outs = []
    for gi, w in enumerate(POOL_WINDOWS):
        lo = jnp.maximum(t + 1 - w, 0)
        sl = slice(gi * dg, (gi + 1) * dg)
        csg = cs[:, :, sl]
        count = (t + 1 - lo).astype(jnp.float32)[None, :, None]
        mean = (csg[:, 1:] - csg[:, lo]) / count
        diff = (mean - cf[:, :, sl]).astype(c.dtype)
        outs.append(jnp.einsum('bsc,cd->bsd', diff, pool_w[gi]))
    return jnp.concatenate(outs, axis=-1) * pool_scale

def _token_mixer(xn, w_in, sgu_norm_g, sgu_w, sgu_b, pool_w, pool_scale, w_out_a, w_out_b, w_o):
    z = xn @ w_in
    i1 = D_GMLP
    i2 = 2 * D_GMLP
    i3 = i2 + D_POOL
    i4 = i3 + D_MODEL
    u = jax.nn.gelu(z[..., :i1])
    v = jax.nn.gelu(z[..., i1:i2])
    c = z[..., i2:i3]
    ga = z[..., i3:i4]
    gb = z[..., i4:]
    a = _spatial_gating(u, v, sgu_norm_g, sgu_w, sgu_b)
    b = _pool_mixer(c, pool_w, pool_scale)
    y = jax.nn.sigmoid(ga) * (a @ w_out_a) + jax.nn.sigmoid(gb) * (b @ w_out_b)
    return y @ w_o

def _gain(k, shape):
    return 1.0 + 0.02 * jax.random.normal(k, shape, jnp.float32)

def _w(k, shape, fan_in):
    return jax.random.normal(k, shape, jnp.float32) * (fan_in ** -0.5)

def second_inputs(seed: int = 0) -> dict:
    key = jax.random.key(seed)
    ks = jax.random.split(key, 32)
    L = DEPTH
    dgp = D_POOL // N_POOL_GROUPS
    return {
        "x": jax.random.normal(ks[0], (BATCH, SEQ, D_MODEL), jnp.float32),
        "p": jax.random.normal(ks[1], (DEPTH, BATCH, SEQ, D_PLE), jnp.float32),
        "ffn1_pre_g": _gain(ks[2], (L, D_MODEL)),
        "ffn1_w_gate": _w(ks[3], (L, D_MODEL, D_FF), D_MODEL),
        "ffn1_w_up": _w(ks[4], (L, D_MODEL, D_FF), D_MODEL),
        "ffn1_w_down": _w(ks[5], (L, D_FF, D_MODEL), D_FF),
        "ffn1_post_g": _gain(ks[6], (L, D_MODEL)),
        "mix_pre_g": _gain(ks[7], (L, D_MODEL)),
        "w_in": _w(ks[8], (L, D_MODEL, D_IN), D_MODEL),
        "sgu_norm_g": _gain(ks[9], (L, D_GMLP)),
        "sgu_w": _w(ks[10], (L, N_SGU_GROUPS, CHUNK_2, CHUNK_2), CHUNK_2),
        "sgu_b": _gain(ks[11], (L, N_SGU_GROUPS, CHUNK_2)),
        "pool_w": _w(ks[12], (L, N_POOL_GROUPS, dgp, dgp), dgp),
        "pool_scale": _gain(ks[13], (L, D_POOL)),
        "w_out_a": _w(ks[14], (L, D_GMLP, D_MODEL), D_GMLP),
        "w_out_b": _w(ks[15], (L, D_POOL, D_MODEL), D_POOL),
        "w_o": _w(ks[16], (L, D_MODEL, D_MODEL), D_MODEL),
        "mix_post_g": _gain(ks[17], (L, D_MODEL)),
        "ffn2_pre_g": _gain(ks[18], (L, D_MODEL)),
        "ffn2_w_gate": _w(ks[19], (L, D_MODEL, D_FF), D_MODEL),
        "ffn2_w_up": _w(ks[20], (L, D_MODEL, D_FF), D_MODEL),
        "ffn2_w_down": _w(ks[21], (L, D_FF, D_MODEL), D_FF),
        "ffn2_post_g": _gain(ks[22], (L, D_MODEL)),
        "ple_pre_g": _gain(ks[23], (L, D_MODEL)),
        "ple_w_gate": _w(ks[24], (L, D_MODEL, D_MODEL), D_MODEL),
        "ple_w_proj": _w(ks[25], (L, D_PLE, D_MODEL), D_PLE),
        "ple_post_g": _gain(ks[26], (L, D_MODEL)),
    }

def second_block(x, p, ffn1_pre_g, ffn1_w_gate, ffn1_w_up, ffn1_w_down, ffn1_post_g,
              mix_pre_g, w_in, sgu_norm_g, sgu_w, sgu_b, pool_w, pool_scale,
              w_out_a, w_out_b, w_o, mix_post_g,
              ffn2_pre_g, ffn2_w_gate, ffn2_w_up, ffn2_w_down, ffn2_post_g,
              ple_pre_g, ple_w_gate, ple_w_proj, ple_post_g):
    h = x
    for i in range(DEPTH):
        f = _swiglu(_rmsnorm(h, ffn1_pre_g[i]), ffn1_w_gate[i], ffn1_w_up[i], ffn1_w_down[i])
        h = h + 0.5 * _rmsnorm(f, ffn1_post_g[i])
        m = _token_mixer(_rmsnorm(h, mix_pre_g[i]), w_in[i], sgu_norm_g[i], sgu_w[i], sgu_b[i],
                         pool_w[i], pool_scale[i], w_out_a[i], w_out_b[i], w_o[i])
        h = h + _rmsnorm(m, mix_post_g[i])
        f = _swiglu(_rmsnorm(h, ffn2_pre_g[i]), ffn2_w_gate[i], ffn2_w_up[i], ffn2_w_down[i])
        h = h + 0.5 * _rmsnorm(f, ffn2_post_g[i])
        gate = jax.nn.sigmoid(_rmsnorm(h, ple_pre_g[i]) @ ple_w_gate[i])
        e = p[i] @ ple_w_proj[i]
        h = h + _rmsnorm(gate * e, ple_post_g[i])
    return h


def setup_inputs(seed=0):
    out = dict(first_inputs(seed))
    for name, value in second_inputs(seed + 1).items():
        if name != "x":
            out[name + "_2"] = value
    return out


def reference(
    x, mem, norm_mix, w_in, fox_fbias, fox_qnorm, fox_knorm, gdn_conv, gdn_a_log, gdn_dt_bias,
    gdn_onorm, gate_bias, w_oa, w_ob, w_oc, w_out, norm_xq, norm_mem, w_mq, w_mkv, mq_norm,
    mk_norm, w_mo, norm_ffn, w_up, ffn_conv, ffn_conv_b, w_down, p_2, ffn1_pre_g_2,
    ffn1_w_gate_2, ffn1_w_up_2, ffn1_w_down_2, ffn1_post_g_2, mix_pre_g_2, w_in_2, sgu_norm_g_2,
    sgu_w_2, sgu_b_2, pool_w_2, pool_scale_2, w_out_a_2, w_out_b_2, w_o_2, mix_post_g_2,
    ffn2_pre_g_2, ffn2_w_gate_2, ffn2_w_up_2, ffn2_w_down_2, ffn2_post_g_2, ple_pre_g_2,
    ple_w_gate_2, ple_w_proj_2, ple_post_g_2,
):
    x = first_block(
        x, mem, norm_mix, w_in, fox_fbias, fox_qnorm, fox_knorm, gdn_conv, gdn_a_log,
        gdn_dt_bias, gdn_onorm, gate_bias, w_oa, w_ob, w_oc, w_out, norm_xq, norm_mem, w_mq,
        w_mkv, mq_norm, mk_norm, w_mo, norm_ffn, w_up, ffn_conv, ffn_conv_b, w_down,
    )
    return second_block(
        x, p_2, ffn1_pre_g_2, ffn1_w_gate_2, ffn1_w_up_2, ffn1_w_down_2, ffn1_post_g_2,
        mix_pre_g_2, w_in_2, sgu_norm_g_2, sgu_w_2, sgu_b_2, pool_w_2, pool_scale_2, w_out_a_2,
        w_out_b_2, w_o_2, mix_post_g_2, ffn2_pre_g_2, ffn2_w_gate_2, ffn2_w_up_2, ffn2_w_down_2,
        ffn2_post_g_2, ple_pre_g_2, ple_w_gate_2, ple_w_proj_2, ple_post_g_2,
    )


_drawn_inputs = setup_inputs


def setup_inputs(seed=0):
    import zlib

    import numpy as np

    out = dict(_drawn_inputs(seed))
    spreads = {}
    factors = {'norm_mix': 3.446,
     'fox_qnorm': 8.0,
     'fox_knorm': 8.0,
     'gdn_onorm': 7.401,
     'gate_bias': 8.0,
     'norm_xq': 8.0,
     'norm_mem': 8.0,
     'mq_norm': 8.0,
     'mk_norm': 8.0,
     'norm_ffn': 11.96,
     'ffn_conv_b': 23.496,
     'ffn1_pre_g_2': 161.339,
     'ffn1_post_g_2': 200.0,
     'mix_pre_g_2': 31.103,
     'sgu_norm_g_2': 200.0,
     'sgu_b_2': 200.0,
     'pool_scale_2': 200.0,
     'mix_post_g_2': 200.0,
     'ffn2_pre_g_2': 200.0,
     'ffn2_post_g_2': 200.0,
     'ple_pre_g_2': 183.742,
     'ple_post_g_2': 200.0}
    for name, (base, spread) in spreads.items():
        noise = np.random.default_rng([zlib.crc32(name.encode()), seed]).standard_normal(out[name].shape)
        drawn = base * np.exp(spread * noise) if base else spread * noise
        out[name] = __import__('jax').numpy.asarray(drawn.astype(out[name].dtype))
    for name, factor in factors.items():
        out[name] = (out[name] * factor).astype(out[name].dtype)
    return out
```

```python
from contextlib import ExitStack

import concourse.bass as bass
from concourse import mybir

P = 128
SEQ = 256
NT = SEQ // P
DM = 1024
KT = DM // P
HEADS = 4
DH = 128
HW = HEADS * DH
DFF = 2816
FT = DFF // P
BLOCK = 2048
RAWS = 2
RING = 4
EPS = 1e-6
BIG = 1e30
POOL_WINDOWS = (2, 4, 8, 16)

C_FQ, C_FK, C_FV, C_FF = 0, HW, 2 * HW, 3 * HW
C_GQKV = C_FF + HEADS
C_GB = C_GQKV + 3 * HW
C_GZ = C_GB + 2 * HEADS
C_SQ = C_GZ + HW
C_SK, C_SV = C_SQ + HW, C_SQ + 2 * HW
C_GATE = C_SQ + 3 * HW

PHASES = [
    ("gdn", 6), ("sbqk", 4), ("sbv", 2), ("foxqk", 4), ("foxv", 2),
    ("gate_c", 4), ("out_c", 2), ("gate_a", 4), ("out_a", 2), ("gz", 2), ("gate_b", 4), ("out_b", 2),
    ("w_out", 4), ("mem_k", 2), ("mem_q", 2), ("mem_v", 2), ("mem_o", 2),
    ("up", 22), ("down", 11),
    ("ffn1", 22), ("down1", 11),
    ("mix_v", 4), ("mix_u", 4), ("mix_c", 4), ("mix_ga", 4), ("mix_gb", 4), ("pool", 1), ("mix_out", 8), ("mix_o", 4),
    ("ffn2", 22), ("down2", 11),
    ("ple_e", 1), ("ple_g", 4),
]
FIRST = {}
_n = 0
for _name, _count in PHASES:
    FIRST[_name] = _n
    _n += _count
N_BLOCKS = _n
COUNT = dict(PHASES)

TILED = {"w_out": 3, "mem_o": 2, "down": 3, "down1": 3, "mix_o": 3, "down2": 3}
OPEN = 3
AFTER = {"w_out": "norm_xq", "mem_o": "norm_ffn", "down": "norm_f1", "down1": "norm_mix2", "mix_o": "norm_f2", "down2": "norm_ple"}
ON_POOL = {FIRST[d] + COUNT[d] + j for d in TILED for j in (1, 2)} | {FIRST["mem_o"], FIRST["mem_o"] + 1, FIRST["up"]}

ACC_BANKS, ACC_LAST, ACC_TURN = {}, {}, {}


PAIRS = ("up", "ffn1", "ffn2")


def _accumulations():
    turns = [0] * 4

    def acc(phase, j, last, *banks):
        ACC_BANKS[phase, j] = banks
        ACC_LAST[phase, j] = FIRST[phase] + last
        ACC_TURN[phase, j] = {b: turns[b] for b in banks}
        for b in banks:
            turns[b] += 1

    for phase, count in PHASES:
        if phase in ("sbv", "foxqk", "foxv", "mem_k", "mem_q", "mem_v", "mix_v", "ple_g"):
            for j in range(count // 2):
                first = 2 * ((j + (phase == "mem_q")) % 2)
                acc(phase, j, 2 * j + 1, first, first + 1)
        elif phase.startswith("out_"):
            for j in range(count):
                acc(phase, j, j, 2 * j, 2 * j + 1)
        elif phase in ("w_out", "mem_o", "down", "down1", "mix_o", "down2", "ple_e"):
            acc(phase, 0, count - 1, 0, 1, 2, 3)
        elif phase == "pool":
            for j in range(4):
                acc(phase, j, 0, j)
        else:
            for j in range(count):
                acc(phase, j, j, (j + (phase in PAIRS) * 2) % 4)


_accumulations()

def norm_turns(r):
    return [f"{r}.{t}{b}" for t in range(NT) for b in range(2)]


SMALL = norm_turns("norm_mix") + ["cols0", "cols1", "cols2", "tiny"]
SMALL += ["gTq0", "gTq1", "gTk0", "gTk1", "gTv0", "gTv1", "gcol", "grow0", "grow1", "gFq0", "gFq1", "gFk0", "gFk1"]
SMALL += ["kk0", "kk1", "kq0", "kq1", "z0", "z1", "z2", "z3", "Dt0", "Dt1", "D2_0", "D2_1", "D2t_0", "D2t_1"]
SMALL += ["P2_0", "P2_1", "D4_0", "D4_1", "D4t_0", "D4t_1", "rc0", "rc1", "rc2", "rc3", "P4_0", "P4_1"]
SMALL += ["D8_0", "D8_1", "P8_0", "P8_1", "so0", "so1", "T16_0", "T16_1", "fTq0", "fTq1", "fTk0", "fTk1"]
SMALL += ["Z16_0", "Z16_1", "Tt32_0", "Tt32_1", "T32_0", "T32_1", "fS0", "fS1a", "fS1b", "Z32_0", "Z32_1"]
SMALL += ["Tt64_0", "Tt64_1", "T64_0", "T64_1", "fP0", "fP1a", "fP1b", "fo0", "fo1", "Z64_0", "Z64_1"]
SMALL += ["Tt128_0", "Tt128_1", "vn0", "S1", "kS", "qS", "vn1", "o0", "o1", "yT0", "yT1"]
SMALL += norm_turns("norm_mem") + norm_turns("norm_xq")
SMALL += ["mkT0", "mkT1", "mqT0", "mqT1", "mS0a", "mS0b", "mS1a", "mS1b", "mP0a", "mP0b", "mP1a", "mP1b", "mo0", "mo1"]
SMALL += norm_turns("norm_ffn") + norm_turns("norm_f1")
SMALL += norm_turns("norm_mix2") + ["sguw"] + [f"sgu{g}" for g in range(4)]
SMALL += norm_turns("norm_f2") + ["pT"] + norm_turns("norm_ple")
SMALL_ORDER = {name: i for i, name in enumerate(SMALL)}

NORMS = ["norm_mix", "norm_mem", "norm_xq", "norm_ffn", "norm_f1", "norm_mix2", "norm_f2", "norm_ple"]
NORM_GAIN = dict(zip(NORMS, ["norm_mix", "norm_mem", "norm_xq", "norm_ffn", "ffn1_pre_g_2", "mix_pre_g_2",
                             "ffn2_pre_g_2", "ple_pre_g_2"]))

COL_ROWS = [
    [("sgu_norm_g_2", 8), ("pool_scale_2", 8), ("fox_qnorm", 1), ("fox_knorm", 1), ("mq_norm", 1), ("mk_norm", 1),
     ("gdn_onorm", 1), ("gate_bias", 24)],
    [("gdn_conv", 48), ("ffn_conv_b", 44)],
]
COL_AT = {}
for _tile, _names in enumerate(COL_ROWS):
    _row = 0
    for _name, _count in _names:
        COL_AT[_name] = (_tile, _row)
        _row += _count
COL_N = [sum(n for _, n in names) for names in COL_ROWS]
CONV_N = 3 * 2 * FT
CONV_TAIL = CONV_N - P
N_ROW_LOADS = sum(len(names) for names in COL_ROWS) + 2


def build(nc, A, out):
    f32, f32r, i32 = mybir.dt.float32, mybir.dt.float32r, mybir.dt.int32
    ALU = mybir.AluOpType
    ACT = mybir.ActivationFunctionType
    AX = mybir.AxisListType.X

    w = {k: A[k][0] for k in ("w_in", "w_oa", "w_ob", "w_oc", "w_out", "w_mq", "w_mkv", "w_mo", "w_up", "w_down",
                              "ffn1_w_gate_2", "ffn1_w_up_2", "ffn1_w_down_2", "w_in_2", "w_out_a_2", "w_out_b_2",
                              "w_o_2", "ffn2_w_gate_2", "ffn2_w_up_2", "ffn2_w_down_2", "ple_w_gate_2", "ple_w_proj_2")}

    def rows(m, k0, kn, c, cn):
        return m[k0 * P:(k0 + kn) * P, bass.ds(c, cn)].rearrange("(k p) n -> p k n", p=P)

    def f_block(m, c):
        return rows(m, 0, KT, c, 256)

    def t_block(m, c, half):
        return rows(m, 4 * half, 4, c, 512)

    def d_block(m, j):
        return m[bass.ds(j * 256, 256), :].rearrange("(k p) n -> p k n", p=P)

    ctx = ExitStack()
    with ctx:
        def sb(name, shape, dt=f32):
            return ctx.enter_context(nc.sbuf_tensor(name, shape, dt))

        def sem(name):
            return ctx.enter_context(nc.semaphore(name))

        RAW = sb("RAW", [P, RAWS, BLOCK])
        HI = sb("HI", [P, RING, BLOCK], f32r)
        LO = sb("LO", [P, RING, BLOCK], f32r)
        XH = sb("XH", [P, KT, SEQ], f32r)
        XL = sb("XL", [P, KT, SEQ], f32r)
        X = sb("X", [P, NT, DM])
        XS = sb("XS", [P, NT, DM])
        COL = [sb(f"COL{i}", [P, n]) for i, n in enumerate(COL_N)]
        FCONV = sb("FCONV", [P, CONV_N])
        IDENT = sb("IDENT", [P, P])
        UPTO = sb("UPTO", [P, 2, P])
        FROM = sb("FROM", [P, P])
        NEG_AFTER = sb("NEG_AFTER", [P, P])
        BIG_NOT_BEFORE = sb("BIG_NOT_BEFORE", [P, P])
        BEFORE = sb("BEFORE", [P, P])
        DIAG16 = sb("DIAG16", [P, P])
        LEVEL = {b: sb(f"LEVEL{b}", [P, P]) for b in (16, 32, 64)}
        KEEP = sb("KEEP", [P, 1])
        ONES = UPTO[:, 1, :]
        TRI = UPTO[:, 0, :]
        STAT = sb("STAT", [P, 288])
        stat_at = [0]

        def stat(n):
            stat_at[0] += n
            return STAT[:, stat_at[0] - n:stat_at[0]]

        ARENA = 86 * 1024
        arena = sb("arena", [P, ARENA // 4])
        base = nc.sbuf_base - ARENA

        def at(name, kib, shape, dt=f32):
            size = 4
            for s in shape[1:]:
                size *= s
            assert kib * 1024 + size <= ARENA, name
            return nc.alloc_sbuf_tensor_at(name, shape, dt, offset=base + int(kib * 1024))

        CONVF = at("CONVF", 0, [P, 12, SEQ])
        QKF = at("QKF", 0, [P, 2 * HEADS, SEQ])
        GZS = at("GZS", 8, [P, HEADS, SEQ])
        GT = at("GT", 12, [P, NT, 3, HW])
        DL, MAT, MA, MB, MC, ME, MP = (at(f"delta_{n}", 24 + 4 * i, [P, NT, HEADS, P])
                                        for i, n in enumerate(["L", "AT", "A", "B", "C", "E", "P"]))
        GSQ = at("GSQ", 32, [P, NT, 2 * HW])
        OSQ = at("OSQ", 32, [P, NT, HW])
        DO = at("DO", 40, [P, NT, HW])
        YB = at("YB", 44, [P, HEADS, SEQ])
        ROWS = [at(f"ROWS{i}", 24 + 0.5 * i, [P, P]) for i in range(3)]
        SQK = at("SQK", 52, [P, 2 * HEADS, SEQ])
        SV = at("SV", 60, [P, NT, HW])
        Z = at("Z", 64, [P, HEADS, 384])
        SP_ = at("SP_", 70, [P, HEADS, 384])
        FV = at("FV", 76, [P, NT, HW])
        FQK = at("FQK", 64, [P, 2 * HEADS, SEQ])
        FP0 = at("FP0", 52, [P, HEADS, P])
        FP1 = at("FP1", 54, [P, HEADS, SEQ])
        FPT0 = at("FPT0", 58, [P, HEADS, P])
        FPT1 = at("FPT1", 60, [P, 2, HEADS, P])
        YH, YL = at("YH", 72, [P, HEADS, SEQ], f32r), at("YL", 82, [P, HEADS, SEQ], f32r)
        TW = at("TW", 80, [P, KT, 12])
        THI = at("THI", 80.5, [P, KT, 12], f32r)
        TLO = at("TLO", 81, [P, KT, 12], f32r)
        G = XS[:, :, :].rearrange("p t (k s) -> p (t k) s", s=SEQ)
        HT = X
        MIX = X[:, :, :].rearrange("p t (k s) -> p (t k) s", s=SEQ)
        MEM = at("MEM", 24, [P, NT, DM])
        MJUNK = at("MJUNK", 0, [P, NT, DM])
        MH = at("MH", 32, [P, KT, SEQ], f32r)
        MLO = at("MLO", 40, [P, KT, SEQ], f32r)
        MK = at("MK", 56, [P, NT, HW])
        MSQ = at("MSQ", 60, [P, NT, HW])
        MKT = at("MKT", 64, [P, HEADS, SEQ])
        MV = at("MV", 68, [P, NT, HW])
        MQ = at("MQ", 48, [P, NT, HW])
        MQT = at("MQT", 76, [P, HEADS, SEQ])
        MPR = at("MPR", 0, [P, NT, HEADS, SEQ])
        MPT = at("MPT", 8, [P, NT, HEADS, SEQ])
        HH = at("HH", 0, [P, FT, SEQ], f32r)
        HL = at("HL", 22, [P, FT, SEQ], f32r)
        UA = at("UA", 44, [P, 2, 2, SEQ])
        UB = at("UB", 48, [P, 2, 2, SEQ])
        PRE_GAIN = at("PRE_GAIN", 52, [P, DM])
        POST_GAIN = at("POST_GAIN", 82, [P, DM])
        U2 = at("U2", 44, [P, KT, SEQ])
        V2 = at("V2", 52, [P, NT, DM])
        C2 = at("C2", 60, [P, KT, SEQ])
        S2A, S2B, S4 = at("S2A", 78, [P, 2, SEQ]), at("S2B", 38, [P, 6, SEQ]), at("S4", 16, [P, 6, SEQ])
        S8, S16 = at("S8", 68, [P, 4, SEQ]), at("S16", 74, [P, 2, SEQ])
        SGA = at("SGA", 44, [P, KT, SEQ])
        SGB = at("SGB", 52, [P, KT, SEQ])
        BS = at("BS", 72, [P, 4, P])
        WST = at("WST", 76, [P, 4, P])
        SGUW = at("SGUW", 78, [P, 4, P])
        PG = at("PG", 44, [P, NT, DM])
        EP = at("EP", 66, [P, NT, DM])
        PR = at("PR", 60, [P, NT, 256])
        PH = at("PH", 62, [P, 2, SEQ], f32r)
        PL = at("PL", 64, [P, 2, SEQ], f32r)

        SS = {r: stat(2) for r in NORMS}
        PSS = {r: stat(2) for r in ("down1", "mix_o", "down2")}
        MS, RS, RT = stat(16), stat(16), stat(16)
        HSS = stat(16)
        BROW, SGN, EA = stat(12), stat(12), stat(4)
        TY, TE, TS = (stat(24).rearrange("p (t c) -> p t c", t=NT) for _ in range(3))
        BETA, NG, NC, EGC = (stat(8).rearrange("p (t c) -> p t c", t=NT) for _ in range(4))
        KD = stat(4)
        MX, RSUM = stat(8), stat(8)
        MEAN, LSS, POST = stat(2), stat(2), stat(2)
        assert stat_at[0] <= STAT.shape[1]
        INV16 = sb("INV16", [P, 4, 16])

        ACCP = ctx.enter_context(nc.psum_tensor("ACCP", [P, 4, 512], f32))
        SMP = ctx.enter_context(nc.psum_tensor("SMP", [P, 4, 512], f32))

        def sems(names):
            return [sem(n) for n in names.split()]

        raw_ready = [sem(f"raw_ready{i}") for i in range(RAWS)]
        x_loaded = [sem(f"x_loaded{t}") for t in range(NT)]
        hi_ready = sem("hi_ready")
        lo_ready = [sem(f"lo_ready{i}") for i in range(RING)]
        block_done = sem("block_done")
        tile_done = sem("tile_done")
        small_done = sem("small_done")
        acc_taken = [sem(f"acc_taken{i}") for i in range(4)]
        small_taken = [sem(f"small_taken{i}") for i in range(4)]
        dve_step, act_step, pool_step = sems("dve_step act_step pool_step")
        x_again, mem_loaded, rows_loaded, tiny_loaded, tiny_w_loaded = sems("x_again mem_loaded rows_loaded tiny_loaded tiny_w_loaded")
        sgu_loaded, p_loaded, pre_gain_loaded, post_gain_loaded, stored = sems(
            "sgu_loaded p_loaded pre_gain_loaded post_gain_loaded stored")
        masks_ready, bias_zeroed, windows_ready = sems("masks_ready bias_zeroed windows_ready")
        sumsq, scaled, norm_hi = sems("sumsq scaled norm_hi")
        tiny_hi, tiny_lo, tiny_abs, tiny_ln, tiny_sp, tiny_exp = sems("tiny_hi tiny_lo tiny_abs tiny_ln tiny_sp tiny_exp")
        conv_base, conv_done = sems("conv_base conv_done")
        heads_sq, heads_ready = sems("heads_sq heads_ready")
        rates_ready, rates_exp, decay_ready, D_ready, level_ready = sems("rates_ready rates_exp decay_ready D_ready level_ready")
        rhs_ready, delta_out = sems("rhs_ready delta_out")
        inverse = sem("inverse")
        keep_abs, keep_ln, keep_ready, stick_ready = sems("keep_abs keep_ln keep_ready stick_ready")
        row_max, probs_ready = sems("row_max probs_ready")
        y_hi, y_lo = sems("y_hi y_lo")
        mixed_ready, mixed_hi, mixed_lo = sems("mixed_ready mixed_hi mixed_lo")
        a_base, a_act, b_base, h_ready, h_hi, h_lo = sems("a_base a_act b_base h_ready h_hi h_lo")
        post_sq, tap_done, dve_mix = sems("post_sq tap_done dve_mix")
        ln_mean, ln_sq, ln_ready = sems("ln_mean ln_sq ln_ready")
        gated, gated_hi, gated_lo, pooled, pooled_hi, pooled_lo, proj_hi = sems(
            "gated gated_hi gated_lo pooled pooled_hi pooled_lo proj_hi")
        y2_ready, y2_hi, y2_lo = sems("y2_ready y2_hi y2_lo")
        p_hi, ple_sq, out_ready = sems("p_hi ple_sq out_ready")

        class Turn:

            def __init__(self, j, i=None, stride=0):
                self.j, self.i, self.stride = j, i, stride

            def count(self, f):
                first = f(self.j)
                return first if self.i is None else first + self.i * (f(self.j + self.stride) - first)

            def part(self, k, n):
                return Turn(n * self.j + k, self.i, n * self.stride)

        def repeat(eng, first, last, stride, step):
            groups, over = divmod(last - first, stride)
            for j in range(first, first + over):
                step(Turn(j))
            with eng.Fori(0, groups) as i:
                for j in range(first + over, first + over + stride):
                    step(Turn(j, i, stride))

        def wait(eng, semaphore, value):
            if not (isinstance(value, int) and value <= 0):
                eng.wait_ge(semaphore, value)

        def small(name):
            return SMP[:, SMALL_ORDER[name] % 4, :]

        def small_bank_free(pe, name):
            wait(pe, small_taken[SMALL_ORDER[name] % 4], SMALL_ORDER[name] // 4)

        def small_is_done(eng, name):
            eng.wait_ge(small_done, SMALL_ORDER[name] + 1)

        def small_is_taken(eng, name):
            eng.wait_ge(small_taken[SMALL_ORDER[name] % 4], SMALL_ORDER[name] // 4 + 1)

        def bank_of(name):
            return small_taken[SMALL_ORDER[name] % 4]

        def acc(phase, t, k=0):
            return ACCP[:, ACC_BANKS[phase, t.j][k], :]

        def acc_banks_free(pe, phase, t, *which):
            for b in [ACC_BANKS[phase, t.j][k] for k in which] or ACC_BANKS[phase, t.j]:
                wait(pe, acc_taken[b], t.count(lambda j: ACC_TURN[phase, j][b]))

        def acc_is_done(eng, phase, t):
            eng.wait_ge(block_done, t.count(lambda j: ACC_LAST[phase, j] + 1))

        def tile_is_done(eng, phase, m):
            if m == 0 and phase in TILED:
                eng.wait_ge(tile_done, list(TILED).index(phase) + 1)
            else:
                acc_is_done(eng, phase, Turn(0))

        def acc_bank(phase, t, k=0):
            return acc_taken[ACC_BANKS[phase, t.j][k]]

        def acc_is_taken(eng, phase, t, k=0):
            b = ACC_BANKS[phase, t.j][k]
            eng.wait_ge(acc_taken[b], t.count(lambda j: ACC_TURN[phase, j][b] + 1))

        def col(name, i=0):
            tile, row = COL_AT[name]
            return COL[tile][:, row + i:row + i + 1]

        def conv_tap(tap, tile, t):
            return FCONV[:, moved(tap * 2 * FT + tile, t, 2)]

        def conv_bias(tile, t):
            tile_, row = COL_AT["ffn_conv_b"]
            return COL[tile_][:, moved(row + tile, t, 2)]

        def moved(c, t, per_turn):
            return slice(c, c + 1) if t.i is None else bass.ds(c + t.i * (t.stride * per_turn), 1)

        def tiles_of(t):
            return slice(2 * t.j, 2 * t.j + 2) if t.i is None else bass.ds(2 * t.j + t.i * (2 * t.stride), 2)

        def lo_is_ready(eng, phase, t, ahead=0):
            n = FIRST[phase] + t.j + ahead
            eng.wait_ge(lo_ready[n % RING], t.count(lambda j: (FIRST[phase] + j + ahead) // RING + 1))
            return n % RING

        def tok(t):
            return slice(t * P, (t + 1) * P)

        def per_head(ap, n):
            return ap.unsqueeze(2).broadcast_to([P, ap.shape[1], n])

        def every(mask, n):
            return mask.unsqueeze(1).broadcast_to([P, n, mask.shape[1]])

        def by_head(ap, d=P):
            return ap.rearrange("p (h d) -> p h d", d=d)

        def flat(ap):
            return ap.rearrange("p a b -> p (a b)")

        block = ctx.enter_context(nc.Block())

        @block.sync
        def _(sp):
            def load(phase, t, source):
                n = FIRST[phase] + t.j
                slot = n % RAWS
                if n >= RAWS:
                    lo_is_ready(sp, phase, t, -RAWS)
                dst = RAW[:, slot, :].rearrange("p (k n) -> p k n", k=source.shape[1])
                sp.dma_start(dst, source).then_inc(raw_ready[slot], 16)

            def load_f(phase, m, c):
                for j in range(dict(PHASES)[phase]):
                    load(phase, Turn(j), f_block(m, c + 256 * j))

            def load_t(phase, m, c):
                for j in range(dict(PHASES)[phase]):
                    load(phase, Turn(j), t_block(m, c + 512 * (j // 2), j % 2))

            def load_d(phase, m):
                for j in range(dict(PHASES)[phase]):
                    load(phase, Turn(j), d_block(m, j))

            def load_pairs(phase, first, second):
                def step(t):
                    at_loop = 0 if t.i is None else t.i * (256 * t.stride)
                    for k, (m, c) in enumerate((first, second)):
                        load(phase, t.part(k, 2), f_block(m, at_loop + (c + 256 * t.j)))
                repeat(sp, 0, FT // 2, 2, step)

            def load_down(phase, m):
                def step(t):
                    load(phase, t, d_block(m, t.j if t.i is None else t.i * t.stride + t.j))
                repeat(sp, 0, FT // 2, 4, step)

            for t in range(NT):
                sp.dma_start(X[:, t, :], A["x"][0, tok(t), :]).then_inc(x_loaded[t], 16)
            load_f("gdn", w["w_in"], C_GQKV)
            load_f("sbqk", w["w_in"], C_SQ)
            load_t("sbv", w["w_in"], C_SV)
            load_t("foxqk", w["w_in"], C_FQ)
            load_t("foxv", w["w_in"], C_FV)
            for g, branch, wo in (("c", 2, "w_oc"), ("a", 0, "w_oa"), ("b", 1, "w_ob")):
                if g == "b":
                    load_f("gz", w["w_in"], C_GZ)
                load_f(f"gate_{g}", w["w_in"], C_GATE + DM * branch)
                for j in range(2):
                    load(f"out_{g}", Turn(j), rows(w[wo], 0, 4, 512 * j, 512))
            load_d("w_out", w["w_out"])
            load_t("mem_k", w["w_mkv"], 0)
            load_t("mem_q", w["w_mq"], 0)
            load_t("mem_v", w["w_mkv"], HW)
            load_d("mem_o", w["w_mo"])
            load_pairs("up", (w["w_up"], 0), (w["w_up"], DFF))
            load_down("down", w["w_down"])
            load_pairs("ffn1", (w["ffn1_w_gate_2"], 0), (w["ffn1_w_up_2"], 0))
            load_down("down1", w["ffn1_w_down_2"])
            load_t("mix_v", w["w_in_2"], DM)
            load_f("mix_u", w["w_in_2"], 0)
            load_f("mix_c", w["w_in_2"], 2 * DM)
            load_f("mix_ga", w["w_in_2"], 3 * DM)
            load_f("mix_gb", w["w_in_2"], 4 * DM)
            load("pool", Turn(0), A["pool_w_2"][0].rearrange("g (k p) n -> p (g k) n", p=P))
            for j in range(8):
                load("mix_out", Turn(j), f_block(w[("w_out_a_2", "w_out_b_2")[j % 2]], 256 * (j // 2)))
            load_d("mix_o", w["w_o_2"])
            load_pairs("ffn2", (w["ffn2_w_gate_2"], 0), (w["ffn2_w_up_2"], 0))
            load_down("down2", w["ffn2_w_down_2"])
            load_d("ple_e", w["ple_w_proj_2"])
            load_t("ple_g", w["ple_w_gate_2"], 0)
            for t in range(NT):
                sp.wait_ge(out_ready, t + 1)
                sp.dma_start(out[0, tok(t), :], X[:, t, :]).then_inc(stored, 16)
            sp.wait_ge(stored, 16 * NT)

        @block.gpsimd
        def _(pool):
            steps = [0]

            def link(ins):
                steps[0] += 1
                ins.then_inc(pool_step, 1)
                pool.wait_ge(pool_step, steps[0])

            def where(dst, keep, pattern, start, per_partition, fill):
                return pool.affine_select(out=dst, in_=dst, compare_op=keep, fill=fill, base=start,
                                          pattern=pattern, channel_multiplier=per_partition)

            def masked(dst, keep, pattern, start, per_partition, fill, value=None):
                if value is not None:
                    link(pool.memset(dst, value))
                link(where(dst, keep, pattern, start, per_partition, fill))

            pool.memset(BROW, 0.0).then_inc(bias_zeroed, 1)
            pool.wait_ge(bias_zeroed, 1)
            pool.dma_start(BROW[:, 0:4], A["fox_fbias"].broadcast_to([P, HEADS])).then_inc(tiny_loaded, 16)
            pool.dma_start(BROW[:, 8:12], A["gdn_dt_bias"].broadcast_to([P, HEADS])).then_inc(tiny_loaded, 16)
            pool.dma_start(EA, A["gdn_a_log"].broadcast_to([P, HEADS])).then_inc(tiny_loaded, 16)
            link(pool.memset(IDENT[:, :], 0.0))
            where(IDENT[:, :], ALU.not_equal, [[-1, P]], 0, 1, 1.0).then_inc(masks_ready, 1)
            link(pool.memset(SGN[:, 0:8], -1.0))
            link(pool.memset(SGN[:, 8:12], 1.0))
            link(pool.memset(ONES, 1.0))
            masked(TRI, ALU.is_ge, [[1, P]], 0, -1, 0.0, 1.0)
            masked(FROM[:, :], ALU.is_ge, [[-1, P]], 0, 1, 0.0, 1.0)
            masked(BEFORE[:, :], ALU.is_ge, [[1, P]], -1, -1, 0.0, 1.0)
            masked(BIG_NOT_BEFORE[:, :], ALU.is_gt, [[1, P]], 0, -1, BIG, 0.0)
            masked(NEG_AFTER[:, :], ALU.is_ge, [[-1, P]], 0, 1, -BIG, 0.0)
            d16 = DIAG16[:, :].rearrange("p (g c) -> p g c", c=16)
            masked(DIAG16[:, :], ALU.is_ge, [[-1, P]], -1, 1, 0.0, 1.0)
            masked(d16, ALU.is_ge, [[-16, P // 16], [0, 16]], 0, 1, 0.0)
            masked(d16, ALU.is_ge, [[16, P // 16], [0, 16]], 15, -1, 0.0)
            for b, m in LEVEL.items():
                link(pool.memset(m[:, :], 0.0))
                left = m[:, :].rearrange("p (g s c) -> p g s c", s=2, c=b)[:, :, 0, :]
                masked(left, ALU.is_ge, [[-2 * b, P // (2 * b)], [0, b]], -b, 1, 0.0, 1.0)
                masked(left, ALU.is_ge, [[2 * b, P // (2 * b)], [0, b]], 2 * b - 1, -1, 0.0)
            link(pool.memset(INV16[:, :, :], 1.0))
            for g, size in enumerate(POOL_WINDOWS):
                for t in range(size - 1):
                    link(pool.memset(INV16[:, g, t:t + 1], size / (t + 1)))
            pool.wait_ge(masks_ready, 1)
            pool.memset(KEEP[:, :], 1.0).then_inc(masks_ready, 1)

            for t in range(NT):
                small_is_taken(pool, f"kk{t}")
                pool.tensor_tensor(MA[:, t], DL[:, t], every(DIAG16[:, :], HEADS), ALU.mult).then_inc(D_ready, 1)
            for b, last in ((16, "D8"), (32, "Z16"), (64, "Z32")):
                for t in range(NT):
                    small_is_done(pool, f"{last}_{t}")
                    pool.tensor_tensor(MA[:, t], DL[:, t], every(LEVEL[b][:, :], HEADS), ALU.mult).then_inc(level_ready, 1)

            def lo_of(n):
                pool.wait_ge(hi_ready, n + 1)
                s = n % RING
                pool.tensor_tensor(LO[:, s, :], RAW[:, n % RAWS, :], HI[:, s, :].bitcast(f32), ALU.subtract).then_inc(lo_ready[s], 1)

            for n in sorted(ON_POOL):
                if n < FIRST["mix_u"]:
                    lo_of(n)

            for j in range(4):
                acc_is_taken(pool, "mix_c", Turn(j))
            small_is_taken(pool, "sguw")
            for dst, src, shift in ((S2A, C2[:, 0:2], 1), (S2B, C2[:, 2:8], 1), (S4, S2B[:, :], 2),
                                    (S8, S4[:, 2:6], 4), (S16, S8[:, 2:4], 8)):
                link(pool.tensor_copy(dst[:, :, 0:shift], src[:, :, 0:shift]))
                pool.tensor_tensor(dst[:, :, shift:SEQ], src[:, :, shift:SEQ], src[:, :, 0:SEQ - shift],
                                   ALU.add).then_inc(windows_ready, 1)
                pool.wait_ge(windows_ready, [S2A, S2B, S4, S8, S16].index(dst) + 1)
            for n in sorted(ON_POOL):
                if n > FIRST["mix_u"]:
                    lo_of(n)

        @block.tensor
        def _(pe):
            def three(dst, lhs, rhs, start, stop):
                pe.matmul(dst, lhs[0], rhs[0], start=start, stop=False)
                pe.matmul(dst, lhs[0], rhs[1], start=False, stop=False)
                return pe.matmul(dst, lhs[1], rhs[0], start=False, stop=stop)

            def f_part(phase, t, xh, xl, tokens, ready=None):
                s = lo_is_ready(pe, phase, t)
                acc_banks_free(pe, phase, t)
                for half in range(2):
                    for k in range(KT):
                        if ready and half == 0:
                            ready(k)
                        c = slice(k * 256 + half * P, k * 256 + half * P + P)
                        dst = acc(phase, t)[:, half * SEQ:(half + 1) * SEQ]
                        last = three(dst[:, tokens], (HI[:, s, c], LO[:, s, c]), (xh[:, k, tokens], xl[:, k, tokens]),
                                     k == 0, k == KT - 1)
                return last

            def f_gemm(phase, t, xh, xl, ready=None):
                f_part(phase, t, xh, xl, slice(0, SEQ), ready).then_inc(block_done, 1)

            def t_part(phase, j, m, xh, xl, ready=None):
                chunk, half = Turn(j // 2), j % 2
                s = lo_is_ready(pe, phase, Turn(j))
                if half == 0:
                    acc_banks_free(pe, phase, chunk, m)
                for k in range(4):
                    kk = 4 * half + k
                    if ready:
                        ready(kk)
                    c = slice(k * 512, (k + 1) * 512)
                    last = three(acc(phase, chunk, m), (xh[:, kk, tok(m)], xl[:, kk, tok(m)]),
                                 (HI[:, s, c], LO[:, s, c]), kk == 0, kk == KT - 1)
                return last

            def t_half(phase, j, xh, xl, ready=None):
                for m in range(NT):
                    last = t_part(phase, j, m, xh, xl, ready and ready[m])
                last.then_inc(block_done, 1)

            def d_part(phase, j, m, xh, xl, ready=None):
                s = lo_is_ready(pe, phase, Turn(j))
                if j == 0:
                    acc_banks_free(pe, phase, Turn(0), 2 * m, 2 * m + 1)
                for k in range(2):
                    kk = 2 * j + k
                    if ready:
                        ready(kk)
                    for half in range(2):
                        c = slice(k * DM + half * 512, k * DM + half * 512 + 512)
                        last = three(acc(phase, Turn(0), 2 * m + half), (xh[:, kk, tok(m)], xl[:, kk, tok(m)]),
                                     (HI[:, s, c], LO[:, s, c]), kk == 0, kk == 2 * COUNT[phase] - 1)
                return last

            def d_gemm(phase, j, xh, xl, ready=None):
                for m in range(NT):
                    last = d_part(phase, j, m, xh, xl, ready)
                last.then_inc(block_done, 1)

            def d_tail(phase, xh, xl, ready, turn_first):
                tail = range(COUNT[phase] - TILED[phase], COUNT[phase])
                for m in range(NT):
                    for j in tail:
                        last = d_part(phase, j, m, xh, xl, ready)
                        if m == 1:
                            last.then_inc(block_done, 1)
                            if turn_first is not None and j == tail[-1] - turn_first:
                                norm_turn(AFTER[phase], XS, 0)
                    if m == 0:
                        last.then_inc(tile_done, 1)

            def t_open(phase, r, blocks, turn_second):
                for m in range(NT):
                    for j in range(blocks):
                        last = t_part(phase, j, m, XH, XL, norm_ready(r, m))
                        if m == 1:
                            last.then_inc(block_done, 1)
                        elif j == turn_second:
                            norm_turn(r, XS, 1)

            def o_gemm(phase, j, ready):
                s = lo_is_ready(pe, phase, Turn(j))
                acc_banks_free(pe, phase, Turn(j))
                ready()
                for n in range(4):
                    for k in range(HEADS):
                        c = slice(k * 512 + n * P, k * 512 + n * P + P)
                        last = three(acc(phase, Turn(j), n // 2)[:, n % 2 * 256:n % 2 * 256 + 256],
                                     (HI[:, s, c], LO[:, s, c]), (YH[:, k, :], YL[:, k, :]), k == 0, k == HEADS - 1)
                last.then_inc(block_done, 1)

            def finish(ins):
                ins.then_inc(small_done, 1)

            def four(name, product):
                small_bank_free(pe, name)
                for h in range(HEADS):
                    lhs, rhs = product(h)
                    last = pe.matmul(small(name)[:, h * P:(h + 1) * P], lhs, rhs, start=True, stop=True)
                finish(last)

            def turn_four(name, source):
                small_bank_free(pe, name)
                for h in range(4):
                    last = pe.transpose(small(name)[:, h * P:(h + 1) * P], source(h), IDENT[:, :])
                finish(last)

            def norm_turn(r, source, t):
                for b in range(2):
                    pe.wait_ge(scaled, 4 * NORMS.index(r) + 2 * t + b + 1)
                    turn_four(f"{r}.{t}{b}", lambda k: source[:, t, (4 * b + k) * P:(4 * b + k + 1) * P])

            def norm_ready(r, *tiles):
                def ready(k):
                    if k % 4 == 0:
                        for t in tiles:
                            small_is_taken(pe, f"{r}.{t}{k // 4}")
                return ready

            pe.wait_ge(masks_ready, 1)
            for t in range(NT):
                norm_turn("norm_mix", XS, t)
            pe.wait_ge(rows_loaded, 16 * N_ROW_LOADS)
            for i, n in enumerate((COL_N[0], COL_N[1] + CONV_TAIL, P)):
                small_bank_free(pe, f"cols{i}")
                finish(pe.transpose(small(f"cols{i}")[:, 0:n], ROWS[i][0:n, :], IDENT[0:n, 0:n]))

            for j in range(6):
                f_gemm("gdn", Turn(j), XH, XL, norm_ready("norm_mix", 0, 1) if j == 0 else None)
            small_bank_free(pe, "tiny")
            pe.wait_ge(tiny_lo, 1)
            for t in range(NT):
                for k in range(KT):
                    last = three(small("tiny")[:, 16 * t:16 * t + 12], (XH[:, k, tok(t)], XL[:, k, tok(t)]),
                                 (THI[:, k, :], TLO[:, k, :]), k == 0, k == KT - 1)
            finish(last)
            f_gemm("sbqk", Turn(0), XH, XL)
            pe.wait_ge(conv_done, 6)
            for i, part in enumerate("qk"):
                for t in range(NT):
                    turn_four(f"gT{part}{t}", lambda h: CONVF[:, 4 * i + h, tok(t)])
            f_gemm("sbqk", Turn(1), XH, XL)
            for t in range(NT):
                turn_four(f"gTv{t}", lambda h: CONVF[:, 8 + h, tok(t)])
            f_gemm("sbqk", Turn(2), XH, XL)
            pe.wait_ge(rates_ready, 1)
            pe.wait_ge(masks_ready, 2)
            small_bank_free(pe, "gcol")
            for t in range(NT):
                pe.matmul(small("gcol")[:, 4 * t:4 * t + 4], TRI, NG[:, t, :], start=True, stop=True)
            finish(pe.matmul(small("gcol")[:, 8:12], ONES, NG[:, 0, :], start=True, stop=True))
            for t in range(NT):
                four(f"grow{t}", lambda h: (NG[:, t, h:h + 1].broadcast_to([P, P]), TRI))
            f_gemm("sbqk", Turn(3), XH, XL)
            for i, part in enumerate("qk"):
                for t in range(NT):
                    pe.wait_ge(heads_ready, t + 1)
                    turn_four(f"gF{part}{t}", lambda h: GT[:, t, i, h * P:(h + 1) * P])
            t_half("sbv", 0, XH, XL)
            for t in range(NT):
                small_is_taken(pe, f"gFk{t}")
                four(f"kk{t}", lambda h: (QKF[:, 4 + h, tok(t)], QKF[:, 4 + h, tok(t)]))
            for t in range(NT):
                small_is_taken(pe, f"gFq{t}")
                four(f"kq{t}", lambda h: (QKF[:, 4 + h, tok(t)], QKF[:, h, tok(t)]))
            t_half("sbv", 1, XH, XL)
            for j in range(4):
                acc_is_taken(pe, "sbqk", Turn(j))
            for h in range(HEADS):
                small_bank_free(pe, f"z{h}")
                pe.matmul(small(f"z{h}")[:, 0:SEQ], SQK[:, 4 + h, tok(0)], SQK[:, h, :], start=True, stop=True)
                finish(pe.matmul(small(f"z{h}")[:, SEQ:SEQ + P], SQK[:, 4 + h, tok(1)], SQK[:, h, tok(1)], start=True, stop=True))
            for t in range(NT):
                pe.wait_ge(D_ready, t + 1)
                turn_four(f"Dt{t}", lambda h: MA[:, t, h, :])
            t_half("foxqk", 0, XH, XL)
            for t in range(NT):
                small_is_taken(pe, f"Dt{t}")
                four(f"D2_{t}", lambda h: (MB[:, t, h, :], MA[:, t, h, :]))
            for t in range(NT):
                four(f"D2t_{t}", lambda h: (MA[:, t, h, :], MB[:, t, h, :]))
            t_half("foxqk", 1, XH, XL)
            for t in range(NT):
                small_is_taken(pe, f"D2_{t}")
                four(f"P2_{t}", lambda h: (MC[:, t, h, :], MP[:, t, h, :]))
            for t in range(NT):
                small_is_taken(pe, f"D2t_{t}")
                four(f"D4_{t}", lambda h: (ME[:, t, h, :], MC[:, t, h, :]))
            t_half("foxqk", 2, XH, XL)
            for t in range(NT):
                four(f"D4t_{t}", lambda h: (MC[:, t, h, :], ME[:, t, h, :]))
            pe.wait_ge(keep_ready, 1)

            def rest_sums(h):
                name = f"rc{h}"
                small_bank_free(pe, name)
                bank = small(name)
                pe.matmul(bank[:, 0:SEQ], FROM[:, :], SP_[:, h, 0:SEQ], start=True, stop=False)
                pe.matmul(bank[:, P:SEQ], ONES, SP_[:, h, SEQ:SEQ + P], start=False, stop=False)
                pe.matmul(bank[:, 0:P], IDENT[:, :], BIG_NOT_BEFORE[:, :], start=False, stop=True)
                pe.matmul(bank[:, SEQ:SEQ + P], FROM[:, :], SP_[:, h, SEQ:SEQ + P], start=True, stop=False)
                finish(pe.matmul(bank[:, SEQ:SEQ + P], IDENT[:, :], BIG_NOT_BEFORE[:, :], start=False, stop=True))

            for h in range(2):
                rest_sums(h)
            t_half("foxqk", 3, XH, XL)
            for h in range(2, 4):
                rest_sums(h)
            for t in range(NT):
                small_is_taken(pe, f"P2_{t}")
                small_is_taken(pe, f"D4_{t}")
                four(f"P4_{t}", lambda h: (MA[:, t, h, :], MP[:, t, h, :]))
            t_half("foxv", 0, XH, XL)
            for t in range(NT):
                small_is_taken(pe, f"D4t_{t}")
                four(f"D8_{t}", lambda h: (MB[:, t, h, :], MA[:, t, h, :]))
            t_half("foxv", 1, XH, XL)
            for t in range(NT):
                small_is_taken(pe, f"D8_{t}")
                small_is_taken(pe, f"P4_{t}")
                four(f"P8_{t}", lambda h: (MC[:, t, h, :], MP[:, t, h, :]))
            pe.wait_ge(stick_ready, 1)
            for m in range(NT):
                acc_is_taken(pe, "sbv", Turn(0), m)
            for g in range(2):
                name = f"so{g}"
                small_bank_free(pe, name)
                for h in (2 * g, 2 * g + 1):
                    dst = small(name)[:, h % 2 * SEQ:h % 2 * SEQ + SEQ]
                    pe.matmul(dst, SV[:, 0, h * P:(h + 1) * P], Z[:, h, 0:SEQ], start=True, stop=False)
                    last = pe.matmul(dst[:, P:SEQ], SV[:, 1, h * P:(h + 1) * P], Z[:, h, SEQ:SEQ + P], start=False, stop=True)
                finish(last)
            f_gemm("gate_c", Turn(0), XH, XL)
            for t in range(NT):
                small_is_taken(pe, f"P8_{t}")
                turn_four(f"T16_{t}", lambda h: MP[:, t, h, :])
            f_gemm("gate_c", Turn(1), XH, XL)
            for i, part in enumerate("qk"):
                for t in range(NT):
                    pe.wait_ge(heads_ready, 2 + t + 1)
                    turn_four(f"fT{part}{t}", lambda h: HT[:, t, i * HW + h * P:i * HW + (h + 1) * P])

            def join(b, n):
                for t in range(NT):
                    pe.wait_ge(level_ready, 2 * n + t + 1)
                    four(f"Z{b}_{t}", lambda h: (MA[:, t, h, :], MP[:, t, h, :]))

            def joined(b, both=True):
                for t in range(NT):
                    small_is_taken(pe, f"Z{b}_{t}")
                    if b == 16:
                        small_is_taken(pe, f"T16_{t}")
                    else:
                        small_is_taken(pe, f"T{b}_{t}")
                    four(f"Tt{2 * b}_{t}", lambda h: (ME[:, t, h, :], MB[:, t, h, :]))
                for t in range(NT if both else 0):
                    four(f"T{2 * b}_{t}", lambda h: (MB[:, t, h, :], ME[:, t, h, :]))

            f_gemm("gate_c", Turn(2), XH, XL)
            join(16, 0)
            f_gemm("gate_c", Turn(3), XH, XL)
            joined(16)

            def y_is_ready(*names):
                def ready():
                    for n in names:
                        small_is_taken(pe, n)
                return ready

            o_gemm("out_c", 0, y_is_ready("so0", "so1"))
            for part in "qk":
                for t in range(NT):
                    small_is_taken(pe, f"fT{part}{t}")

            def fox_scores(name, t, heads):
                small_bank_free(pe, name)
                for i, h in enumerate(heads):
                    n = (t + 1) * P
                    dst = small(name)[:, i * n:(i + 1) * n]
                    pe.matmul(dst, FQK[:, h, tok(t)], FQK[:, 4 + h, 0:n], start=True, stop=False)
                    pe.matmul(dst, TS[:, 0, h:h + 1].broadcast_to([P, P]), flat(UPTO[:, 0:t + 1, :]), start=False, stop=False)
                    if t == 1:
                        pe.matmul(dst[:, P:SEQ], TS[:, 1, h:h + 1].broadcast_to([P, P]), TRI, start=False, stop=False)
                    last = pe.matmul(dst[:, t * P:n], IDENT[:, :], NEG_AFTER[:, :], start=False, stop=True)
                finish(last)

            fox_scores("fS0", 0, range(4))
            fox_scores("fS1a", 1, (0, 1))
            fox_scores("fS1b", 1, (2, 3))
            o_gemm("out_c", 1, y_is_ready())
            for t in range(NT):
                small_is_taken(pe, f"Tt32_{t}")
            join(32, 1)
            f_gemm("gate_a", Turn(0), XH, XL)
            joined(32)
            f_gemm("gate_a", Turn(1), XH, XL)
            pe.wait_ge(probs_ready, 1)
            turn_four("fP0", lambda h: FP0[:, h, :])
            pe.wait_ge(probs_ready, 2)
            for i, part in enumerate("ab"):
                turn_four(f"fP1{part}", lambda h: FP1[:, h, tok(i)])
            f_gemm("gate_a", Turn(2), XH, XL)
            for m in range(NT):
                acc_is_taken(pe, "foxv", Turn(0), m)
            small_is_taken(pe, "fP0")
            four("fo0", lambda h: (FV[:, 0, h * P:(h + 1) * P], FPT0[:, h, :]))
            small_is_taken(pe, "fP1a")
            small_is_taken(pe, "fP1b")
            small_bank_free(pe, "fo1")
            for h in range(HEADS):
                for k in range(2):
                    last = pe.matmul(small("fo1")[:, h * P:(h + 1) * P], FV[:, k, h * P:(h + 1) * P], FPT1[:, k, h, :],
                                     start=k == 0, stop=k == 1)
            finish(last)
            for t in range(NT):
                small_is_taken(pe, f"Tt64_{t}")
            join(64, 2)
            f_gemm("gate_a", Turn(3), XH, XL)
            joined(64, both=False)
            o_gemm("out_a", 0, y_is_ready("fo0", "fo1"))
            small_is_taken(pe, "Tt128_0")
            pe.wait_ge(rhs_ready, 2)
            four("vn0", lambda h: (MP[:, 0, h, :], GT[:, 0, 0, h * P:(h + 1) * P]))
            o_gemm("out_a", 1, y_is_ready())
            small_is_taken(pe, "vn0")
            four("S1", lambda h: (GT[:, 0, 1, h * P:(h + 1) * P], GT[:, 1, 0, h * P:(h + 1) * P]))
            f_gemm("gz", Turn(0), XH, XL)
            small_is_taken(pe, "S1")
            four("kS", lambda h: (QKF[:, 4 + h, tok(1)], MA[:, 0, h, :]))
            four("qS", lambda h: (QKF[:, h, tok(1)], MA[:, 0, h, :]))
            f_gemm("gz", Turn(1), XH, XL)
            small_is_taken(pe, "Tt128_1")
            pe.wait_ge(rhs_ready, 3)
            four("vn1", lambda h: (MP[:, 1, h, :], GT[:, 1, 2, h * P:(h + 1) * P]))
            f_gemm("gate_b", Turn(0), XH, XL)
            small_is_taken(pe, "kq0")
            four("o0", lambda h: (MAT[:, 0, h, :], GT[:, 1, 0, h * P:(h + 1) * P]))
            small_is_taken(pe, "kq1")
            small_is_taken(pe, "vn1")
            four("o1", lambda h: (MAT[:, 1, h, :], MA[:, 1, h, :]))
            f_gemm("gate_b", Turn(1), XH, XL)
            f_gemm("gate_b", Turn(2), XH, XL)
            for t in range(NT):
                pe.wait_ge(heads_ready, 4 + t + 1)
                turn_four(f"yT{t}", lambda h: DO[:, t, h * P:(h + 1) * P])
            f_gemm("gate_b", Turn(3), XH, XL)

            def delta_ready():
                pe.wait_ge(y_lo, 2)

            o_gemm("out_b", 0, delta_ready)
            for t in range(NT):
                norm_turn("norm_mem", MEM, t)
            o_gemm("out_b", 1, delta_ready)

            def mixed_is_ready(k):
                pe.wait_ge(mixed_lo, k // 2 + 1)

            d_gemm("w_out", 0, XH, XL, mixed_is_ready)
            d_tail("w_out", XH, XL, mixed_is_ready, 1)
            for j in range(2):
                t_half("mem_k", j, MH, MLO, [norm_ready("norm_mem", m) for m in range(NT)])
            norm_turn("norm_xq", XS, 1)
            t_half("mem_q", 0, XH, XL, [norm_ready("norm_xq", m) for m in range(NT)])
            for t in range(NT):
                pe.wait_ge(heads_ready, 6 + t + 1)
                turn_four(f"mkT{t}", lambda h: MK[:, t, h * P:(h + 1) * P])
            t_half("mem_q", 1, XH, XL)
            t_half("mem_v", 0, MH, MLO)
            for t in range(NT):
                pe.wait_ge(heads_ready, 8 + t + 1)
                turn_four(f"mqT{t}", lambda h: MQ[:, t, h * P:(h + 1) * P])
            for t in range(NT):
                small_is_taken(pe, f"mkT{t}")
            for t in range(NT):
                small_is_taken(pe, f"mqT{t}")
                for part, heads in (("a", (0, 1)), ("b", (2, 3))):
                    name = f"mS{t}{part}"
                    small_bank_free(pe, name)
                    for i, h in enumerate(heads):
                        last = pe.matmul(small(name)[:, i * SEQ:(i + 1) * SEQ], MQT[:, h, tok(t)], MKT[:, h, :], start=True, stop=True)
                    finish(last)
            t_half("mem_v", 1, MH, MLO)
            for t in range(NT):
                pe.wait_ge(probs_ready, 2 + 2 * t + 2)
                for i, part in enumerate("ab"):
                    turn_four(f"mP{t}{part}", lambda h: MPR[:, t, h, tok(i)])
            for m in range(NT):
                acc_is_taken(pe, "mem_v", Turn(0), m)
            for name in ("mP0a", "mP0b", "mP1a", "mP1b"):
                small_is_taken(pe, name)
            for g in range(2):
                name = f"mo{g}"
                small_bank_free(pe, name)
                for h in (2 * g, 2 * g + 1):
                    for k in range(2):
                        last = pe.matmul(small(name)[:, h % 2 * SEQ:h % 2 * SEQ + SEQ], MV[:, k, h * P:(h + 1) * P],
                                         MPT[:, k, h, :], start=k == 0, stop=k == 1)
                finish(last)
            d_tail("mem_o", YH, YL, lambda k: small_is_taken(pe, f"mo{k // 2}"), 0)

            def ffn(r, up, down, before, turn_first):
                def step(t):
                    for k in range(2):
                        f_gemm(up, t.part(k, 2), XH, XL)

                def hidden_ready(k):
                    pe.wait_ge(h_lo, before * (FT // 2) + k // 2 + 1)

                norm_turn(r, XS, 1)
                f_gemm(up, Turn(0), XH, XL, norm_ready(r, 0, 1))
                f_gemm(up, Turn(1), XH, XL)
                repeat(pe, 1, FT // 2, 2, step)
                if down == "down2":
                    turn_p()
                for m in range(NT):
                    for j in range(2):
                        last = d_part(down, j, m, HH, HL, hidden_ready)
                        if m == 1:
                            last.then_inc(block_done, 1)
                for j in range(2, COUNT[down] - TILED[down]):
                    d_gemm(down, j, HH, HL, hidden_ready)
                d_tail(down, HH, HL, hidden_ready, turn_first)

            def turn_p():
                small_bank_free(pe, "pT")
                pe.wait_ge(p_loaded, 16)
                for k in range(2):
                    for t in range(NT):
                        last = pe.transpose(small("pT")[:, k * SEQ + t * P:k * SEQ + (t + 1) * P], PR[:, t, k * P:(k + 1) * P], IDENT[:, :])
                finish(last)

            ffn("norm_ffn", "up", "down", 0, 1)
            ffn("norm_f1", "ffn1", "down1", 1, 0)

            t_open("mix_v", "norm_mix2", OPEN, 2)
            t_half("mix_v", 3, XH, XL)
            small_bank_free(pe, "sguw")
            pe.wait_ge(sgu_loaded, 32)
            for g in range(4):
                last = pe.transpose(small("sguw")[:, g * P:(g + 1) * P], SGUW[:, g, :], IDENT[:, :])
            finish(last)
            for j in range(4):
                f_gemm("mix_u", Turn(j), XH, XL)
            f_gemm("mix_c", Turn(0), XH, XL)
            pe.wait_ge(ln_ready, 2)
            small_is_taken(pe, "sguw")
            for g in range(4):
                name = f"sgu{g}"
                small_bank_free(pe, name)
                for i in range(2):
                    for t in range(NT):
                        d = 2 * g + i
                        last = pe.matmul(small(name)[:, i * SEQ + t * P:i * SEQ + (t + 1) * P], V2[:, t, d * P:(d + 1) * P],
                                         WST[:, g, :], start=True, stop=True)
                finish(last)
            for j in range(1, 4):
                f_gemm("mix_c", Turn(j), XH, XL)
            for j in range(4):
                f_gemm("mix_ga", Turn(j), XH, XL)
            for j in range(4):
                f_gemm("mix_gb", Turn(j), XH, XL)
            s = lo_is_ready(pe, "pool", Turn(0))
            for g in range(4):
                acc_banks_free(pe, "pool", Turn(g))
                pe.wait_ge(pooled_lo, g + 1)
                for n in range(2):
                    for k in range(2):
                        c = slice((2 * g + k) * 256 + n * P, (2 * g + k) * 256 + n * P + P)
                        last = three(acc("pool", Turn(g))[:, n * 256:(n + 1) * 256], (HI[:, s, c], LO[:, s, c]),
                                     (HH[:, 8 + 2 * g + k, :], HL[:, 8 + 2 * g + k, :]), k == 0, k == 1)
            last.then_inc(block_done, 1)
            pe.wait_ge(gated_lo, 4)

            def projected(k):
                acc_is_taken(pe, "pool", Turn(k // 2))

            for j in range(8):
                k0 = 8 * (j % 2)
                f_gemm("mix_out", Turn(j), HH[:, k0:k0 + 8, :], HL[:, k0:k0 + 8, :], projected if j == 1 else None)

            def y2_is_ready(k):
                pe.wait_ge(y2_lo, k // 2 + 1)

            d_gemm("mix_o", 0, XH, XL, y2_is_ready)
            d_tail("mix_o", XH, XL, y2_is_ready, 0)

            ffn("norm_f2", "ffn2", "down2", 2, None)
            small_is_taken(pe, "pT")
            d_part("ple_e", 0, 0, PH, PL)
            norm_turn("norm_ple", XS, 0)
            d_part("ple_e", 0, 1, PH, PL).then_inc(block_done, 1)
            t_open("ple_g", "norm_ple", OPEN - 1, 1)
            for j in range(OPEN - 1, 4):
                t_half("ple_g", j, XH, XL)

        @block.scalar
        def _(act):
            steps = [0]

            def link(ins):
                steps[0] += 1
                ins.then_inc(act_step, 1)
                act.wait_ge(act_step, steps[0])

            def split(n):
                act.wait_ge(raw_ready[n % RAWS], 16 * (n // RAWS + 1))
                act.activation(HI[:, n % RING, :], RAW[:, n % RAWS, :], ACT.Copy).then_inc(hi_ready, 1)

            def split_ahead(phase, t):
                n = FIRST[phase] + t.j + RING
                if n >= N_BLOCKS:
                    return
                act.wait_ge(raw_ready[n % RAWS], t.count(lambda j: 16 * ((FIRST[phase] + j + RING) // RAWS + 1)))
                act.wait_ge(block_done, t.count(lambda j: FIRST[phase] + j + 1))
                act.activation(HI[:, n % RING, :], RAW[:, n % RAWS, :], ACT.Copy).then_inc(hi_ready, 1)

            def copy(dst, src, signal, scale=1.0):
                act.activation(dst, src, ACT.Copy, scale=scale).then_inc(signal, 1)

            def take_small(name, dst, src, scale=1.0):
                small_is_done(act, name)
                copy(dst, src, bank_of(name), scale)

            def norm_square(r, t, src, junk):
                act.activation(junk[:, t, :], src[:, t, :], ACT.Square, accum_out=SS[r][:, t:t + 1]).then_inc(sumsq, 1)

            def norm_split(r, t, hi):
                for b in range(2):
                    name = f"{r}.{t}{b}"
                    small_is_done(act, name)
                    copy(hi[:, 4 * b:4 * b + 4, tok(t)], by_head(small(name)), norm_hi)

            def pre_gain_load(name):
                act.dma_start(PRE_GAIN[:, :], A[name].broadcast_to([P, DM])).then_inc(pre_gain_loaded, 16)

            def post_gain_load(name):
                act.dma_start(POST_GAIN[:, :], A[name].broadcast_to([P, DM])).then_inc(post_gain_loaded, 16)

            def gates(phase, j, name, branch):
                acc_is_done(act, phase, Turn(j))
                for i in range(2):
                    ins = act.activation(G[:, 2 * j + i, :], acc(phase, Turn(j))[:, i * 256:(i + 1) * 256], ACT.Sigmoid,
                                         bias=col("gate_bias", 8 * branch + 2 * j + i))
                ins.then_inc(acc_bank(phase, Turn(j)), 1)

            def softmax_exp(name, rows_, scores, first):
                for i in range(scores.shape[1]):
                    ins = act.activation(rows_[:, i, :], scores[:, i, :], ACT.Exp, bias=MX[:, first + i:first + i + 1],
                                         accum_out=RSUM[:, first + i:first + i + 1])
                ins.then_inc(bank_of(name), 1)

            pre_gain_load("norm_mix")
            for tile, names in enumerate(COL_ROWS):
                row = 0
                for name, n in names:
                    a = A[name]
                    src = a.rearrange("a (r p) -> (a r) p", p=P) if len(a.shape) == 2 else a.rearrange("a t (r p) -> (a t r) p", p=P)
                    act.dma_start(ROWS[tile][row:row + n, :], src).then_inc(rows_loaded, 16)
                    row += n
            taps = A["ffn_conv"].rearrange("a t (r p) -> (a t r) p", p=P)
            act.dma_start(ROWS[2][:, :], taps[0:P, :]).then_inc(rows_loaded, 16)
            act.dma_start(ROWS[1][COL_N[1]:COL_N[1] + CONV_TAIL, :], taps[P:CONV_N, :]).then_inc(rows_loaded, 16)
            tiny_rows = w["w_in"].rearrange("(k p) n -> p k n", p=P)
            act.dma_start(TW[:, :, 0:4], tiny_rows[:, :, C_FF:C_FF + 4]).then_inc(tiny_w_loaded, 16)
            act.dma_start(TW[:, :, 4:12], tiny_rows[:, :, C_GB:C_GB + 8]).then_inc(tiny_w_loaded, 16)

            for t in range(NT):
                act.wait_ge(x_loaded[t], 16)
                norm_square("norm_mix", t, X, XS)
            split(0)
            for t in range(NT):
                norm_split("norm_mix", t, XH)
            for n in range(1, RING):
                split(n)
            act.wait_ge(tiny_w_loaded, 16 * 2)
            copy(THI[:, :, :], TW[:, :, :], tiny_hi)

            def conv_silu(j):
                acc_is_taken(act, "gdn", Turn(j))
                act.activation(CONVF[:, 2 * j:2 * j + 2, :], CONVF[:, 2 * j:2 * j + 2, :], ACT.Silu).then_inc(conv_done, 1)

            for j in range(6):
                if j:
                    conv_silu(j - 1)
                acc_is_done(act, "gdn", Turn(j))
                for i in range(2):
                    for cols in range(3):
                        small_is_taken(act, f"cols{cols}")
                    copy(CONVF[:, 2 * j + i, :], acc("gdn", Turn(j))[:, i * 256:(i + 1) * 256], conv_base,
                         col("gdn_conv", 3 * 12 + 2 * j + i))
                split_ahead("gdn", Turn(j))
            conv_silu(5)

            def take_f(phase, j, dst, scale):
                acc_is_done(act, phase, Turn(j))
                copy(dst, acc(phase, Turn(j)).rearrange("p (n s) -> p n s", s=SEQ), acc_bank(phase, Turn(j)), scale)

            def take_t(phase, chunk, dst):
                acc_is_done(act, phase, Turn(chunk))
                for m in range(NT):
                    copy(dst[:, m], acc(phase, Turn(chunk), m), acc_bank(phase, Turn(chunk), m))

            take_f("sbqk", 0, SQK[:, 0:2, :], DH ** -0.5)
            split_ahead("sbqk", Turn(0))
            act.wait_ge(tiny_abs, 1)
            link(act.activation(TE, TE, ACT.Exp, scale=-1.0))
            act.activation(TE, TE, ACT.Ln, bias=1.0).then_inc(tiny_ln, 1)
            take_small("gTq0", GT[:, 0, 0, :], small("gTq0"))
            take_small("gTk0", GT[:, 0, 1, :], small("gTk0"))
            take_f("sbqk", 1, SQK[:, 2:4, :], DH ** -0.5)
            split_ahead("sbqk", Turn(1))
            act.wait_ge(tiny_sp, 1)
            act.activation(BETA, TS[:, :, 4:8], ACT.Exp, scale=-1.0)
            act.wait_ge(tiny_loaded, 16 * 3)
            act.activation(EA, EA, ACT.Exp).then_inc(tiny_exp, 1)
            for t in range(NT):
                for part in "qk":
                    small_is_taken(act, f"gT{part}{t}")
                act.activation(GSQ[:, t, :], flat(GT[:, t, 0:2, :]), ACT.Square).then_inc(heads_sq, 1)
            take_small("gTv0", GT[:, 0, 2, :], small("gTv0"))
            take_f("sbqk", 2, SQK[:, 4:6, :], 1.0)
            split_ahead("sbqk", Turn(2))
            small_is_taken(act, "gcol")
            act.activation(EGC, NC, ACT.Exp, scale=-1.0)
            act.activation(KD, KD, ACT.Exp).then_inc(rates_exp, 1)
            for t in range(NT):
                small_is_taken(act, f"grow{t}")
                act.activation(MA[:, t], MA[:, t], ACT.Exp).then_inc(decay_ready, 1)
                act.activation(MB[:, t], MB[:, t], ACT.Exp, scale=-1.0).then_inc(decay_ready, 1)
            take_f("sbqk", 3, SQK[:, 6:8, :], 1.0)
            split_ahead("sbqk", Turn(3))
            take_small("gFq0", QKF[:, 0:4, tok(0)], by_head(small("gFq0")))
            take_small("gFk0", QKF[:, 4:8, tok(0)], by_head(small("gFk0")))
            split_ahead("sbv", Turn(0))
            take_t("sbv", 0, SV)
            split_ahead("sbv", Turn(1))
            for h in range(HEADS):
                take_small(f"z{h}", Z[:, h, :], small(f"z{h}")[:, 0:384])
            split_ahead("foxqk", Turn(0))
            act.wait_ge(keep_abs, 1)
            link(act.activation(SP_[:, :, :], SP_[:, :, :], ACT.Exp, scale=-1.0))
            act.activation(SP_[:, :, :], SP_[:, :, :], ACT.Ln, bias=1.0).then_inc(keep_ln, 1)
            take_small("D2_0", MC[:, 0], by_head(small("D2_0")))
            take_small("D2t_0", ME[:, 0], by_head(small("D2t_0")))
            take_t("foxqk", 0, HT[:, :, 0:HW])
            split_ahead("foxqk", Turn(1))
            take_small("D4_0", MA[:, 0], by_head(small("D4_0")))
            split_ahead("foxqk", Turn(2))
            take_small("D4t_0", MB[:, 0], by_head(small("D4t_0")))
            take_t("foxqk", 1, HT[:, :, HW:2 * HW])
            split_ahead("foxqk", Turn(3))
            for t in range(NT):
                for c in range(2):
                    acc_is_taken(act, "foxqk", Turn(c), t)
                act.activation(XS[:, t, :], HT[:, t, :], ACT.Square).then_inc(heads_sq, 1)
            split_ahead("foxv", Turn(0))
            for h in range(HEADS):
                small_is_taken(act, f"rc{h}")
            act.activation(Z[:, :, :], Z[:, :, :], ACT.Exp).then_inc(stick_ready, 1)
            take_small("D8_0", MC[:, 0], by_head(small("D8_0")))
            take_t("foxv", 0, FV)
            split_ahead("foxv", Turn(1))
            for g in range(2):
                small_is_done(act, f"so{g}")
                copy(YH[:, 2 * g:2 * g + 2, :], by_head(small(f"so{g}"), SEQ), y_hi)
            act.wait_ge(heads_ready, 4)
            gates("gate_c", 0, G, 2)
            split_ahead("gate_c", Turn(0))
            take_small("T16_0", ME[:, 0], by_head(small("T16_0")))
            gates("gate_c", 1, G, 2)
            split_ahead("gate_c", Turn(1))
            take_small("fTq0", FQK[:, 0:4, tok(0)], by_head(small("fTq0")), col("fox_qnorm"))
            take_small("fTk0", FQK[:, 4:8, tok(0)], by_head(small("fTk0")), col("fox_knorm"))
            gates("gate_c", 2, G, 2)
            split_ahead("gate_c", Turn(2))
            take_small("Z16_0", MB[:, 0], by_head(small("Z16_0")))
            gates("gate_c", 3, G, 2)
            split_ahead("gate_c", Turn(3))
            split_ahead("out_c", Turn(0))
            act.wait_ge(row_max, 1)
            softmax_exp("fS0", FP0, by_head(small("fS0")), 0)
            act.wait_ge(row_max, 3)
            softmax_exp("fS1a", FP1[:, 0:2, :], by_head(small("fS1a"), SEQ), 4)
            softmax_exp("fS1b", FP1[:, 2:4, :], by_head(small("fS1b"), SEQ), 6)
            split_ahead("out_c", Turn(1))
            take_small("Z32_0", MB[:, 0], by_head(small("Z32_0")))
            for k in range(2):
                acc_is_taken(act, "out_c", Turn(1), k)
            gates("gate_a", 0, G, 0)
            split_ahead("gate_a", Turn(0))
            gates("gate_a", 1, G, 0)
            split_ahead("gate_a", Turn(1))
            take_small("fP0", FPT0[:, :, :], by_head(small("fP0")))
            take_small("fP1a", FPT1[:, 0], by_head(small("fP1a")))
            gates("gate_a", 2, G, 0)
            split_ahead("gate_a", Turn(2))
            for t in range(NT):
                small_is_done(act, f"fo{t}")
                copy(YH[:, :, tok(t)], by_head(small(f"fo{t}")), y_hi)
            take_small("Z64_0", MB[:, 0], by_head(small("Z64_0")))
            gates("gate_a", 3, G, 0)
            split_ahead("gate_a", Turn(3))
            split_ahead("out_a", Turn(0))
            take_small("vn0", GT[:, 1, 0, :], small("vn0"))
            split_ahead("out_a", Turn(1))
            take_small("S1", MA[:, 0], by_head(small("S1")))

            def gz_silu(j):
                acc_is_done(act, "gz", Turn(j))
                act.activation(GZS[:, 2 * j:2 * j + 2, :], acc("gz", Turn(j)).rearrange("p (n s) -> p n s", s=SEQ),
                               ACT.Silu).then_inc(acc_bank("gz", Turn(j)), 1)

            gz_silu(0)
            split_ahead("gz", Turn(0))
            gz_silu(1)
            split_ahead("gz", Turn(1))
            take_small("vn1", MA[:, 1], by_head(small("vn1")))
            for k in range(2):
                acc_is_taken(act, "out_a", Turn(1), k)
            gates("gate_b", 0, G, 1)
            split_ahead("gate_b", Turn(0))
            take_small("o0", DO[:, 0, :], small("o0"))
            for t in range(NT):
                small_is_taken(act, f"o{t}")
                act.activation(OSQ[:, t, :], DO[:, t, :], ACT.Square).then_inc(heads_sq, 1)
            pre_gain_load("norm_mem")
            act.dma_start(MEM[:, :, :], A["mem"][0].rearrange("(t p) d -> p t d", p=P)).then_inc(mem_loaded, 16)
            for j in range(1, 4):
                gates("gate_b", j, G, 1)
                split_ahead("gate_b", Turn(j))
                if j == 2:
                    for t in range(NT):
                        small_is_taken(act, f"yT{t}")
                        copy(YH[:, :, tok(t)], YB[:, :, tok(t)], y_hi)
            act.wait_ge(mem_loaded, 16)
            for t in range(NT):
                norm_square("norm_mem", t, MEM, MJUNK)
            for j in range(2):
                for k in range(2):
                    act.wait_ge(mixed_ready, 2 * j + k + 1)
                    copy(XH[:, 4 * j + 2 * k:4 * j + 2 * k + 2, :], MIX[:, 4 * j + 2 * k:4 * j + 2 * k + 2, :], mixed_hi)
                split_ahead("out_b", Turn(j))
                if j == 0:
                    for t in range(NT):
                        norm_split("norm_mem", t, MH)
                    pre_gain_load("norm_xq")
            act.wait_ge(mixed_lo, 4)
            act.dma_start(X[:, :, :], A["x"][0].rearrange("(t p) d -> p t d", p=P)).then_inc(x_again, 16)

            def new_square(phase, r, m):
                acc_is_taken(act, phase, Turn(0), 2 * m)
                acc_is_taken(act, phase, Turn(0), 2 * m + 1)
                norm_square(r, m, X, XS)

            def post_square(phase, m):
                tile_is_done(act, phase, m)
                act.activation(XS[:, m, :], flat(ACCP[:, 2 * m:2 * m + 2, :]), ACT.Square,
                               accum_out=PSS[phase][:, m:m + 1]).then_inc(post_sq, 1)

            def norm_behind(phase, r):
                n = COUNT[phase]
                split_ahead(phase, Turn(n - 4))
                split_ahead(phase, Turn(n - 3))
                new_square(phase, r, 0)
                split_ahead(phase, Turn(n - 2))
                norm_split(r, 0, XH)
                new_square(phase, r, 1)
                norm_split(r, 1, XH)
                split_ahead(phase, Turn(n - 1))

            def post_norm_behind(phase, r, between=None):
                n = COUNT[phase]
                split_ahead(phase, Turn(n - 4))
                post_square(phase, 0)
                split_ahead(phase, Turn(n - 3))
                new_square(phase, r, 0)
                post_square(phase, 1)
                norm_split(r, 0, XH)
                new_square(phase, r, 1)
                split_ahead(phase, Turn(n - 2))
                if between:
                    between()
                norm_split(r, 1, XH)
                split_ahead(phase, Turn(n - 1))

            norm_behind("w_out", "norm_xq")
            pre_gain_load("norm_ffn")
            take_t("mem_k", 0, MK)
            for t in range(NT):
                acc_is_taken(act, "mem_k", Turn(0), t)
                act.activation(MSQ[:, t, :], MK[:, t, :], ACT.Square).then_inc(heads_sq, 1)
            split_ahead("mem_k", Turn(0))
            split_ahead("mem_k", Turn(1))
            take_small("mkT0", MKT[:, :, tok(0)], by_head(small("mkT0")), col("mk_norm"))
            split_ahead("mem_q", Turn(0))
            take_t("mem_q", 0, MQ)
            act.wait_ge(heads_ready, 8)
            for t in range(NT):
                acc_is_taken(act, "mem_q", Turn(0), t)
                act.activation(MSQ[:, t, :], MQ[:, t, :], ACT.Square).then_inc(heads_sq, 1)
            split_ahead("mem_q", Turn(1))
            split_ahead("mem_v", Turn(0))
            take_small("mqT0", MQT[:, :, tok(0)], by_head(small("mqT0")), col("mq_norm"))
            for t in range(NT):
                for i, part in enumerate("ab"):
                    act.wait_ge(row_max, 3 + 2 * t + i + 1)
                    softmax_exp(f"mS{t}{part}", MPR[:, t, 2 * i:2 * i + 2, :], by_head(small(f"mS{t}{part}"), SEQ), 4 * t + 2 * i)
            take_t("mem_v", 0, MV)
            split_ahead("mem_v", Turn(1))
            for t in range(NT):
                take_small(f"mP{t}a", MPT[:, 0, :, tok(t)], by_head(small(f"mP{t}a")))
            for g in range(2):
                small_is_done(act, f"mo{g}")
                copy(YH[:, 2 * g:2 * g + 2, :], by_head(small(f"mo{g}"), SEQ), y_hi)
            new_square("mem_o", "norm_ffn", 0)
            norm_split("norm_ffn", 0, XH)
            split_ahead("mem_o", Turn(0))
            new_square("mem_o", "norm_ffn", 1)
            norm_split("norm_ffn", 1, XH)
            split_ahead("mem_o", Turn(1))
            act.wait_ge(block_done, FIRST["up"])
            act.dma_start(SGUW[:, :, :], A["sgu_w_2"][0].rearrange("g t s -> t g s")).then_inc(sgu_loaded, 16)
            act.dma_start(flat(BS[:, :, :]), A["sgu_b_2"][0].rearrange("g t -> (g t)").unsqueeze(0).broadcast_to([P, 4 * P])).then_inc(sgu_loaded, 16)
            post_gain_load("ffn1_post_g_2")
            pre_gain_load("ffn1_pre_g_2")

            def ffn_hi(t):
                copy(HH[:, tiles_of(t), :], UB[:, t.j % 2], h_hi)

            def up_step(t):
                u = t.j % 2
                for k, half in enumerate((UA, UB)):
                    b = t.part(k, 2)
                    acc_is_done(act, "up", b)
                    for i in range(2):
                        tile = k * FT + 2 * t.j + i
                        ins = act.activation(half[:, u, i, :], acc("up", b)[:, i * 256:(i + 1) * 256], ACT.Identity,
                                             scale=conv_tap(2, tile, t), bias=conv_bias(tile, t))
                    ins.then_inc((a_base, b_base)[k], 1)
                    if k == 1:
                        acc_is_taken(act, "up", t.part(0, 2))
                        act.activation(UA[:, u], UA[:, u], ACT.Silu).then_inc(a_act, 1)
                    split_ahead("up", b)
                act.wait_ge(h_ready, t.count(lambda j: j + 1))
                ffn_hi(t)

            repeat(act, 0, FT // 2, 2, up_step)

            def down_splits(phase):
                for j in range(COUNT[phase] - RING):
                    split_ahead(phase, Turn(j))

            down_splits("down")
            norm_behind("down", "norm_f1")
            pre_gain_load("mix_pre_g_2")

            def glu_steps(phase):
                def step(t):
                    a, b = t.part(0, 2), t.part(1, 2)
                    acc_is_done(act, phase, a)
                    act.activation(UA[:, t.j % 2], acc(phase, a).rearrange("p (n s) -> p n s", s=SEQ),
                                   ACT.Silu).then_inc(acc_bank(phase, a), 1)
                    split_ahead(phase, a)
                    split_ahead(phase, b)
                    acc_is_taken(act, phase, b)
                    ffn_hi(t)
                repeat(act, 0, FT // 2, 2, step)

            glu_steps("ffn1")
            down_splits("down1")
            post_norm_behind("down1", "norm_mix2")
            post_gain_load("mix_post_g_2")

            for chunk in range(2):
                split_ahead("mix_v", Turn(2 * chunk))
                acc_is_done(act, "mix_v", Turn(chunk))
                for m in range(NT):
                    act.activation(V2[:, m, chunk * 512:(chunk + 1) * 512], acc("mix_v", Turn(chunk), m),
                                   ACT.Gelu_apprx_tanh).then_inc(acc_bank("mix_v", Turn(chunk), m), 1)
                split_ahead("mix_v", Turn(2 * chunk + 1))
            for j in range(4):
                acc_is_done(act, "mix_u", Turn(j))
                act.activation(U2[:, 2 * j:2 * j + 2, :], acc("mix_u", Turn(j)).rearrange("p (n s) -> p n s", s=SEQ),
                               ACT.Gelu_apprx_tanh).then_inc(acc_bank("mix_u", Turn(j)), 1)
                split_ahead("mix_u", Turn(j))
                if j == 1:
                    for t in range(NT):
                        act.wait_ge(ln_mean, t + 1)
                        act.activation(XS[:, t, :], V2[:, t, :], ACT.Square, accum_out=LSS[:, t:t + 1]).then_inc(ln_sq, 1)
            for j in range(4):
                take_f("mix_c", j, C2[:, 2 * j:2 * j + 2, :], 1.0)
                split_ahead("mix_c", Turn(j))
                act.wait_ge(gated, j + 1)
                copy(HH[:, 2 * j:2 * j + 2, :], U2[:, 2 * j:2 * j + 2, :], gated_hi)
            act.wait_ge(gated_lo, 4)

            def branch_gates(phase, j, dst):
                acc_is_done(act, phase, Turn(j))
                act.activation(dst[:, 2 * j:2 * j + 2, :], acc(phase, Turn(j)).rearrange("p (n s) -> p n s", s=SEQ),
                               ACT.Sigmoid).then_inc(acc_bank(phase, Turn(j)), 1)
                split_ahead(phase, Turn(j))

            for j in range(4):
                branch_gates("mix_ga", j, SGA)
                act.wait_ge(pooled, j + 1)
                copy(HH[:, 8 + 2 * j:10 + 2 * j, :], C2[:, 2 * j:2 * j + 2, :], pooled_hi)
            for j in range(4):
                branch_gates("mix_gb", j, SGB)
            for g in range(4):
                acc_is_done(act, "pool", Turn(g))
                for i in range(2):
                    copy(HH[:, 8 + 2 * g + i, :], acc("pool", Turn(g))[:, i * 256:(i + 1) * 256], proj_hi,
                         col("pool_scale_2", 2 * g + i))
            split_ahead("pool", Turn(0))
            for j in range(4):
                split_ahead("mix_out", Turn(2 * j))
                split_ahead("mix_out", Turn(2 * j + 1))
                act.wait_ge(y2_ready, j + 1)
                copy(XH[:, 2 * j:2 * j + 2, :], SGA[:, 2 * j:2 * j + 2, :], y2_hi)
            pre_gain_load("ffn2_pre_g_2")
            post_norm_behind("mix_o", "norm_f2")
            post_gain_load("ffn2_post_g_2")
            pre_gain_load("ple_pre_g_2")
            act.dma_start(PR[:, :, :], A["p_2"][0, 0].rearrange("(t p) d -> p t d", p=P)).then_inc(p_loaded, 16)
            glu_steps("ffn2")
            small_is_done(act, "pT")
            copy(PH[:, :, :], by_head(small("pT"), SEQ), p_hi)
            down_splits("down2")

            def take_projection():
                acc_is_done(act, "ple_e", Turn(0))
                for k in range(4):
                    copy(EP[:, k // 2, k % 2 * 512:(k % 2 + 1) * 512], acc("ple_e", Turn(0), k), acc_bank("ple_e", Turn(0), k))

            post_norm_behind("down2", "norm_ple", take_projection)
            post_gain_load("ple_post_g_2")
            split_ahead("ple_e", Turn(0))
            for chunk in range(2):
                acc_is_done(act, "ple_g", Turn(chunk))
                for m in range(NT):
                    act.activation(PG[:, m, chunk * 512:(chunk + 1) * 512], acc("ple_g", Turn(chunk), m),
                                   ACT.Sigmoid).then_inc(acc_bank("ple_g", Turn(chunk), m), 1)

        @block.vector
        def _(dve):
            steps = [0]

            def link(ins):
                steps[0] += 1
                ins.then_inc(dve_step, 1)
                dve.wait_ge(dve_step, steps[0])

            def lo_of(n, hi_count):
                dve.wait_ge(hi_ready, hi_count)
                s = n % RING
                dve.tensor_tensor(LO[:, s, :], RAW[:, n % RAWS, :], HI[:, s, :].bitcast(f32), ALU.subtract).then_inc(lo_ready[s], 1)

            def split(n):
                lo_of(n, n + 1)

            def split_ahead(phase, t):
                n = FIRST[phase] + t.j + RING
                if n < N_BLOCKS and n not in ON_POOL:
                    lo_of(n, t.count(lambda j: FIRST[phase] + j + RING + 1))

            def rsqrt(dst, total, mult, n):
                ms, y, tmp = MS[:, 0:n], dst, RT[:, 0:n]
                link(dve.tensor_scalar(ms, total, mult, EPS, ALU.mult, ALU.add))
                if n == 1:
                    half = MS[:, 1:2]
                    dve.tensor_scalar(half, ms, -0.5, None, ALU.mult)
                link(dve.tensor_scalar(y.bitcast(i32), ms.bitcast(i32), -0.5, 1597463007.0, ALU.mult, ALU.add))
                for _ in range(3):
                    if n == 1:
                        link(dve.scalar_tensor_tensor(out=tmp, in0=y, scalar=y, in1=half, op0=ALU.mult, op1=ALU.mult))
                        link(dve.scalar_tensor_tensor(out=y, in0=tmp, scalar=1.5, in1=y, op0=ALU.add, op1=ALU.mult))
                    else:
                        link(dve.tensor_tensor(tmp, y, y, ALU.mult))
                        link(dve.scalar_tensor_tensor(out=tmp, in0=tmp, scalar=-0.5, in1=ms, op0=ALU.mult, op1=ALU.mult))
                        link(dve.scalar_tensor_tensor(out=y, in0=tmp, scalar=1.5, in1=y, op0=ALU.add, op1=ALU.mult))

            def copy(dst, src, signal):
                dve.tensor_copy(dst, src).then_inc(signal, 1)

            def take_small(name, dst, src):
                small_is_done(dve, name)
                copy(dst, src, bank_of(name))

            def norm_scale(r, t, src, dst):
                n = NORMS.index(r)
                dve.wait_ge(sumsq, 2 * n + t + 1)
                rsqrt(RS[:, t:t + 1], SS[r][:, t:t + 1], 1.0 / DM, 1)
                dve.wait_ge(pre_gain_loaded, 16 * (n + 1))
                for half in (slice(0, DM // 2), slice(DM // 2, DM)):
                    dve.scalar_tensor_tensor(out=dst[:, t, half], in0=src[:, t, half], scalar=RS[:, t:t + 1],
                                             in1=PRE_GAIN[:, half], op0=ALU.mult, op1=ALU.mult).then_inc(scaled, 1)

            def norm_split(r, t, hi, lo):
                for b in range(2):
                    name = f"{r}.{t}{b}"
                    dve.wait_ge(norm_hi, 4 * NORMS.index(r) + 2 * t + b + 1)
                    quarter = slice(4 * b, 4 * b + 4)
                    dve.tensor_tensor(lo[:, quarter, tok(t)], by_head(small(name)), hi[:, quarter, tok(t)].bitcast(f32),
                                      ALU.subtract).then_inc(bank_of(name), 1)

            def heads_norm(n, squares, mult, width):
                heads = width // P
                for t in range(NT):
                    dve.wait_ge(heads_sq, 2 * n + t + 1)
                    link(dve.tensor_reduce(HSS[:, t * heads:(t + 1) * heads], by_head(squares[:, t, :]), AX, ALU.add))
                rsqrt(RS[:, 0:NT * heads], HSS[:, 0:NT * heads], mult, NT * heads)

            def heads_scale(rows_, heads):
                for t in range(NT):
                    x = by_head(rows_(t))
                    dve.tensor_tensor(x, x, per_head(RS[:, t * heads:(t + 1) * heads], P), ALU.mult).then_inc(heads_ready, 1)

            def y_split(n, names, view):
                for i, name in enumerate(names):
                    dve.wait_ge(y_hi, n + i + 1)
                    hi, lo, src = view(i)
                    dve.tensor_tensor(lo, src, hi.bitcast(f32), ALU.subtract).then_inc(bank_of(name), 1)

            for t in range(NT):
                dve.wait_ge(x_loaded[t], 16)
                norm_scale("norm_mix", t, X, XS)
            split(0)
            for t in range(NT):
                norm_split("norm_mix", t, XH, XL)
            split(1)
            take_small("cols0", COL[0][:, :], small("cols0")[:, 0:COL_N[0]])
            small_is_done(dve, "cols1")
            dve.tensor_copy(FCONV[:, P:CONV_N], small("cols1")[:, COL_N[1]:COL_N[1] + CONV_TAIL])
            copy(COL[1][:, :], small("cols1")[:, 0:COL_N[1]], bank_of("cols1"))
            take_small("cols2", FCONV[:, 0:P], small("cols2")[:, 0:P])
            small_is_taken(dve, "cols0")
            link(dve.tensor_scalar(col("fox_qnorm"), col("fox_qnorm"), DH ** -0.5, None, ALU.mult))
            link(dve.tensor_scalar(col("mq_norm"), col("mq_norm"), DH ** -0.5, None, ALU.mult))

            for n in range(2, RING):
                split(n)
            dve.wait_ge(tiny_hi, 1)
            dve.tensor_tensor(TLO[:, :, :], TW[:, :, :], THI[:, :, :].bitcast(f32), ALU.subtract).then_inc(tiny_lo, 1)

            for j in range(6):
                dve.wait_ge(conv_base, 2 * j + 2)
                for i in range(2):
                    tile = 2 * j + i
                    u = acc("gdn", Turn(j))[:, i * 256:(i + 1) * 256]
                    for back in (1, 2, 3):
                        y = CONVF[:, tile, back:SEQ]
                        ins = dve.scalar_tensor_tensor(out=y, in0=u[:, 0:SEQ - back], scalar=col("gdn_conv", (3 - back) * 12 + tile),
                                                       in1=y, op0=ALU.mult, op1=ALU.add)
                        if i == 0 or back < 3:
                            link(ins)
                ins.then_inc(acc_bank("gdn", Turn(j)), 1)
                split_ahead("gdn", Turn(j))
            small_is_done(dve, "tiny")
            dve.wait_ge(masks_ready, 2)
            tiny = small("tiny")[:, 0:32].rearrange("p (t c) -> p t c", t=NT)[:, :, 0:12]
            dve.wait_ge(tiny_loaded, 16 * 3)
            dve.tensor_tensor(TY, tiny, every(BROW, NT), ALU.add).then_inc(bank_of("tiny"), 1)
            small_is_taken(dve, "tiny")
            link(dve.tensor_tensor(TY, TY, every(SGN, NT), ALU.mult))
            dve.scalar_tensor_tensor(out=TE, in0=TY, scalar=-1.0, in1=TY, op0=ALU.mult, op1=ALU.max).then_inc(tiny_abs, 1)
            split_ahead("sbqk", Turn(0))
            take_small("gTq1", GT[:, 1, 0, :], small("gTq1"))
            take_small("gTk1", GT[:, 1, 1, :], small("gTk1"))
            dve.wait_ge(tiny_ln, 1)
            dve.scalar_tensor_tensor(out=TS, in0=TY, scalar=0.0, in1=TE, op0=ALU.max, op1=ALU.add).then_inc(tiny_sp, 1)
            split_ahead("sbqk", Turn(1))
            dve.wait_ge(tiny_exp, 1)
            dve.tensor_tensor(NG, TS[:, :, 8:12], every(EA, NT), ALU.mult).then_inc(rates_ready, 1)
            take_small("gTv1", GT[:, 1, 2, :], small("gTv1"))
            heads_norm(0, GSQ, 1.0, 2 * HW)
            rq = RS[:, 0:16].rearrange("p (t h) -> p t h", t=NT)[:, :, 0:4]
            link(dve.tensor_scalar(rq, rq, DH ** -0.5, None, ALU.mult))
            heads_scale(lambda t: flat(GT[:, t, 0:2, :]), 8)
            split_ahead("sbqk", Turn(2))
            small_is_done(dve, "gcol")
            link(dve.tensor_copy(NC, small("gcol")[:, 0:8].rearrange("p (t c) -> p t c", t=NT)))
            dve.tensor_tensor(KD, NC[:, 0, :], small("gcol")[:, 8:12], ALU.subtract).then_inc(bank_of("gcol"), 1)
            for t in range(NT):
                small_is_done(dve, f"grow{t}")
                for h in range(HEADS):
                    row = small(f"grow{t}")[:, h * P:(h + 1) * P]
                    dve.tensor_scalar(MA[:, t, h, :], row, NC[:, t, h:h + 1], 0.0, ALU.subtract, ALU.min)
                    ins = dve.tensor_scalar(MB[:, t, h, :], row, NC[:, t, h:h + 1], 0.0, ALU.subtract, ALU.max)
                ins.then_inc(bank_of(f"grow{t}"), 1)
            split_ahead("sbqk", Turn(3))
            take_small("gFq1", QKF[:, 0:4, tok(1)], by_head(small("gFq1")))
            take_small("gFk1", QKF[:, 4:8, tok(1)], by_head(small("gFk1")))
            for t in range(NT):
                dve.wait_ge(decay_ready, 2 * t + 2)
                link(dve.tensor_tensor(MB[:, t], MB[:, t], every(TRI, HEADS), ALU.mult))
            split_ahead("sbv", Turn(0))
            for t in range(NT):
                small_is_done(dve, f"kk{t}")
                for h in range(HEADS):
                    ins = dve.scalar_tensor_tensor(out=DL[:, t, h, :], in0=small(f"kk{t}")[:, h * P:(h + 1) * P],
                                                   scalar=BETA[:, t, h:h + 1], in1=MA[:, t, h, :], op0=ALU.mult, op1=ALU.mult)
                ins.then_inc(bank_of(f"kk{t}"), 1)
            for t in range(NT):
                small_is_done(dve, f"kq{t}")
                dve.tensor_tensor(MAT[:, t], by_head(small(f"kq{t}")), MB[:, t], ALU.mult).then_inc(bank_of(f"kq{t}"), 1)
            split_ahead("sbv", Turn(1))
            for h in range(HEADS):
                small_is_taken(dve, f"z{h}")
            dve.scalar_tensor_tensor(out=SP_[:, :, :], in0=Z[:, :, :], scalar=-1.0, in1=Z[:, :, :], op0=ALU.mult, op1=ALU.max).then_inc(keep_abs, 1)

            def first_factor(t):
                name = f"Dt{t}"
                small_is_done(dve, name)
                dve.tensor_copy(MB[:, t], by_head(small(name)))
                dve.tensor_tensor(MP[:, t], every(IDENT[:, :], HEADS), by_head(small(name)), ALU.subtract).then_inc(bank_of(name), 1)

            for t in range(NT):
                first_factor(t)
            split_ahead("foxqk", Turn(0))
            take_small("D2_1", MC[:, 1], by_head(small("D2_1")))
            take_small("D2t_1", ME[:, 1], by_head(small("D2t_1")))
            dve.wait_ge(keep_ln, 1)
            link(dve.scalar_tensor_tensor(out=SP_[:, :, :], in0=Z[:, :, :], scalar=0.0, in1=SP_[:, :, :], op0=ALU.max, op1=ALU.add))
            link(dve.tensor_tensor(SP_[:, :, 0:P], SP_[:, :, 0:P], every(BEFORE[:, :], HEADS), ALU.mult))
            dve.tensor_tensor(SP_[:, :, SEQ:SEQ + P], SP_[:, :, SEQ:SEQ + P], every(BEFORE[:, :], HEADS), ALU.mult).then_inc(keep_ready, 1)
            split_ahead("foxqk", Turn(1))

            def factor(n, t):
                name = f"P{n}_{t}"
                small_is_done(dve, name)
                dve.tensor_tensor(MP[:, t], MP[:, t], by_head(small(name)), ALU.add).then_inc(bank_of(name), 1)

            for t in range(NT):
                factor(2, t)
            take_small("D4_1", MA[:, 1], by_head(small("D4_1")))
            split_ahead("foxqk", Turn(2))
            take_small("D4t_1", MB[:, 1], by_head(small("D4t_1")))

            def stick_arg(h):
                small_is_done(dve, f"rc{h}")
                dve.tensor_tensor(Z[:, h, :], Z[:, h, :], small(f"rc{h}")[:, 0:384], ALU.subtract).then_inc(bank_of(f"rc{h}"), 1)

            for h in range(2):
                stick_arg(h)
            split_ahead("foxqk", Turn(3))
            for h in range(2, 4):
                stick_arg(h)
            for t in range(NT):
                factor(4, t)
            heads_norm(1, XS, 1.0 / DH, 2 * HW)
            heads_scale(lambda t: HT[:, t, :], 8)
            split_ahead("foxv", Turn(0))
            take_small("D8_1", MC[:, 1], by_head(small("D8_1")))
            split_ahead("foxv", Turn(1))
            for t in range(NT):
                factor(8, t)
            y_split(0, ("so0", "so1"), lambda g: (YH[:, 2 * g:2 * g + 2, :], YL[:, 2 * g:2 * g + 2, :], by_head(small(f"so{g}"), SEQ)))
            split_ahead("gate_c", Turn(0))
            take_small("T16_1", ME[:, 1], by_head(small("T16_1")))
            split_ahead("gate_c", Turn(1))
            for i, (part, gain) in enumerate((("q", "fox_qnorm"), ("k", "fox_knorm"))):
                name = f"fT{part}1"
                small_is_done(dve, name)
                dve.tensor_scalar(FQK[:, 4 * i:4 * i + 4, tok(1)], by_head(small(name)), col(gain), None, ALU.mult).then_inc(bank_of(name), 1)
            split_ahead("gate_c", Turn(2))
            take_small("Z16_1", MB[:, 1], by_head(small("Z16_1")))
            split_ahead("gate_c", Turn(3))

            def join(b, both=True):
                for t in range(NT):
                    name = f"Tt{b}_{t}"
                    small_is_done(dve, name)
                    dve.tensor_tensor(MP[:, t], MP[:, t], by_head(small(name)), ALU.subtract).then_inc(bank_of(name), 1)
                for t in range(NT if both else 0):
                    name = f"T{b}_{t}"
                    small_is_done(dve, name)
                    dve.tensor_tensor(ME[:, t], ME[:, t], by_head(small(name)), ALU.subtract).then_inc(bank_of(name), 1)

            def row_maxima(name, scores, first):
                small_is_done(dve, name)
                m = MX[:, first:first + scores.shape[1]]
                link(dve.tensor_reduce(m, scores, AX, ALU.max))
                dve.tensor_scalar(m, m, -1.0, None, ALU.mult).then_inc(row_max, 1)

            def normalise(names, rows_, first):
                for n in names:
                    small_is_taken(dve, n)
                s = RSUM[:, first:first + rows_.shape[1]]
                link(dve.reciprocal(s, s))
                dve.tensor_tensor(rows_, rows_, per_head(s, rows_.shape[2]), ALU.mult).then_inc(probs_ready, 1)

            def mix(g, j):
                phase = f"out_{g}"
                acc_is_done(dve, phase, Turn(j))
                for i in range(2 * j, 2 * j + 2):
                    acc_is_taken(dve, f"gate_{g}", Turn(i))
                for k in range(2):
                    tiles = slice(4 * j + 2 * k, 4 * j + 2 * k + 2)
                    src = acc(phase, Turn(j), k).rearrange("p (n s) -> p n s", s=SEQ)
                    dst = MIX if g == "c" else G
                    dve.tensor_tensor(dst[:, tiles, :], src, G[:, tiles, :], ALU.mult).then_inc(acc_bank(phase, Turn(j), k), 1)
                if g == "c":
                    return
                for k in range(2):
                    tiles = slice(4 * j + 2 * k, 4 * j + 2 * k + 2)
                    acc_is_taken(dve, phase, Turn(j), k)
                    ins = dve.tensor_tensor(MIX[:, tiles, :], MIX[:, tiles, :], G[:, tiles, :], ALU.add)
                    ins.then_inc(mixed_ready if g == "b" else dve_mix, 1)

            join(32)
            mix("c", 0)
            split_ahead("out_c", Turn(0))
            row_maxima("fS0", by_head(small("fS0")), 0)
            row_maxima("fS1a", by_head(small("fS1a"), SEQ), 4)
            row_maxima("fS1b", by_head(small("fS1b"), SEQ), 6)
            mix("c", 1)
            split_ahead("out_c", Turn(1))
            take_small("Z32_1", MB[:, 1], by_head(small("Z32_1")))
            normalise(("fS0",), FP0[:, :, :], 0)
            normalise(("fS1a", "fS1b"), FP1[:, :, :], 4)
            split_ahead("gate_a", Turn(0))
            join(64)
            dve.wait_ge(rates_exp, 1)
            dve.tensor_tensor(by_head(GT[:, 0, 0, :]), by_head(GT[:, 0, 2, :]), per_head(BETA[:, 0, :], P), ALU.mult).then_inc(rhs_ready, 1)
            dve.tensor_tensor(by_head(GT[:, 0, 1, :]), by_head(GT[:, 0, 1, :]), per_head(KD, P), ALU.mult).then_inc(rhs_ready, 1)
            split_ahead("gate_a", Turn(1))
            take_small("fP1b", FPT1[:, 1], by_head(small("fP1b")))
            split_ahead("gate_a", Turn(2))
            y_split(2, ("fo0", "fo1"), lambda t: (YH[:, :, tok(t)], YL[:, :, tok(t)], by_head(small(f"fo{t}"))))
            take_small("Z64_1", MB[:, 1], by_head(small("Z64_1")))
            split_ahead("gate_a", Turn(3))
            join(128, both=False)
            mix("a", 0)
            split_ahead("out_a", Turn(0))
            mix("a", 1)
            split_ahead("out_a", Turn(1))
            split_ahead("gz", Turn(0))
            small_is_done(dve, "kS")
            dve.tensor_tensor(MB[:, 0], by_head(small("kS")), per_head(EGC[:, 1, :], P), ALU.mult).then_inc(bank_of("kS"), 1)
            small_is_done(dve, "qS")
            dve.tensor_tensor(MB[:, 1], by_head(small("qS")), per_head(EGC[:, 1, :], P), ALU.mult).then_inc(bank_of("qS"), 1)
            small_is_taken(dve, "kS")
            link(dve.tensor_tensor(MB[:, 0], by_head(GT[:, 1, 2, :]), MB[:, 0], ALU.subtract))
            dve.tensor_tensor(by_head(GT[:, 1, 2, :]), MB[:, 0], per_head(BETA[:, 1, :], P), ALU.mult).then_inc(rhs_ready, 1)
            split_ahead("gz", Turn(1))
            split_ahead("gate_b", Turn(0))
            small_is_done(dve, "o1")
            small_is_taken(dve, "qS")
            dve.tensor_tensor(by_head(DO[:, 1, :]), by_head(small("o1")), MB[:, 1], ALU.add).then_inc(bank_of("o1"), 1)
            heads_norm(2, OSQ, 1.0 / DH, HW)
            heads_scale(lambda t: DO[:, t, :], 4)
            split_ahead("gate_b", Turn(1))
            split_ahead("gate_b", Turn(2))
            for j in range(2):
                acc_is_taken(dve, "gz", Turn(j))
            for t in range(NT):
                name = f"yT{t}"
                small_is_done(dve, name)
                dve.scalar_tensor_tensor(out=YB[:, :, tok(t)], in0=by_head(small(name)), scalar=col("gdn_onorm"),
                                         in1=GZS[:, :, tok(t)], op0=ALU.mult, op1=ALU.mult).then_inc(bank_of(name), 1)
            for t in range(NT):
                dve.wait_ge(y_hi, 4 + t + 1)
                dve.tensor_tensor(YL[:, :, tok(t)], YB[:, :, tok(t)], YH[:, :, tok(t)].bitcast(f32), ALU.subtract).then_inc(y_lo, 1)
            split_ahead("gate_b", Turn(3))
            for t in range(NT):
                norm_scale("norm_mem", t, MEM, MEM)
            for j in range(2):
                dve.wait_ge(dve_mix, 4)
                mix("b", j)
                for k in range(2):
                    i = 2 * j + k
                    dve.wait_ge(mixed_hi, i + 1)
                    dve.tensor_tensor(XL[:, 2 * i:2 * i + 2, :], MIX[:, 2 * i:2 * i + 2, :], XH[:, 2 * i:2 * i + 2, :].bitcast(f32),
                                      ALU.subtract).then_inc(mixed_lo, 1)
                split_ahead("out_b", Turn(j))
                if j == 0:
                    for t in range(NT):
                        norm_split("norm_mem", t, MH, MLO)

            def add_residual(phase, m):
                tile_is_done(dve, phase, m)
                for k in range(2):
                    part = X[:, m, k * 512:(k + 1) * 512]
                    dve.tensor_tensor(part, part, acc(phase, Turn(0), 2 * m + k), ALU.add).then_inc(acc_bank(phase, Turn(0), 2 * m + k), 1)
                acc_is_taken(dve, phase, Turn(0), 2 * m)
                acc_is_taken(dve, phase, Turn(0), 2 * m + 1)

            def norm_behind(phase, r):
                n = COUNT[phase]
                split_ahead(phase, Turn(n - 4))
                for m in range(NT):
                    add_residual(phase, m)
                    norm_scale(r, m, X, XS)
                    norm_split(r, m, XH, XL)
                split_ahead(phase, Turn(n - 1))

            dve.wait_ge(x_again, 16)
            norm_behind("w_out", "norm_xq")
            heads_norm(3, MSQ, 1.0 / DH, HW)
            heads_scale(lambda t: MK[:, t, :], 4)
            split_ahead("mem_k", Turn(0))
            split_ahead("mem_k", Turn(1))

            def take_scaled(name, dst, gain):
                small_is_done(dve, name)
                dve.tensor_scalar(dst, by_head(small(name)), col(gain), None, ALU.mult).then_inc(bank_of(name), 1)

            take_scaled("mkT1", MKT[:, :, tok(1)], "mk_norm")
            heads_norm(4, MSQ, 1.0 / DH, HW)
            heads_scale(lambda t: MQ[:, t, :], 4)
            take_scaled("mqT1", MQT[:, :, tok(1)], "mq_norm")
            for t in range(NT):
                for i, part in enumerate("ab"):
                    row_maxima(f"mS{t}{part}", by_head(small(f"mS{t}{part}"), SEQ), 4 * t + 2 * i)
            for t in range(NT):
                for i, part in enumerate("ab"):
                    normalise((f"mS{t}{part}",), MPR[:, t, 2 * i:2 * i + 2, :], 4 * t + 2 * i)
            for t in range(NT):
                take_small(f"mP{t}b", MPT[:, 1, :, tok(t)], by_head(small(f"mP{t}b")))
            y_split(6, ("mo0", "mo1"), lambda g: (YH[:, 2 * g:2 * g + 2, :], YL[:, 2 * g:2 * g + 2, :], by_head(small(f"mo{g}"), SEQ)))
            for m in range(NT):
                add_residual("mem_o", m)
                norm_scale("norm_ffn", m, X, XS)
                norm_split("norm_ffn", m, XH, XL)
            split_ahead("mem_o", Turn(1))

            def hidden_lo(t, pairs):
                dve.wait_ge(h_hi, t.count(lambda j: pairs + j + 1))
                dve.tensor_tensor(HL[:, tiles_of(t), :], UB[:, t.j % 2], HH[:, tiles_of(t), :].bitcast(f32),
                                  ALU.subtract).then_inc(h_lo, 1)

            def up_step(t):
                u = t.j % 2
                for k, half in enumerate((UA, UB)):
                    b = t.part(k, 2)
                    dve.wait_ge((a_base, b_base)[k], t.count(lambda j: j + 1))
                    for back in (1, 2):
                        for i in range(2):
                            if back == 2:
                                dve.wait_ge(tap_done, t.count(lambda j: 4 * j + 2 * k + i + 1))
                            y = half[:, u, i, back:SEQ]
                            ins = dve.scalar_tensor_tensor(out=y, in0=acc("up", b)[:, i * 256:i * 256 + SEQ - back],
                                                           scalar=conv_tap(2 - back, k * FT + 2 * t.j + i, t), in1=y,
                                                           op0=ALU.mult, op1=ALU.add)
                            if back == 1:
                                ins.then_inc(tap_done, 1)
                    ins.then_inc(acc_bank("up", b), 1)
                    if k == 1:
                        dve.wait_ge(a_act, t.count(lambda j: j + 1))
                        acc_is_taken(dve, "up", b)
                        dve.tensor_tensor(UB[:, u], UB[:, u], UA[:, u], ALU.mult).then_inc(h_ready, 1)
                    split_ahead("up", b)
                hidden_lo(t, 0)

            repeat(dve, 0, FT // 2, 2, up_step)

            def down_splits(phase):
                for j in range(COUNT[phase] - RING):
                    split_ahead(phase, Turn(j))

            down_splits("down")
            norm_behind("down", "norm_f1")

            def glu_steps(phase, pairs):
                def step(t):
                    a, b = t.part(0, 2), t.part(1, 2)
                    split_ahead(phase, a)
                    acc_is_done(dve, phase, b)
                    acc_is_taken(dve, phase, a)
                    dve.tensor_tensor(UB[:, t.j % 2], acc(phase, b).rearrange("p (n s) -> p n s", s=SEQ), UA[:, t.j % 2],
                                      ALU.mult).then_inc(acc_bank(phase, b), 1)
                    split_ahead(phase, b)
                    hidden_lo(t, pairs)
                repeat(dve, 0, FT // 2, 2, step)

            def post_norm(n, phase, factor, m):
                dve.wait_ge(post_sq, 2 * n + m + 1)
                rsqrt(RS[:, m:m + 1], PSS[phase][:, m:m + 1], 1.0 / DM, 1)
                dve.wait_ge(post_gain_loaded, 16 * (n + 1))
                dve.scalar_tensor_tensor(out=XS[:, m, :], in0=flat(ACCP[:, 2 * m:2 * m + 2, :]), scalar=RS[:, m:m + 1],
                                         in1=POST_GAIN[:, :], op0=ALU.mult, op1=ALU.mult).then_inc(acc_bank(phase, Turn(0), 2 * m), 1)
                acc_is_taken(dve, phase, Turn(0), 2 * m)
                dve.scalar_tensor_tensor(out=X[:, m, :], in0=XS[:, m, :], scalar=factor, in1=X[:, m, :],
                                         op0=ALU.mult, op1=ALU.add).then_inc(acc_bank(phase, Turn(0), 2 * m + 1), 1)
                acc_is_taken(dve, phase, Turn(0), 2 * m + 1)

            def post_norm_behind(n, phase, r, factor):
                blocks = COUNT[phase]
                split_ahead(phase, Turn(blocks - 4))
                post_norm(n, phase, factor, 0)
                norm_scale(r, 0, X, XS)
                post_norm(n, phase, factor, 1)
                norm_split(r, 0, XH, XL)
                norm_scale(r, 1, X, XS)
                norm_split(r, 1, XH, XL)
                split_ahead(phase, Turn(blocks - 1))

            glu_steps("ffn1", FT // 2)
            down_splits("down1")
            post_norm_behind(0, "down1", "norm_mix2", 0.5)

            for j in range(4):
                split_ahead("mix_v", Turn(j))
            small_is_done(dve, "sguw")
            dve.tensor_tensor(WST[:, :, :], by_head(small("sguw")), every(TRI, 4), ALU.mult).then_inc(bank_of("sguw"), 1)
            split_ahead("mix_u", Turn(0))
            for t in range(NT):
                for chunk in range(2):
                    acc_is_taken(dve, "mix_v", Turn(chunk), t)
                link(dve.tensor_reduce(MEAN[:, t:t + 1], V2[:, t, :], AX, ALU.add))
                link(dve.tensor_scalar(MEAN[:, t:t + 1], MEAN[:, t:t + 1], 1.0 / DM, None, ALU.mult))
                dve.tensor_scalar(V2[:, t, :], V2[:, t, :], MEAN[:, t:t + 1], None, ALU.subtract).then_inc(ln_mean, 1)
            split_ahead("mix_u", Turn(1))
            dve.wait_ge(ln_sq, NT)
            rsqrt(RS[:, 0:2], LSS, 1.0 / DM, 2)
            for t in range(NT):
                dve.tensor_scalar(V2[:, t, :], V2[:, t, :], RS[:, t:t + 1], None, ALU.mult).then_inc(ln_ready, 1)
            split_ahead("mix_u", Turn(2))
            split_ahead("mix_u", Turn(3))
            dve.wait_ge(sgu_loaded, 32)
            for g in range(4):
                split_ahead("mix_c", Turn(g))
                name = f"sgu{g}"
                small_is_done(dve, name)
                for i in range(2):
                    d = 2 * g + i
                    ins = dve.scalar_tensor_tensor(out=by_head(G[:, d, :]), in0=by_head(small(name)[:, i * SEQ:(i + 1) * SEQ]),
                                                   scalar=col("sgu_norm_g_2", d), in1=every(BS[:, g, :], NT),
                                                   op0=ALU.mult, op1=ALU.add)
                ins.then_inc(bank_of(name), 1)
                small_is_taken(dve, name)
                acc_is_taken(dve, "mix_u", Turn(g))
                pair = slice(2 * g, 2 * g + 2)
                dve.tensor_tensor(U2[:, pair, :], U2[:, pair, :], G[:, pair, :], ALU.mult).then_inc(gated, 1)
                dve.wait_ge(gated_hi, g + 1)
                dve.tensor_tensor(HL[:, pair, :], U2[:, pair, :], HH[:, pair, :].bitcast(f32), ALU.subtract).then_inc(gated_lo, 1)
            for g, (sums, size) in enumerate(zip((S2A[:, :, :], S4[:, 0:2, :], S8[:, 0:2, :], S16[:, :, :]), POOL_WINDOWS)):
                split_ahead("mix_ga", Turn(g))
                dve.wait_ge(windows_ready, (2, 3, 4, 5)[g])
                link(dve.tensor_tensor(sums[:, :, 0:16], sums[:, :, 0:16], every(INV16[:, g, :], 2), ALU.mult))
                pair, dst = slice(2 * g, 2 * g + 2), slice(8 + 2 * g, 10 + 2 * g)
                dve.scalar_tensor_tensor(out=C2[:, pair, :], in0=sums, scalar=1.0 / size, in1=C2[:, pair, :],
                                         op0=ALU.mult, op1=ALU.subtract).then_inc(pooled, 1)
                dve.wait_ge(pooled_hi, g + 1)
                dve.tensor_tensor(HL[:, dst, :], C2[:, pair, :], HH[:, dst, :].bitcast(f32), ALU.subtract).then_inc(pooled_lo, 1)
            for j in range(4):
                split_ahead("mix_gb", Turn(j))
            for g in range(4):
                dve.wait_ge(proj_hi, 2 * g + 2)
                for i in range(2):
                    d = 2 * g + i
                    ins = dve.scalar_tensor_tensor(out=HL[:, 8 + d, :], in0=acc("pool", Turn(g))[:, i * 256:(i + 1) * 256],
                                                   scalar=col("pool_scale_2", d), in1=HH[:, 8 + d, :].bitcast(f32),
                                                   op0=ALU.mult, op1=ALU.subtract)
                ins.then_inc(acc_bank("pool", Turn(g)), 1)
            split_ahead("pool", Turn(0))
            for j in range(4):
                pair = slice(2 * j, 2 * j + 2)
                for k, (gate, dst) in enumerate((("mix_ga", SGA), ("mix_gb", SGB))):
                    t = Turn(2 * j + k)
                    acc_is_taken(dve, gate, Turn(j))
                    acc_is_done(dve, "mix_out", t)
                    dve.tensor_tensor(dst[:, pair, :], acc("mix_out", t).rearrange("p (n s) -> p n s", s=SEQ), dst[:, pair, :],
                                      ALU.mult).then_inc(acc_bank("mix_out", t), 1)
                    split_ahead("mix_out", t)
                for k in range(2):
                    acc_is_taken(dve, "mix_out", Turn(2 * j + k))
                dve.tensor_tensor(SGA[:, pair, :], SGA[:, pair, :], SGB[:, pair, :], ALU.add).then_inc(y2_ready, 1)
                dve.wait_ge(y2_hi, j + 1)
                dve.tensor_tensor(XL[:, pair, :], SGA[:, pair, :], XH[:, pair, :].bitcast(f32), ALU.subtract).then_inc(y2_lo, 1)
            post_norm_behind(1, "mix_o", "norm_f2", 1.0)

            glu_steps("ffn2", 2 * (FT // 2))
            dve.wait_ge(p_hi, 1)
            dve.tensor_tensor(PL[:, :, :], by_head(small("pT"), SEQ), PH[:, :, :].bitcast(f32), ALU.subtract).then_inc(bank_of("pT"), 1)
            down_splits("down2")
            post_norm_behind(2, "down2", "norm_ple", 0.5)
            split_ahead("ple_e", Turn(0))

            for t in range(NT):
                for k in range(2):
                    acc_is_taken(dve, "ple_e", Turn(0), 2 * t + k)
                    acc_is_taken(dve, "ple_g", Turn(k), t)
                link(dve.tensor_tensor(PG[:, t, :], PG[:, t, :], EP[:, t, :], ALU.mult))
                link(dve.tensor_tensor_reduce(out=EP[:, t, :], in0=PG[:, t, :], in1=PG[:, t, :], scale=1.0, scalar=0.0,
                                              op0=ALU.mult, op1=ALU.add, accum_out=POST[:, t:t + 1]))
            rsqrt(RS[:, 0:2], POST, 1.0 / DM, 2)
            dve.wait_ge(post_gain_loaded, 16 * 4)
            for t in range(NT):
                link(dve.scalar_tensor_tensor(out=PG[:, t, :], in0=PG[:, t, :], scalar=RS[:, t:t + 1], in1=POST_GAIN[:, :],
                                              op0=ALU.mult, op1=ALU.mult))
                dve.tensor_tensor(X[:, t, :], X[:, t, :], PG[:, t, :], ALU.add).then_inc(out_ready, 1)


def kernel(**inputs):
    import numpy as np
    import concourse.bacc as bacc
    from concourse.bass_utils import run_bass_kernel_spmd

    nc = bacc.Bacc("TRN2", target_bir_lowering=False, num_devices=1)
    arrays, args = {}, {}
    for name, value in inputs.items():
        a = np.ascontiguousarray(value)
        arrays[f"in_{name}_dram"] = a
        args[name] = nc.dram_tensor(f"in_{name}_dram", a.shape, mybir.dt.from_np(a.dtype), kind="ExternalInput").ap()
    out = nc.dram_tensor("out_0_dram", (1, SEQ, DM), mybir.dt.float32, kind="ExternalOutput").ap()
    build(nc, args, out)
    r = run_bass_kernel_spmd(nc, [arrays], core_ids=[0])
    return r.results[0]["out_0_dram"]
```

```python
from contextlib import ExitStack

import concourse.bass as bass
from concourse import mybir

P = 128
SEQ = 256
NT = SEQ // P
DM = 1024
KT = DM // P
HEADS = 4
DH = 128
HW = HEADS * DH
DFF = 2816
FT = DFF // P
BLOCK = 2048
HALF = BLOCK // 2
RAWS = 2
RING = 4
EPS = 1e-6
BIG = 1e30
POOL_WINDOWS = (2, 4, 8, 16)

C_FQ, C_FK, C_FV, C_FF = 0, HW, 2 * HW, 3 * HW
C_GQKV = C_FF + HEADS
C_GB = C_GQKV + 3 * HW
C_GZ = C_GB + 2 * HEADS
C_SQ = C_GZ + HW
C_SK, C_SV = C_SQ + HW, C_SQ + 2 * HW
C_GATE = C_SQ + 3 * HW

PHASES = [
    ("gdn", 6), ("sbqk", 4), ("sbv", 2), ("foxqk", 4), ("foxv", 2),
    ("gate_c", 4), ("out_c", 2), ("gate_a", 4), ("out_a", 2), ("gz", 2), ("gate_b", 4), ("out_b", 2),
    ("w_out", 4), ("mem_k", 2), ("mem_q", 2), ("mem_v", 2), ("mem_o", 2),
    ("up", 22), ("down", 11),
    ("ffn1", 22), ("down1", 11),
    ("mix_v", 4), ("mix_u", 4), ("mix_c", 4), ("mix_ga", 4), ("mix_gb", 4), ("pool", 1), ("mix_out", 8), ("mix_o", 4),
    ("ffn2", 22), ("down2", 11),
    ("ple_e", 1), ("ple_g", 4),
]
FIRST = {}
_n = 0
for _name, _count in PHASES:
    FIRST[_name] = _n
    _n += _count
N_BLOCKS = _n
COUNT = dict(PHASES)

TILED = {"w_out": 3, "mem_o": 2, "down": 3, "down1": 4, "mix_o": 4, "down2": 4}
T_OPEN = {"mix_v": 4, "ple_g": 3}
F_OPEN = {"up": 3, "ffn1": 3, "ffn2": 4}
ON_POOL = {FIRST["mem_o"], FIRST["mem_o"] + 1, FIRST["up"]}

ACC_BANKS, ACC_LAST, ACC_TURN = {}, {}, {}


PAIRS = ("up", "ffn1", "ffn2")


def _accumulations():
    turns = [0] * 4

    def acc(phase, j, last, *banks):
        ACC_BANKS[phase, j] = banks
        ACC_LAST[phase, j] = FIRST[phase] + last
        ACC_TURN[phase, j] = {b: turns[b] for b in banks}
        for b in banks:
            turns[b] += 1

    for phase, count in PHASES:
        if phase in ("sbv", "foxqk", "foxv", "mem_k", "mem_q", "mem_v", "mix_v", "ple_g"):
            for j in range(count // 2):
                first = 2 * ((j + (phase == "mem_q")) % 2)
                acc(phase, j, 2 * j + 1, first, first + 1)
        elif phase.startswith("out_"):
            for j in range(count):
                acc(phase, j, j, 2 * j, 2 * j + 1)
        elif phase in ("w_out", "mem_o", "down", "down1", "mix_o", "down2"):
            acc(phase, 0, count - 1, 0, 1, 2, 3)
        elif phase == "ple_e":
            pass
        elif phase == "pool":
            for j in range(4):
                acc(phase, j, 0, j)
        else:
            for j in range(count):
                acc(phase, j, j, (j + (phase in PAIRS) * 2) % 4)


_accumulations()

def norm_turns(r):
    return [f"{r}.{t}{b}" for t in range(NT) for b in range(2)]


def open_turns(r, phase):
    norms = norm_turns(r)
    blocks = [f"{phase}.{t}{b}" for t in range(NT) for b in range((F_OPEN[phase] + 1) // 2)]
    return norms[:2] + blocks[:1] + norms[2:] + blocks[1:]


SMALL = norm_turns("norm_mix") + ["cols0", "cols1", "cols2", "tiny"]
SMALL += ["gTq0", "gTq1", "gTk0", "gTk1", "gTv0", "gTv1", "gcol", "grow0", "grow1", "gFq0", "gFq1", "gFk0", "gFk1"]
SMALL += ["kk0", "kk1", "kq0", "kq1", "z0", "z1", "z2", "z3", "Dt0", "Dt1", "D2_0", "D2_1", "D2t_0", "D2t_1"]
SMALL += ["P2_0", "P2_1", "D4_0", "D4_1", "D4t_0", "D4t_1", "rc0", "rc1", "rc2", "rc3", "P4_0", "P4_1"]
SMALL += ["D8_0", "D8_1", "P8_0", "P8_1", "so0", "so1", "T16_0", "T16_1", "fTq0", "fTq1", "fTk0", "fTk1"]
SMALL += ["Z16_0", "Z16_1", "Tt32_0", "Tt32_1", "T32_0", "T32_1", "fS0", "fS1a", "fS1b", "Z32_0", "Z32_1"]
SMALL += ["Tt64_0", "Tt64_1", "T64_0", "T64_1", "fP0", "fP1a", "fP1b", "fo0", "fo1", "Z64_0", "Z64_1"]
SMALL += ["Tt128_0", "Tt128_1", "vn0", "S1", "kS", "qS", "vn1", "o0", "o1", "yT0", "yT1"]
SMALL += norm_turns("norm_mem") + norm_turns("norm_xq")
SMALL += ["mkT0", "mkT1", "mqT0", "mqT1", "mS0a", "mS0b", "mS1a", "mS1b", "mP0a", "mP0b", "mP1a", "mP1b", "mo0", "mo1"]
SMALL += open_turns("norm_ffn", "up") + open_turns("norm_f1", "ffn1")
SMALL += norm_turns("norm_mix2") + ["sguw"] + [f"sgu{g}" for g in range(4)]
SMALL += open_turns("norm_f2", "ffn2") + ["pT", "norm_ple.00", "norm_ple.01", "ple.0a", "ple.0b", "ple.1a", "ple.1b", "norm_ple.10", "norm_ple.11"]
SMALL_ORDER = {name: i for i, name in enumerate(SMALL)}
BY_BLOCK = {f"{phase}.1{b}": FIRST[phase] + min(2 * b + 2, n) for phase, n in F_OPEN.items() for b in range((n + 1) // 2)}
BY_BLOCK["ple.1b"] = FIRST["ple_e"] + 1
SMALL_COUNT = {name: sum(n not in BY_BLOCK for n in SMALL[:i + 1]) for i, name in enumerate(SMALL)}

NORMS = ["norm_mix", "norm_mem", "norm_xq", "norm_ffn", "norm_f1", "norm_mix2", "norm_f2", "norm_ple"]
NORM_GAIN = dict(zip(NORMS, ["norm_mix", "norm_mem", "norm_xq", "norm_ffn", "ffn1_pre_g_2", "mix_pre_g_2",
                             "ffn2_pre_g_2", "ple_pre_g_2"]))

ROOTS = {f"norm_mix.{t}": 1 for t in range(NT)} | {"heads0": 16, "heads1": 16, "heads2": 8}
ROOTS |= {f"{r}.{t}": 1 for r in ("norm_mem", "norm_xq") for t in range(NT)} | {"heads3": 8, "heads4": 8}
ROOTS |= {f"{r}.{t}": 1 for r in ("norm_ffn", "norm_f1") for t in range(NT)}
ROOTS |= {f"{r}.{t}": 1 for t in range(NT) for r in ("down1", "norm_mix2")} | {"layer": 2}
ROOTS |= {f"{r}.{t}": 1 for phase, norm in (("mix_o", "norm_f2"), ("down2", "norm_ple")) for t in range(NT) for r in (phase, norm)}
ROOTS |= {f"last.{t}": 1 for t in range(NT)}
ROOT_ORDER = {name: i for i, name in enumerate(ROOTS)}

COL_ROWS = [
    [("sgu_norm_g_2", 8), ("pool_scale_2", 8), ("fox_qnorm", 1), ("fox_knorm", 1), ("mq_norm", 1), ("mk_norm", 1),
     ("gdn_onorm", 1), ("gate_bias", 24)],
    [("gdn_conv", 48), ("ffn_conv_b", 44)],
]
COL_AT = {}
for _tile, _names in enumerate(COL_ROWS):
    _row = 0
    for _name, _count in _names:
        COL_AT[_name] = (_tile, _row)
        _row += _count
COL_N = [sum(n for _, n in names) for names in COL_ROWS]
CONV_N = 3 * 2 * FT
CONV_TAIL = CONV_N - P
N_ROW_LOADS = sum(len(names) for names in COL_ROWS) + 2


def build(nc, A, out):
    f32, f32r, i32 = mybir.dt.float32, mybir.dt.float32r, mybir.dt.int32
    ALU = mybir.AluOpType
    ACT = mybir.ActivationFunctionType
    AX = mybir.AxisListType.X

    w = {k: A[k][0] for k in ("w_in", "w_oa", "w_ob", "w_oc", "w_out", "w_mq", "w_mkv", "w_mo", "w_up", "w_down",
                              "ffn1_w_gate_2", "ffn1_w_up_2", "ffn1_w_down_2", "w_in_2", "w_out_a_2", "w_out_b_2",
                              "w_o_2", "ffn2_w_gate_2", "ffn2_w_up_2", "ffn2_w_down_2", "ple_w_gate_2", "ple_w_proj_2")}

    def rows(m, k0, kn, c, cn):
        return m[k0 * P:(k0 + kn) * P, bass.ds(c, cn)].rearrange("(k p) n -> p k n", p=P)

    def f_block(m, c):
        return rows(m, 0, KT, c, 256)

    def t_block(m, c, half):
        return rows(m, 4 * half, 4, c, 512)

    def d_block(m, j):
        return m[bass.ds(j * 256, 256), :].rearrange("(k p) n -> p k n", p=P)

    ctx = ExitStack()
    with ctx:
        def sb(name, shape, dt=f32):
            return ctx.enter_context(nc.sbuf_tensor(name, shape, dt))

        def sem(name):
            return ctx.enter_context(nc.semaphore(name))

        RAW = sb("RAW", [P, RAWS, 2, HALF])
        HI = sb("HI", [P, RING, BLOCK], f32r)
        LO = sb("LO", [P, RING, BLOCK], f32r)
        XH = sb("XH", [P, KT, SEQ], f32r)
        XL = sb("XL", [P, KT, SEQ], f32r)
        X = sb("X", [P, NT, DM])
        XS = sb("XS", [P, NT, DM])
        COL = [sb(f"COL{i}", [P, n]) for i, n in enumerate(COL_N)]
        FCONV = sb("FCONV", [P, CONV_N])
        IDENT = sb("IDENT", [P, P])
        UPTO = sb("UPTO", [P, 2, P])
        FROM = sb("FROM", [P, P])
        NEG_AFTER = sb("NEG_AFTER", [P, P])
        BIG_NOT_BEFORE = sb("BIG_NOT_BEFORE", [P, P])
        BEFORE = sb("BEFORE", [P, P])
        DIAG16 = sb("DIAG16", [P, P])
        LEVEL = {b: sb(f"LEVEL{b}", [P, P]) for b in (16, 32, 64)}
        KEEP = sb("KEEP", [P, 1])
        ONES = UPTO[:, 1, :]
        TRI = UPTO[:, 0, :]
        STAT = sb("STAT", [P, 384])
        stat_at = [0]

        def stat(n):
            stat_at[0] += n
            return STAT[:, stat_at[0] - n:stat_at[0]]

        ARENA = 86 * 1024
        arena = sb("arena", [P, ARENA // 4])
        base = nc.sbuf_base - ARENA

        def at(name, kib, shape, dt=f32):
            size = 4
            for s in shape[1:]:
                size *= s
            assert kib * 1024 + size <= ARENA, name
            return nc.alloc_sbuf_tensor_at(name, shape, dt, offset=base + int(kib * 1024))

        CONVF = at("CONVF", 0, [P, 12, SEQ])
        QKF = at("QKF", 0, [P, 2 * HEADS, SEQ])
        GZS = at("GZS", 8, [P, HEADS, SEQ])
        GT = at("GT", 12, [P, NT, 3, HW])
        DL, MAT, MA, MB, MC, ME, MP = (at(f"delta_{n}", 24 + 4 * i, [P, NT, HEADS, P])
                                        for i, n in enumerate(["L", "AT", "A", "B", "C", "E", "P"]))
        GSQ = at("GSQ", 32, [P, NT, 2 * HW])
        OSQ = at("OSQ", 32, [P, NT, HW])
        DO = at("DO", 40, [P, NT, HW])
        YB = at("YB", 44, [P, HEADS, SEQ])
        ROWS = [at(f"ROWS{i}", 24 + 0.5 * i, [P, P]) for i in range(3)]
        SQK = at("SQK", 52, [P, 2 * HEADS, SEQ])
        SV = at("SV", 60, [P, NT, HW])
        Z = at("Z", 64, [P, HEADS, 384])
        SP_ = at("SP_", 70, [P, HEADS, 384])
        FV = at("FV", 76, [P, NT, HW])
        FQK = at("FQK", 64, [P, 2 * HEADS, SEQ])
        FP0 = at("FP0", 52, [P, HEADS, P])
        FP1 = at("FP1", 54, [P, HEADS, SEQ])
        FPT0 = at("FPT0", 58, [P, HEADS, P])
        FPT1 = at("FPT1", 60, [P, 2, HEADS, P])
        YH, YL = at("YH", 72, [P, HEADS, SEQ], f32r), at("YL", 82, [P, HEADS, SEQ], f32r)
        TW = at("TW", 80, [P, KT, 12])
        THI = at("THI", 80.5, [P, KT, 12], f32r)
        TLO = at("TLO", 81, [P, KT, 12], f32r)
        G = XS[:, :, :].rearrange("p t (k s) -> p (t k) s", s=SEQ)
        HT = X
        MIX = X[:, :, :].rearrange("p t (k s) -> p (t k) s", s=SEQ)
        MEM = at("MEM", 24, [P, NT, DM])
        MJUNK = at("MJUNK", 0, [P, NT, DM])
        MH = at("MH", 32, [P, KT, SEQ], f32r)
        MLO = at("MLO", 40, [P, KT, SEQ], f32r)
        MK = at("MK", 56, [P, NT, HW])
        MSQ = at("MSQ", 60, [P, NT, HW])
        MKT = at("MKT", 64, [P, HEADS, SEQ])
        MV = at("MV", 68, [P, NT, HW])
        MQ = at("MQ", 48, [P, NT, HW])
        MQT = at("MQT", 76, [P, HEADS, SEQ])
        MPR = at("MPR", 0, [P, NT, HEADS, SEQ])
        MPT = at("MPT", 8, [P, NT, HEADS, SEQ])
        HH = at("HH", 0, [P, FT, SEQ], f32r)
        HL = at("HL", 22, [P, FT, SEQ], f32r)
        UA = at("UA", 44, [P, 2, 2, SEQ])
        UB = at("UB", 48, [P, 2, 2, SEQ])
        OPENED = at("OPENED", 56, [P, NT, 4 * 256])
        PRE_GAIN = at("PRE_GAIN", 52, [P, DM])
        POST_GAIN = at("POST_GAIN", 82, [P, DM])
        U2 = at("U2", 44, [P, KT, SEQ])
        V2 = at("V2", 52, [P, NT, DM])
        C2 = at("C2", 60, [P, KT, SEQ])
        S2A, S2B, S4 = at("S2A", 78, [P, 2, SEQ]), at("S2B", 38, [P, 6, SEQ]), at("S4", 16, [P, 6, SEQ])
        S8, S16 = at("S8", 68, [P, 4, SEQ]), at("S16", 74, [P, 2, SEQ])
        SGA = at("SGA", 44, [P, KT, SEQ])
        SGB = at("SGB", 52, [P, KT, SEQ])
        BS = at("BS", 72, [P, 4, P])
        WST = at("WST", 76, [P, 4, P])
        SGUW = at("SGUW", 78, [P, 4, P])
        PG = at("PG", 44, [P, NT, DM])
        EP = at("EP", 66, [P, NT, DM])
        PR = at("PR", 78, [P, NT, 256])
        PH = at("PH", 62, [P, 2, SEQ], f32r)
        PL = at("PL", 64, [P, 2, SEQ], f32r)

        SS = {r: stat(2) for r in NORMS}
        PSS = {r: stat(2) for r in ("down1", "mix_o", "down2")}
        HSS = [stat(ROOTS[f"heads{n}"]) for n in range(5)]
        ROOT = {name: stat(n) for name, n in ROOTS.items()}
        BROW, SGN, EA = stat(12), stat(12), stat(4)
        TY, TE, TS = (stat(24).rearrange("p (t c) -> p t c", t=NT) for _ in range(3))
        BETA, NG, NC, EGC = (stat(8).rearrange("p (t c) -> p t c", t=NT) for _ in range(4))
        KD = stat(4)
        MX, RSUM = stat(8), stat(8)
        MINUS_HALF = stat(16)
        MEAN, LSS, POST = stat(2), stat(2), stat(4)
        assert stat_at[0] <= STAT.shape[1]
        INV16 = sb("INV16", [P, 4, 16])

        ACCP = ctx.enter_context(nc.psum_tensor("ACCP", [P, 4, 512], f32))
        SMP = ctx.enter_context(nc.psum_tensor("SMP", [P, 4, 512], f32))

        def sems(names):
            return [sem(n) for n in names.split()]

        raw_ready = [[sem(f"raw_ready{i}{h}") for h in range(2)] for i in range(RAWS)]
        x_loaded = [sem(f"x_loaded{t}") for t in range(NT)]
        hi_ready = sem("hi_ready")
        lo_ready = [sem(f"lo_ready{i}") for i in range(RING)]
        block_done = sem("block_done")
        opened = sem("opened")
        tile_done = sem("tile_done")
        small_done = sem("small_done")
        acc_taken = [sem(f"acc_taken{i}") for i in range(4)]
        small_taken = [sem(f"small_taken{i}") for i in range(4)]
        dve_step, act_step, pool_step = sems("dve_step act_step pool_step")
        x_again, mem_loaded, rows_loaded, tiny_loaded, tiny_w_loaded = sems("x_again mem_loaded rows_loaded tiny_loaded tiny_w_loaded")
        sgu_loaded, p_loaded, pre_gain_loaded, post_gain_loaded, stored = sems(
            "sgu_loaded p_loaded pre_gain_loaded post_gain_loaded stored")
        masks_ready, bias_zeroed, windows_ready = sems("masks_ready bias_zeroed windows_ready")
        sumsq, scaled, norm_hi = sems("sumsq scaled norm_hi")
        tiny_hi, tiny_lo, tiny_abs, tiny_ln, tiny_sp, tiny_exp = sems("tiny_hi tiny_lo tiny_abs tiny_ln tiny_sp tiny_exp")
        conv_base, conv_done = sems("conv_base conv_done")
        heads_sq, heads_sums, heads_ready, root_ready = sems("heads_sq heads_sums heads_ready root_ready")
        rates_ready, rates_exp, decay_ready, D_ready, level_ready = sems("rates_ready rates_exp decay_ready D_ready level_ready")
        rhs_ready, delta_out = sems("rhs_ready delta_out")
        inverse = sem("inverse")
        keep_abs, keep_ln, keep_ready, stick_ready = sems("keep_abs keep_ln keep_ready stick_ready")
        row_max, probs_ready = sems("row_max probs_ready")
        y_hi, y_lo = sems("y_hi y_lo")
        mixed_ready, mixed_hi, mixed_lo = sems("mixed_ready mixed_hi mixed_lo")
        a_base, a_act, b_base, h_ready, h_hi, h_lo = sems("a_base a_act b_base h_ready h_hi h_lo")
        post_sq, tap_done, dve_mix = sems("post_sq tap_done dve_mix")
        ln_mean, ln_sq, ln_ready = sems("ln_mean ln_sq ln_ready")
        gated, gated_hi, gated_lo, pooled, pooled_hi, pooled_lo, proj_hi = sems(
            "gated gated_hi gated_lo pooled pooled_hi pooled_lo proj_hi")
        y2_ready, y2_hi, y2_lo = sems("y2_ready y2_hi y2_lo")
        p_hi, last_sq, out_ready = sems("p_hi last_sq out_ready")

        class Turn:

            def __init__(self, j, i=None, stride=0):
                self.j, self.i, self.stride = j, i, stride

            def count(self, f):
                first = f(self.j)
                return first if self.i is None else first + self.i * (f(self.j + self.stride) - first)

            def part(self, k, n):
                return Turn(n * self.j + k, self.i, n * self.stride)

        def repeat(eng, first, last, stride, step):
            groups, over = divmod(last - first, stride)
            for j in range(first, first + over):
                step(Turn(j))
            with eng.Fori(0, groups) as i:
                for j in range(first + over, first + over + stride):
                    step(Turn(j, i, stride))

        def wait(eng, semaphore, value):
            if not (isinstance(value, int) and value <= 0):
                eng.wait_ge(semaphore, value)

        def small(name):
            return SMP[:, SMALL_ORDER[name] % 4, :]

        def small_bank_free(pe, name):
            wait(pe, small_taken[SMALL_ORDER[name] % 4], SMALL_ORDER[name] // 4)

        def small_is_done(eng, name):
            if name in BY_BLOCK:
                eng.wait_ge(block_done, BY_BLOCK[name])
            else:
                eng.wait_ge(small_done, SMALL_COUNT[name])

        def small_is_taken(eng, name):
            eng.wait_ge(small_taken[SMALL_ORDER[name] % 4], SMALL_ORDER[name] // 4 + 1)

        def bank_of(name):
            return small_taken[SMALL_ORDER[name] % 4]

        def acc(phase, t, k=0):
            return ACCP[:, ACC_BANKS[phase, t.j][k], :]

        def acc_banks_free(pe, phase, t, *which):
            for b in [ACC_BANKS[phase, t.j][k] for k in which] or ACC_BANKS[phase, t.j]:
                wait(pe, acc_taken[b], t.count(lambda j: ACC_TURN[phase, j][b]))

        def acc_is_done(eng, phase, t):
            if t.j < F_OPEN.get(phase, 0):
                before = list(F_OPEN.values())[:list(F_OPEN).index(phase)]
                eng.wait_ge(opened, sum(before) + t.j + 1)
                return
            eng.wait_ge(block_done, t.count(lambda j: ACC_LAST[phase, j] + 1))

        def tile_is_done(eng, phase, m):
            if m == 0 and phase in TILED:
                eng.wait_ge(tile_done, list(TILED).index(phase) + 1)
            elif m == 0 and phase == "ple_g":
                eng.wait_ge(tile_done, len(TILED) + 1)
            elif phase == "ple_g":
                eng.wait_ge(block_done, N_BLOCKS)
            else:
                acc_is_done(eng, phase, Turn(0))

        def acc_bank(phase, t, k=0):
            return acc_taken[ACC_BANKS[phase, t.j][k]]

        def acc_is_taken(eng, phase, t, k=0):
            b = ACC_BANKS[phase, t.j][k]
            eng.wait_ge(acc_taken[b], t.count(lambda j: ACC_TURN[phase, j][b] + 1))

        def col(name, i=0):
            tile, row = COL_AT[name]
            return COL[tile][:, row + i:row + i + 1]

        def conv_tap(tap, tile, t):
            return FCONV[:, moved(tap * 2 * FT + tile, t, 2)]

        def conv_bias(tile, t):
            tile_, row = COL_AT["ffn_conv_b"]
            return COL[tile_][:, moved(row + tile, t, 2)]

        def moved(c, t, per_turn):
            return slice(c, c + 1) if t.i is None else bass.ds(c + t.i * (t.stride * per_turn), 1)

        def tiles_of(t):
            return slice(2 * t.j, 2 * t.j + 2) if t.i is None else bass.ds(2 * t.j + t.i * (2 * t.stride), 2)

        def lo_is_ready(eng, phase, t, ahead=0, half=1):
            n = FIRST[phase] + t.j + ahead
            eng.wait_ge(lo_ready[n % RING], t.count(lambda j: 2 * ((FIRST[phase] + j + ahead) // RING) + half + 1))
            return n % RING

        def half_of(half):
            return slice(half * HALF, (half + 1) * HALF)

        def tok(t):
            return slice(t * P, (t + 1) * P)

        def per_head(ap, n):
            return ap.unsqueeze(2).broadcast_to([P, ap.shape[1], n])

        def every(mask, n):
            return mask.unsqueeze(1).broadcast_to([P, n, mask.shape[1]])

        def by_head(ap, d=P):
            return ap.rearrange("p (h d) -> p h d", d=d)

        def flat(ap):
            return ap.rearrange("p a b -> p (a b)")

        block = ctx.enter_context(nc.Block())

        @block.sync
        def _(sp):
            def load(phase, t, source):
                n = FIRST[phase] + t.j
                slot, k = n % RAWS, source.shape[1] // 2
                for half in range(2):
                    if n >= RAWS:
                        lo_is_ready(sp, phase, t, -RAWS, half)
                    dst = RAW[:, slot, half, :].rearrange("p (k n) -> p k n", k=k)
                    sp.dma_start(dst, source[:, half * k:(half + 1) * k, :]).then_inc(raw_ready[slot][half], 16)

            def load_f(phase, m, c):
                for j in range(dict(PHASES)[phase]):
                    load(phase, Turn(j), f_block(m, c + 256 * j))

            def load_t(phase, m, c):
                for j in range(dict(PHASES)[phase]):
                    load(phase, Turn(j), t_block(m, c + 512 * (j // 2), j % 2))

            def load_d(phase, m):
                for j in range(dict(PHASES)[phase]):
                    load(phase, Turn(j), d_block(m, j))

            def load_pairs(phase, first, second):
                def step(t):
                    at_loop = 0 if t.i is None else t.i * (256 * t.stride)
                    for k, (m, c) in enumerate((first, second)):
                        load(phase, t.part(k, 2), f_block(m, at_loop + (c + 256 * t.j)))
                repeat(sp, 0, FT // 2, 2, step)

            def load_down(phase, m):
                def step(t):
                    load(phase, t, d_block(m, t.j if t.i is None else t.i * t.stride + t.j))
                repeat(sp, 0, FT // 2, 4, step)

            for t in range(NT):
                sp.dma_start(X[:, t, :], A["x"][0, tok(t), :]).then_inc(x_loaded[t], 16)
            sp.dma_start(PRE_GAIN[:, :], A["norm_mix"].broadcast_to([P, DM])).then_inc(pre_gain_loaded, 16)
            for j in range(RAWS):
                load("gdn", Turn(j), f_block(w["w_in"], C_GQKV + 256 * j))
            for tile, names in enumerate(COL_ROWS):
                row = 0
                for name, n in names:
                    a = A[name]
                    src = a.rearrange("a (r p) -> (a r) p", p=P) if len(a.shape) == 2 else a.rearrange("a t (r p) -> (a t r) p", p=P)
                    sp.dma_start(ROWS[tile][row:row + n, :], src).then_inc(rows_loaded, 16)
                    row += n
            taps = A["ffn_conv"].rearrange("a t (r p) -> (a t r) p", p=P)
            sp.dma_start(ROWS[2][:, :], taps[0:P, :]).then_inc(rows_loaded, 16)
            sp.dma_start(ROWS[1][COL_N[1]:COL_N[1] + CONV_TAIL, :], taps[P:CONV_N, :]).then_inc(rows_loaded, 16)
            tiny_rows = w["w_in"].rearrange("(k p) n -> p k n", p=P)
            sp.dma_start(TW[:, :, 0:4], tiny_rows[:, :, C_FF:C_FF + 4]).then_inc(tiny_w_loaded, 16)
            sp.dma_start(TW[:, :, 4:12], tiny_rows[:, :, C_GB:C_GB + 8]).then_inc(tiny_w_loaded, 16)
            for j in range(RAWS, 6):
                load("gdn", Turn(j), f_block(w["w_in"], C_GQKV + 256 * j))
            load_f("sbqk", w["w_in"], C_SQ)
            load_t("sbv", w["w_in"], C_SV)
            load_t("foxqk", w["w_in"], C_FQ)
            load_t("foxv", w["w_in"], C_FV)
            for g, branch, wo in (("c", 2, "w_oc"), ("a", 0, "w_oa"), ("b", 1, "w_ob")):
                if g == "b":
                    load_f("gz", w["w_in"], C_GZ)
                load_f(f"gate_{g}", w["w_in"], C_GATE + DM * branch)
                for j in range(2):
                    load(f"out_{g}", Turn(j), rows(w[wo], 0, 4, 512 * j, 512))
            load_d("w_out", w["w_out"])
            load_t("mem_k", w["w_mkv"], 0)
            load_t("mem_q", w["w_mq"], 0)
            load_t("mem_v", w["w_mkv"], HW)
            load_d("mem_o", w["w_mo"])
            load_pairs("up", (w["w_up"], 0), (w["w_up"], DFF))
            load_down("down", w["w_down"])
            load_pairs("ffn1", (w["ffn1_w_gate_2"], 0), (w["ffn1_w_up_2"], 0))
            load_down("down1", w["ffn1_w_down_2"])
            load_t("mix_v", w["w_in_2"], DM)
            load_f("mix_u", w["w_in_2"], 0)
            load_f("mix_c", w["w_in_2"], 2 * DM)
            load_f("mix_ga", w["w_in_2"], 3 * DM)
            load_f("mix_gb", w["w_in_2"], 4 * DM)
            load("pool", Turn(0), A["pool_w_2"][0].rearrange("g (k p) n -> p (g k) n", p=P))
            for j in range(8):
                load("mix_out", Turn(j), f_block(w[("w_out_a_2", "w_out_b_2")[j % 2]], 256 * (j // 2)))
            load_d("mix_o", w["w_o_2"])
            load_pairs("ffn2", (w["ffn2_w_gate_2"], 0), (w["ffn2_w_up_2"], 0))
            load_down("down2", w["ffn2_w_down_2"])
            load_d("ple_e", w["ple_w_proj_2"])
            load_t("ple_g", w["ple_w_gate_2"], 0)
            for t in range(NT):
                for half in range(2):
                    part = slice(half * 512, (half + 1) * 512)
                    sp.wait_ge(out_ready, 2 * t + half + 1)
                    sp.dma_start(out[0, tok(t), part], X[:, t, part]).then_inc(stored, 16)
            sp.wait_ge(stored, 16 * 2 * NT)

        @block.gpsimd
        def _(pool):
            steps = [0]

            def link(ins):
                steps[0] += 1
                ins.then_inc(pool_step, 1)
                pool.wait_ge(pool_step, steps[0])

            def where(dst, keep, pattern, start, per_partition, fill):
                return pool.affine_select(out=dst, in_=dst, compare_op=keep, fill=fill, base=start,
                                          pattern=pattern, channel_multiplier=per_partition)

            def masked(dst, keep, pattern, start, per_partition, fill, value=None):
                if value is not None:
                    link(pool.memset(dst, value))
                link(where(dst, keep, pattern, start, per_partition, fill))

            pool.memset(BROW, 0.0).then_inc(bias_zeroed, 1)
            pool.wait_ge(bias_zeroed, 1)
            pool.dma_start(BROW[:, 0:4], A["fox_fbias"].broadcast_to([P, HEADS])).then_inc(tiny_loaded, 16)
            pool.dma_start(BROW[:, 8:12], A["gdn_dt_bias"].broadcast_to([P, HEADS])).then_inc(tiny_loaded, 16)
            pool.dma_start(EA, A["gdn_a_log"].broadcast_to([P, HEADS])).then_inc(tiny_loaded, 16)
            link(pool.memset(IDENT[:, :], 0.0))
            where(IDENT[:, :], ALU.not_equal, [[-1, P]], 0, 1, 1.0).then_inc(masks_ready, 1)

            def inverse_root(name, mean_square):
                n = ROOTS[name]
                link(pool.tensor_scalar(mean_square, mean_square, EPS, None, ALU.add))
                pool.tensor_tensor(ROOT[name], mean_square, MINUS_HALF[:, 0:n], ALU.pow).then_inc(root_ready, 1)

            def heads_root(n, mult):
                pool.wait_ge(heads_sums, NT * (n + 1))
                if mult != 1.0:
                    link(pool.tensor_scalar(HSS[n], HSS[n], mult, None, ALU.mult))
                inverse_root(f"heads{n}", HSS[n])

            def norm_root(r, t):
                pool.wait_ge(sumsq, 2 * NORMS.index(r) + t + 1)
                inverse_root(f"{r}.{t}", SS[r][:, t:t + 1])

            def norm_roots(*names):
                for r in names:
                    for t in range(NT):
                        norm_root(r, t)

            def lo_half(n, half):
                s, c = n % RING, half_of(half)
                pool.wait_ge(hi_ready, 2 * n + half + 1)
                pool.tensor_tensor(LO[:, s, c], RAW[:, n % RAWS, half, :], HI[:, s, c].bitcast(f32), ALU.subtract).then_inc(lo_ready[s], 1)

            def post_norm_roots(phase, r):
                for t in range(NT):
                    pool.wait_ge(post_sq, NT * list(PSS).index(phase) + t + 1)
                    inverse_root(f"{phase}.{t}", PSS[phase][:, t:t + 1])
                    if t == 1:
                        n = FIRST[phase] + COUNT[phase] - 2 + RING
                        pool.wait_ge(lo_ready[n % RING], 2 * (n // RING) + 1)
                        lo_half(n, 1)
                    norm_root(r, t)

            link(pool.memset(MINUS_HALF, -0.5))
            norm_root("norm_mix", 0)
            link(pool.memset(SGN[:, 0:8], -1.0))
            link(pool.memset(SGN[:, 8:12], 1.0))
            link(pool.memset(ONES, 1.0))
            masked(TRI, ALU.is_ge, [[1, P]], 0, -1, 0.0, 1.0)
            masked(FROM[:, :], ALU.is_ge, [[-1, P]], 0, 1, 0.0, 1.0)
            masked(BEFORE[:, :], ALU.is_ge, [[1, P]], -1, -1, 0.0, 1.0)
            norm_root("norm_mix", 1)
            masked(BIG_NOT_BEFORE[:, :], ALU.is_gt, [[1, P]], 0, -1, BIG, 0.0)
            masked(NEG_AFTER[:, :], ALU.is_ge, [[-1, P]], 0, 1, -BIG, 0.0)
            d16 = DIAG16[:, :].rearrange("p (g c) -> p g c", c=16)
            masked(DIAG16[:, :], ALU.is_ge, [[-1, P]], -1, 1, 0.0, 1.0)
            masked(d16, ALU.is_ge, [[-16, P // 16], [0, 16]], 0, 1, 0.0)
            masked(d16, ALU.is_ge, [[16, P // 16], [0, 16]], 15, -1, 0.0)
            for b, m in LEVEL.items():
                link(pool.memset(m[:, :], 0.0))
                left = m[:, :].rearrange("p (g s c) -> p g s c", s=2, c=b)[:, :, 0, :]
                masked(left, ALU.is_ge, [[-2 * b, P // (2 * b)], [0, b]], -b, 1, 0.0, 1.0)
                masked(left, ALU.is_ge, [[2 * b, P // (2 * b)], [0, b]], 2 * b - 1, -1, 0.0)
            link(pool.memset(INV16[:, :, :], 1.0))
            for g, size in enumerate(POOL_WINDOWS):
                for t in range(size - 1):
                    link(pool.memset(INV16[:, g, t:t + 1], size / (t + 1)))
            pool.wait_ge(masks_ready, 1)
            pool.memset(KEEP[:, :], 1.0).then_inc(masks_ready, 1)

            heads_root(0, 1.0)
            for t in range(NT):
                small_is_taken(pool, f"kk{t}")
                pool.tensor_tensor(MA[:, t], DL[:, t], every(DIAG16[:, :], HEADS), ALU.mult).then_inc(D_ready, 1)
            heads_root(1, 1.0 / DH)
            for b, last in ((16, "D8"), (32, "Z16"), (64, "Z32")):
                for t in range(NT):
                    small_is_done(pool, f"{last}_{t}")
                    pool.tensor_tensor(MA[:, t], DL[:, t], every(LEVEL[b][:, :], HEADS), ALU.mult).then_inc(level_ready, 1)

            heads_root(2, 1.0 / DH)
            norm_roots("norm_mem", "norm_xq")
            for n in (3, 4):
                heads_root(n, 1.0 / DH)
            for n in sorted(ON_POOL):
                for half in range(2):
                    lo_half(n, half)
            norm_roots("norm_ffn", "norm_f1")
            post_norm_roots("down1", "norm_mix2")
            pool.wait_ge(ln_sq, NT)
            inverse_root("layer", LSS)

            for j in range(4):
                acc_is_taken(pool, "mix_c", Turn(j))
            small_is_taken(pool, "sguw")
            for dst, src, shift in ((S2A, C2[:, 0:2], 1), (S2B, C2[:, 2:8], 1), (S4, S2B[:, :], 2),
                                    (S8, S4[:, 2:6], 4), (S16, S8[:, 2:4], 8)):
                link(pool.tensor_copy(dst[:, :, 0:shift], src[:, :, 0:shift]))
                pool.tensor_tensor(dst[:, :, shift:SEQ], src[:, :, shift:SEQ], src[:, :, 0:SEQ - shift],
                                   ALU.add).then_inc(windows_ready, 1)
                pool.wait_ge(windows_ready, [S2A, S2B, S4, S8, S16].index(dst) + 1)
            post_norm_roots("mix_o", "norm_f2")
            post_norm_roots("down2", "norm_ple")
            for t in range(NT):
                pool.wait_ge(last_sq, NT + t + 1)
                mean_square = POST[:, 2 * t:2 * t + 1]
                link(pool.tensor_tensor(mean_square, mean_square, POST[:, 2 * t + 1:2 * t + 2], ALU.add))
                inverse_root(f"last.{t}", mean_square)

        @block.tensor
        def _(pe):
            def three(dst, lhs, rhs, start, stop):
                pe.matmul(dst, lhs[0], rhs[0], start=start, stop=False)
                pe.matmul(dst, lhs[0], rhs[1], start=False, stop=False)
                return pe.matmul(dst, lhs[1], rhs[0], start=False, stop=stop)

            def f_part(phase, t, xh, xl, tokens, ready=None):
                s = lo_is_ready(pe, phase, t)
                acc_banks_free(pe, phase, t)
                for half in range(2):
                    for k in range(KT):
                        if ready and half == 0:
                            ready(k)
                        c = slice(k * 256 + half * P, k * 256 + half * P + P)
                        dst = acc(phase, t)[:, half * SEQ:(half + 1) * SEQ]
                        last = three(dst[:, tokens], (HI[:, s, c], LO[:, s, c]), (xh[:, k, tokens], xl[:, k, tokens]),
                                     k == 0, k == KT - 1)
                return last

            def f_gemm(phase, t, xh, xl, ready=None):
                f_part(phase, t, xh, xl, slice(0, SEQ), ready).then_inc(block_done, 1)

            def t_part(phase, j, m, xh, xl, ready=None):
                chunk, half = Turn(j // 2), j % 2
                s = lo_is_ready(pe, phase, Turn(j))
                if half == 0:
                    acc_banks_free(pe, phase, chunk, m)
                for k in range(4):
                    kk = 4 * half + k
                    if ready:
                        ready(kk)
                    c = slice(k * 512, (k + 1) * 512)
                    last = three(acc(phase, chunk, m), (xh[:, kk, tok(m)], xl[:, kk, tok(m)]),
                                 (HI[:, s, c], LO[:, s, c]), kk == 0, kk == KT - 1)
                return last

            def t_half(phase, j, xh, xl, ready=None):
                for m in range(NT):
                    last = t_part(phase, j, m, xh, xl, ready and ready[m])
                last.then_inc(block_done, 1)

            def d_part(phase, j, m, xh, xl, ready=None):
                s = lo_is_ready(pe, phase, Turn(j))
                if j == 0:
                    acc_banks_free(pe, phase, Turn(0), 2 * m, 2 * m + 1)
                for k in range(2):
                    kk = 2 * j + k
                    if ready:
                        ready(kk)
                    for half in range(2):
                        c = slice(k * DM + half * 512, k * DM + half * 512 + 512)
                        last = three(acc(phase, Turn(0), 2 * m + half), (xh[:, kk, tok(m)], xl[:, kk, tok(m)]),
                                     (HI[:, s, c], LO[:, s, c]), kk == 0, kk == 2 * COUNT[phase] - 1)
                return last

            def d_gemm(phase, j, xh, xl, ready=None):
                for m in range(NT):
                    last = d_part(phase, j, m, xh, xl, ready)
                last.then_inc(block_done, 1)

            def d_tail(phase, r, xh, xl, ready):
                tail = range(COUNT[phase] - TILED[phase], COUNT[phase])
                for m in range(NT):
                    for j in tail:
                        if m == 1 and j == tail[-1] and len(tail) > 2:
                            norm_turn(r, XS, 0)
                        last = d_part(phase, j, m, xh, xl, ready)
                        if m == 1:
                            last.then_inc(block_done, 1)
                    if m == 0:
                        last.then_inc(tile_done, 1)
                if len(tail) <= 2:
                    norm_turn(r, XS, 0)

            def t_open(phase, r):
                for m in range(NT):
                    for j in range(T_OPEN[phase]):
                        if m == 0 and j == T_OPEN[phase] - 1:
                            norm_turn(r, XS, 1)
                        last = t_part(phase, j, m, XH, XL, norm_ready(r, m))
                        if m == 1:
                            last.then_inc(block_done, 1)

            def f_open(phase, r):
                n = F_OPEN[phase]
                for t in range(NT):
                    for j in range(n):
                        if t == 0 and j == n - 1:
                            norm_turn(r, XS, 1)
                        s = lo_is_ready(pe, phase, Turn(j))
                        name = f"{phase}.{t}{j // 2}"
                        if j % 2 == 0:
                            small_bank_free(pe, name)
                        for k in range(KT):
                            norm_ready(r, t)(k)
                            c = slice(k * 256, (k + 1) * 256)
                            last = three(small(name)[:, j % 2 * 256:j % 2 * 256 + 256], (XH[:, k, tok(t)], XL[:, k, tok(t)]),
                                         (HI[:, s, c], LO[:, s, c]), k == 0, k == KT - 1)
                        if t == 1:
                            last.then_inc(block_done, 1)
                        elif j % 2 == 1 or j == n - 1:
                            finish(last)
                for j in range(n):
                    acc_banks_free(pe, phase, Turn(j))
                    for t in range(NT):
                        small_is_taken(pe, f"{phase}.{t}{j // 2}")
                    for half in range(2):
                        for t in range(NT):
                            dst = acc(phase, Turn(j))[:, half * SEQ + t * P:half * SEQ + (t + 1) * P]
                            c = j * 256 + half * P
                            last = pe.transpose(dst, OPENED[:, t, c:c + P], IDENT[:, :])
                    last.then_inc(opened, 1)

            def o_gemm(phase, j, ready):
                s = lo_is_ready(pe, phase, Turn(j))
                acc_banks_free(pe, phase, Turn(j))
                ready()
                for n in range(4):
                    for k in range(HEADS):
                        c = slice(k * 512 + n * P, k * 512 + n * P + P)
                        last = three(acc(phase, Turn(j), n // 2)[:, n % 2 * 256:n % 2 * 256 + 256],
                                     (HI[:, s, c], LO[:, s, c]), (YH[:, k, :], YL[:, k, :]), k == 0, k == HEADS - 1)
                last.then_inc(block_done, 1)

            def finish(ins):
                ins.then_inc(small_done, 1)

            def four(name, product):
                small_bank_free(pe, name)
                for h in range(HEADS):
                    lhs, rhs = product(h)
                    last = pe.matmul(small(name)[:, h * P:(h + 1) * P], lhs, rhs, start=True, stop=True)
                finish(last)

            def turn_four(name, source):
                small_bank_free(pe, name)
                for h in range(4):
                    last = pe.transpose(small(name)[:, h * P:(h + 1) * P], source(h), IDENT[:, :])
                finish(last)

            def norm_turn(r, source, t):
                for b in range(2):
                    pe.wait_ge(scaled, 4 * NORMS.index(r) + 2 * t + b + 1)
                    turn_four(f"{r}.{t}{b}", lambda k: source[:, t, (4 * b + k) * P:(4 * b + k + 1) * P])

            def norm_ready(r, *tiles):
                def ready(k):
                    if k % 4 == 0:
                        for t in tiles:
                            small_is_taken(pe, f"{r}.{t}{k // 4}")
                return ready

            pe.wait_ge(masks_ready, 1)
            for t in range(NT):
                norm_turn("norm_mix", XS, t)
            for j in range(6):
                f_gemm("gdn", Turn(j), XH, XL, norm_ready("norm_mix", 0, 1) if j == 0 else None)
                if j == 0:
                    pe.wait_ge(rows_loaded, 16 * N_ROW_LOADS)
                    for i, n in enumerate((COL_N[0], COL_N[1] + CONV_TAIL, P)):
                        small_bank_free(pe, f"cols{i}")
                        finish(pe.transpose(small(f"cols{i}")[:, 0:n], ROWS[i][0:n, :], IDENT[0:n, 0:n]))
            small_bank_free(pe, "tiny")
            pe.wait_ge(tiny_lo, 1)
            for t in range(NT):
                for k in range(KT):
                    last = three(small("tiny")[:, 16 * t:16 * t + 12], (XH[:, k, tok(t)], XL[:, k, tok(t)]),
                                 (THI[:, k, :], TLO[:, k, :]), k == 0, k == KT - 1)
            finish(last)
            f_gemm("sbqk", Turn(0), XH, XL)
            pe.wait_ge(conv_done, 6)
            for i, part in enumerate("qk"):
                for t in range(NT):
                    turn_four(f"gT{part}{t}", lambda h: CONVF[:, 4 * i + h, tok(t)])
            f_gemm("sbqk", Turn(1), XH, XL)
            for t in range(NT):
                turn_four(f"gTv{t}", lambda h: CONVF[:, 8 + h, tok(t)])
            f_gemm("sbqk", Turn(2), XH, XL)
            pe.wait_ge(rates_ready, 1)
            pe.wait_ge(masks_ready, 2)
            small_bank_free(pe, "gcol")
            for t in range(NT):
                pe.matmul(small("gcol")[:, 4 * t:4 * t + 4], TRI, NG[:, t, :], start=True, stop=True)
            finish(pe.matmul(small("gcol")[:, 8:12], ONES, NG[:, 0, :], start=True, stop=True))
            for t in range(NT):
                four(f"grow{t}", lambda h: (NG[:, t, h:h + 1].broadcast_to([P, P]), TRI))
            f_gemm("sbqk", Turn(3), XH, XL)
            for i, part in enumerate("qk"):
                for t in range(NT):
                    pe.wait_ge(heads_ready, t + 1)
                    turn_four(f"gF{part}{t}", lambda h: GT[:, t, i, h * P:(h + 1) * P])
            t_half("sbv", 0, XH, XL)
            for t in range(NT):
                small_is_taken(pe, f"gFk{t}")
                four(f"kk{t}", lambda h: (QKF[:, 4 + h, tok(t)], QKF[:, 4 + h, tok(t)]))
            for t in range(NT):
                small_is_taken(pe, f"gFq{t}")
                four(f"kq{t}", lambda h: (QKF[:, 4 + h, tok(t)], QKF[:, h, tok(t)]))
            t_half("sbv", 1, XH, XL)
            for j in range(4):
                acc_is_taken(pe, "sbqk", Turn(j))
            for h in range(HEADS):
                small_bank_free(pe, f"z{h}")
                pe.matmul(small(f"z{h}")[:, 0:SEQ], SQK[:, 4 + h, tok(0)], SQK[:, h, :], start=True, stop=True)
                finish(pe.matmul(small(f"z{h}")[:, SEQ:SEQ + P], SQK[:, 4 + h, tok(1)], SQK[:, h, tok(1)], start=True, stop=True))
            for t in range(NT):
                pe.wait_ge(D_ready, t + 1)
                turn_four(f"Dt{t}", lambda h: MA[:, t, h, :])
            t_half("foxqk", 0, XH, XL)
            for t in range(NT):
                small_is_taken(pe, f"Dt{t}")
                four(f"D2_{t}", lambda h: (MB[:, t, h, :], MA[:, t, h, :]))
            for t in range(NT):
                four(f"D2t_{t}", lambda h: (MA[:, t, h, :], MB[:, t, h, :]))
            t_half("foxqk", 1, XH, XL)
            for t in range(NT):
                small_is_taken(pe, f"D2_{t}")
                four(f"P2_{t}", lambda h: (MC[:, t, h, :], MP[:, t, h, :]))
            for t in range(NT):
                small_is_taken(pe, f"D2t_{t}")
                four(f"D4_{t}", lambda h: (ME[:, t, h, :], MC[:, t, h, :]))
            t_half("foxqk", 2, XH, XL)
            for t in range(NT):
                four(f"D4t_{t}", lambda h: (MC[:, t, h, :], ME[:, t, h, :]))
            pe.wait_ge(keep_ready, 1)

            def rest_sums(h):
                name = f"rc{h}"
                small_bank_free(pe, name)
                bank = small(name)
                pe.matmul(bank[:, 0:SEQ], FROM[:, :], SP_[:, h, 0:SEQ], start=True, stop=False)
                pe.matmul(bank[:, P:SEQ], ONES, SP_[:, h, SEQ:SEQ + P], start=False, stop=False)
                pe.matmul(bank[:, 0:P], IDENT[:, :], BIG_NOT_BEFORE[:, :], start=False, stop=True)
                pe.matmul(bank[:, SEQ:SEQ + P], FROM[:, :], SP_[:, h, SEQ:SEQ + P], start=True, stop=False)
                finish(pe.matmul(bank[:, SEQ:SEQ + P], IDENT[:, :], BIG_NOT_BEFORE[:, :], start=False, stop=True))

            for h in range(2):
                rest_sums(h)
            t_half("foxqk", 3, XH, XL)
            for h in range(2, 4):
                rest_sums(h)
            for t in range(NT):
                small_is_taken(pe, f"P2_{t}")
                small_is_taken(pe, f"D4_{t}")
                four(f"P4_{t}", lambda h: (MA[:, t, h, :], MP[:, t, h, :]))
            t_half("foxv", 0, XH, XL)
            for t in range(NT):
                small_is_taken(pe, f"D4t_{t}")
                four(f"D8_{t}", lambda h: (MB[:, t, h, :], MA[:, t, h, :]))
            t_half("foxv", 1, XH, XL)
            for t in range(NT):
                small_is_taken(pe, f"D8_{t}")
                small_is_taken(pe, f"P4_{t}")
                four(f"P8_{t}", lambda h: (MC[:, t, h, :], MP[:, t, h, :]))
            pe.wait_ge(stick_ready, 1)
            for m in range(NT):
                acc_is_taken(pe, "sbv", Turn(0), m)
            for g in range(2):
                name = f"so{g}"
                small_bank_free(pe, name)
                for h in (2 * g, 2 * g + 1):
                    dst = small(name)[:, h % 2 * SEQ:h % 2 * SEQ + SEQ]
                    pe.matmul(dst, SV[:, 0, h * P:(h + 1) * P], Z[:, h, 0:SEQ], start=True, stop=False)
                    last = pe.matmul(dst[:, P:SEQ], SV[:, 1, h * P:(h + 1) * P], Z[:, h, SEQ:SEQ + P], start=False, stop=True)
                finish(last)
            f_gemm("gate_c", Turn(0), XH, XL)
            for t in range(NT):
                small_is_taken(pe, f"P8_{t}")
                turn_four(f"T16_{t}", lambda h: MP[:, t, h, :])
            f_gemm("gate_c", Turn(1), XH, XL)
            for i, part in enumerate("qk"):
                for t in range(NT):
                    pe.wait_ge(heads_ready, 2 + t + 1)
                    turn_four(f"fT{part}{t}", lambda h: HT[:, t, i * HW + h * P:i * HW + (h + 1) * P])

            def join(b, n):
                for t in range(NT):
                    pe.wait_ge(level_ready, 2 * n + t + 1)
                    four(f"Z{b}_{t}", lambda h: (MA[:, t, h, :], MP[:, t, h, :]))

            def joined(b, both=True):
                for t in range(NT):
                    small_is_taken(pe, f"Z{b}_{t}")
                    if b == 16:
                        small_is_taken(pe, f"T16_{t}")
                    else:
                        small_is_taken(pe, f"T{b}_{t}")
                    four(f"Tt{2 * b}_{t}", lambda h: (ME[:, t, h, :], MB[:, t, h, :]))
                for t in range(NT if both else 0):
                    four(f"T{2 * b}_{t}", lambda h: (MB[:, t, h, :], ME[:, t, h, :]))

            f_gemm("gate_c", Turn(2), XH, XL)
            join(16, 0)
            f_gemm("gate_c", Turn(3), XH, XL)
            joined(16)

            def y_is_ready(*names):
                def ready():
                    for n in names:
                        small_is_taken(pe, n)
                return ready

            o_gemm("out_c", 0, y_is_ready("so0", "so1"))
            for part in "qk":
                for t in range(NT):
                    small_is_taken(pe, f"fT{part}{t}")

            def fox_scores(name, t, heads):
                small_bank_free(pe, name)
                for i, h in enumerate(heads):
                    n = (t + 1) * P
                    dst = small(name)[:, i * n:(i + 1) * n]
                    pe.matmul(dst, FQK[:, h, tok(t)], FQK[:, 4 + h, 0:n], start=True, stop=False)
                    pe.matmul(dst, TS[:, 0, h:h + 1].broadcast_to([P, P]), flat(UPTO[:, 0:t + 1, :]), start=False, stop=False)
                    if t == 1:
                        pe.matmul(dst[:, P:SEQ], TS[:, 1, h:h + 1].broadcast_to([P, P]), TRI, start=False, stop=False)
                    last = pe.matmul(dst[:, t * P:n], IDENT[:, :], NEG_AFTER[:, :], start=False, stop=True)
                finish(last)

            fox_scores("fS0", 0, range(4))
            fox_scores("fS1a", 1, (0, 1))
            fox_scores("fS1b", 1, (2, 3))
            o_gemm("out_c", 1, y_is_ready())
            for t in range(NT):
                small_is_taken(pe, f"Tt32_{t}")
            join(32, 1)
            f_gemm("gate_a", Turn(0), XH, XL)
            joined(32)
            f_gemm("gate_a", Turn(1), XH, XL)
            pe.wait_ge(probs_ready, 1)
            turn_four("fP0", lambda h: FP0[:, h, :])
            pe.wait_ge(probs_ready, 2)
            for i, part in enumerate("ab"):
                turn_four(f"fP1{part}", lambda h: FP1[:, h, tok(i)])
            f_gemm("gate_a", Turn(2), XH, XL)
            for m in range(NT):
                acc_is_taken(pe, "foxv", Turn(0), m)
            small_is_taken(pe, "fP0")
            four("fo0", lambda h: (FV[:, 0, h * P:(h + 1) * P], FPT0[:, h, :]))
            small_is_taken(pe, "fP1a")
            small_is_taken(pe, "fP1b")
            small_bank_free(pe, "fo1")
            for h in range(HEADS):
                for k in range(2):
                    last = pe.matmul(small("fo1")[:, h * P:(h + 1) * P], FV[:, k, h * P:(h + 1) * P], FPT1[:, k, h, :],
                                     start=k == 0, stop=k == 1)
            finish(last)
            for t in range(NT):
                small_is_taken(pe, f"Tt64_{t}")
            join(64, 2)
            f_gemm("gate_a", Turn(3), XH, XL)
            joined(64, both=False)
            o_gemm("out_a", 0, y_is_ready("fo0", "fo1"))
            small_is_taken(pe, "Tt128_0")
            pe.wait_ge(rhs_ready, 2)
            four("vn0", lambda h: (MP[:, 0, h, :], GT[:, 0, 0, h * P:(h + 1) * P]))
            o_gemm("out_a", 1, y_is_ready())
            small_is_taken(pe, "vn0")
            four("S1", lambda h: (GT[:, 0, 1, h * P:(h + 1) * P], GT[:, 1, 0, h * P:(h + 1) * P]))
            f_gemm("gz", Turn(0), XH, XL)
            small_is_taken(pe, "S1")
            four("kS", lambda h: (QKF[:, 4 + h, tok(1)], MA[:, 0, h, :]))
            four("qS", lambda h: (QKF[:, h, tok(1)], MA[:, 0, h, :]))
            f_gemm("gz", Turn(1), XH, XL)
            small_is_taken(pe, "Tt128_1")
            pe.wait_ge(rhs_ready, 3)
            four("vn1", lambda h: (MP[:, 1, h, :], GT[:, 1, 2, h * P:(h + 1) * P]))
            f_gemm("gate_b", Turn(0), XH, XL)
            small_is_taken(pe, "kq0")
            four("o0", lambda h: (MAT[:, 0, h, :], GT[:, 1, 0, h * P:(h + 1) * P]))
            small_is_taken(pe, "kq1")
            small_is_taken(pe, "vn1")
            four("o1", lambda h: (MAT[:, 1, h, :], MA[:, 1, h, :]))
            f_gemm("gate_b", Turn(1), XH, XL)
            f_gemm("gate_b", Turn(2), XH, XL)
            for t in range(NT):
                pe.wait_ge(heads_ready, 4 + t + 1)
                turn_four(f"yT{t}", lambda h: DO[:, t, h * P:(h + 1) * P])
            f_gemm("gate_b", Turn(3), XH, XL)

            def delta_ready():
                pe.wait_ge(y_lo, 2)

            o_gemm("out_b", 0, delta_ready)
            for t in range(NT):
                norm_turn("norm_mem", MEM, t)
            o_gemm("out_b", 1, delta_ready)

            def mixed_is_ready(k):
                pe.wait_ge(mixed_lo, k // 2 + 1)

            d_gemm("w_out", 0, XH, XL, mixed_is_ready)
            d_tail("w_out", "norm_xq", XH, XL, mixed_is_ready)
            for j in range(2):
                if j == 1:
                    norm_turn("norm_xq", XS, 1)
                t_half("mem_k", j, MH, MLO, [norm_ready("norm_mem", m) for m in range(NT)])
            t_half("mem_q", 0, XH, XL, [norm_ready("norm_xq", m) for m in range(NT)])
            t_half("mem_q", 1, XH, XL)
            for t in range(NT):
                pe.wait_ge(heads_ready, 6 + t + 1)
                turn_four(f"mkT{t}", lambda h: MK[:, t, h * P:(h + 1) * P])
            t_half("mem_v", 0, MH, MLO)
            for t in range(NT):
                pe.wait_ge(heads_ready, 8 + t + 1)
                turn_four(f"mqT{t}", lambda h: MQ[:, t, h * P:(h + 1) * P])
            for t in range(NT):
                small_is_taken(pe, f"mkT{t}")
            for t in range(NT):
                small_is_taken(pe, f"mqT{t}")
                for part, heads in (("a", (0, 1)), ("b", (2, 3))):
                    name = f"mS{t}{part}"
                    small_bank_free(pe, name)
                    for i, h in enumerate(heads):
                        last = pe.matmul(small(name)[:, i * SEQ:(i + 1) * SEQ], MQT[:, h, tok(t)], MKT[:, h, :], start=True, stop=True)
                    finish(last)
            t_half("mem_v", 1, MH, MLO)
            for t in range(NT):
                pe.wait_ge(probs_ready, 2 + 2 * t + 2)
                for i, part in enumerate("ab"):
                    turn_four(f"mP{t}{part}", lambda h: MPR[:, t, h, tok(i)])
            for m in range(NT):
                acc_is_taken(pe, "mem_v", Turn(0), m)
            for name in ("mP0a", "mP0b", "mP1a", "mP1b"):
                small_is_taken(pe, name)
            for g in range(2):
                name = f"mo{g}"
                small_bank_free(pe, name)
                for h in (2 * g, 2 * g + 1):
                    for k in range(2):
                        last = pe.matmul(small(name)[:, h % 2 * SEQ:h % 2 * SEQ + SEQ], MV[:, k, h * P:(h + 1) * P],
                                         MPT[:, k, h, :], start=k == 0, stop=k == 1)
                finish(last)
            d_tail("mem_o", "norm_ffn", YH, YL, lambda k: small_is_taken(pe, f"mo{k // 2}"))

            def ffn(r, up, down, behind, before):
                def step(t):
                    for k in range(2):
                        f_gemm(up, t.part(k, 2), XH, XL)

                def hidden_ready(k):
                    pe.wait_ge(h_lo, before * (FT // 2) + k // 2 + 1)

                f_open(up, r)
                for j in range(F_OPEN[up], 4):
                    f_gemm(up, Turn(j), XH, XL)
                repeat(pe, 2, FT // 2, 2, step)
                if down == "down2":
                    turn_p()
                for m in range(NT):
                    for j in range(2):
                        last = d_part(down, j, m, HH, HL, hidden_ready)
                        if m == 1:
                            last.then_inc(block_done, 1)
                for j in range(2, COUNT[down] - TILED[down]):
                    d_gemm(down, j, HH, HL, hidden_ready)
                d_tail(down, behind, HH, HL, hidden_ready)

            def turn_p():
                small_bank_free(pe, "pT")
                pe.wait_ge(p_loaded, 16)
                for k in range(2):
                    for t in range(NT):
                        last = pe.transpose(small("pT")[:, k * SEQ + t * P:k * SEQ + (t + 1) * P], PR[:, t, k * P:(k + 1) * P], IDENT[:, :])
                finish(last)

            ffn("norm_ffn", "up", "down", "norm_f1", 0)
            ffn("norm_f1", "ffn1", "down1", "norm_mix2", 1)

            t_open("mix_v", "norm_mix2")
            small_bank_free(pe, "sguw")
            pe.wait_ge(sgu_loaded, 32)
            for g in range(4):
                last = pe.transpose(small("sguw")[:, g * P:(g + 1) * P], SGUW[:, g, :], IDENT[:, :])
            finish(last)
            for j in range(4):
                f_gemm("mix_u", Turn(j), XH, XL)
            f_gemm("mix_c", Turn(0), XH, XL)
            pe.wait_ge(ln_ready, 2)
            small_is_taken(pe, "sguw")
            for g in range(4):
                name = f"sgu{g}"
                small_bank_free(pe, name)
                for i in range(2):
                    for t in range(NT):
                        d = 2 * g + i
                        last = pe.matmul(small(name)[:, i * SEQ + t * P:i * SEQ + (t + 1) * P], V2[:, t, d * P:(d + 1) * P],
                                         WST[:, g, :], start=True, stop=True)
                finish(last)
            for j in range(1, 4):
                f_gemm("mix_c", Turn(j), XH, XL)
            for j in range(4):
                f_gemm("mix_ga", Turn(j), XH, XL)
            for j in range(4):
                f_gemm("mix_gb", Turn(j), XH, XL)
            s = lo_is_ready(pe, "pool", Turn(0))
            for g in range(4):
                acc_banks_free(pe, "pool", Turn(g))
                pe.wait_ge(pooled_lo, g + 1)
                for n in range(2):
                    for k in range(2):
                        c = slice((2 * g + k) * 256 + n * P, (2 * g + k) * 256 + n * P + P)
                        last = three(acc("pool", Turn(g))[:, n * 256:(n + 1) * 256], (HI[:, s, c], LO[:, s, c]),
                                     (HH[:, 8 + 2 * g + k, :], HL[:, 8 + 2 * g + k, :]), k == 0, k == 1)
            last.then_inc(block_done, 1)
            pe.wait_ge(gated_lo, 4)

            def projected(k):
                acc_is_taken(pe, "pool", Turn(k // 2))

            for j in range(8):
                k0 = 8 * (j % 2)
                f_gemm("mix_out", Turn(j), HH[:, k0:k0 + 8, :], HL[:, k0:k0 + 8, :], projected if j == 1 else None)

            def y2_is_ready(k):
                pe.wait_ge(y2_lo, k // 2 + 1)

            d_tail("mix_o", "norm_f2", XH, XL, y2_is_ready)

            ffn("norm_f2", "ffn2", "down2", "norm_ple", 2)
            small_is_taken(pe, "pT")

            def project(m):
                s = lo_is_ready(pe, "ple_e", Turn(0))
                for half in range(2):
                    name = f"ple.{m}{'ab'[half]}"
                    small_bank_free(pe, name)
                    for k in range(2):
                        c = slice(k * DM + half * 512, k * DM + half * 512 + 512)
                        last = three(small(name), (PH[:, k, tok(m)], PL[:, k, tok(m)]), (HI[:, s, c], LO[:, s, c]), k == 0, k == 1)
                    if name in BY_BLOCK:
                        last.then_inc(block_done, 1)
                    else:
                        finish(last)

            for m in range(NT):
                project(m)
            t_open("ple_g", "norm_ple")
            for m in range(NT):
                t_part("ple_g", 3, m, XH, XL).then_inc(block_done if m == 1 else tile_done, 1)

        @block.scalar
        def _(act):
            steps = [0]

            def link(ins):
                steps[0] += 1
                ins.then_inc(act_step, 1)
                act.wait_ge(act_step, steps[0])

            def split(n):
                for half in range(2):
                    act.wait_ge(raw_ready[n % RAWS][half], 16 * (n // RAWS + 1))
                    act.activation(HI[:, n % RING, half_of(half)], RAW[:, n % RAWS, half, :], ACT.Copy).then_inc(hi_ready, 1)

            def split_ahead(phase, t, halves=range(2)):
                n = FIRST[phase] + t.j + RING
                if n >= N_BLOCKS:
                    return
                act.wait_ge(block_done, t.count(lambda j: FIRST[phase] + j + 1))
                for half in halves:
                    act.wait_ge(raw_ready[n % RAWS][half], t.count(lambda j: 16 * ((FIRST[phase] + j + RING) // RAWS + 1)))
                    act.activation(HI[:, n % RING, half_of(half)], RAW[:, n % RAWS, half, :], ACT.Copy).then_inc(hi_ready, 1)

            def split_behind(phase, t):
                if t.i is not None or t.j >= 2:
                    split_ahead(phase, t)

            def copy(dst, src, signal, scale=1.0):
                act.activation(dst, src, ACT.Copy, scale=scale).then_inc(signal, 1)

            def take_small(name, dst, src, scale=1.0):
                small_is_done(act, name)
                copy(dst, src, bank_of(name), scale)

            def norm_square(r, t, src, junk):
                act.activation(junk[:, t, :], src[:, t, :], ACT.Square, scale=DM ** -0.5, accum_out=SS[r][:, t:t + 1]).then_inc(sumsq, 1)

            def norm_split(r, t, hi):
                for b in range(2):
                    name = f"{r}.{t}{b}"
                    small_is_done(act, name)
                    copy(hi[:, 4 * b:4 * b + 4, tok(t)], by_head(small(name)), norm_hi)

            def pre_gain_load(name):
                act.dma_start(PRE_GAIN[:, :], A[name].broadcast_to([P, DM])).then_inc(pre_gain_loaded, 16)

            def post_gain_load(name):
                act.dma_start(POST_GAIN[:, :], A[name].broadcast_to([P, DM])).then_inc(post_gain_loaded, 16)

            def gates(phase, j, name, branch):
                acc_is_done(act, phase, Turn(j))
                for i in range(2):
                    ins = act.activation(G[:, 2 * j + i, :], acc(phase, Turn(j))[:, i * 256:(i + 1) * 256], ACT.Sigmoid,
                                         bias=col("gate_bias", 8 * branch + 2 * j + i))
                ins.then_inc(acc_bank(phase, Turn(j)), 1)

            def softmax_exp(name, rows_, scores, first):
                for i in range(scores.shape[1]):
                    ins = act.activation(rows_[:, i, :], scores[:, i, :], ACT.Exp, bias=MX[:, first + i:first + i + 1],
                                         accum_out=RSUM[:, first + i:first + i + 1])
                ins.then_inc(bank_of(name), 1)

            for t in range(NT):
                act.wait_ge(x_loaded[t], 16)
                norm_square("norm_mix", t, X, XS)
            norm_split("norm_mix", 0, XH)
            split(0)
            norm_split("norm_mix", 1, XH)
            for n in range(1, RING):
                split(n)
            act.wait_ge(tiny_w_loaded, 16 * 2)
            copy(THI[:, :, :], TW[:, :, :], tiny_hi)

            def conv_silu(j):
                acc_is_taken(act, "gdn", Turn(j))
                act.activation(CONVF[:, 2 * j:2 * j + 2, :], CONVF[:, 2 * j:2 * j + 2, :], ACT.Silu).then_inc(conv_done, 1)

            for j in range(6):
                if j:
                    conv_silu(j - 1)
                acc_is_done(act, "gdn", Turn(j))
                for i in range(2):
                    for cols in range(3):
                        small_is_taken(act, f"cols{cols}")
                    copy(CONVF[:, 2 * j + i, :], acc("gdn", Turn(j))[:, i * 256:(i + 1) * 256], conv_base,
                         col("gdn_conv", 3 * 12 + 2 * j + i))
                split_ahead("gdn", Turn(j))
            conv_silu(5)

            def take_f(phase, j, dst, scale):
                acc_is_done(act, phase, Turn(j))
                copy(dst, acc(phase, Turn(j)).rearrange("p (n s) -> p n s", s=SEQ), acc_bank(phase, Turn(j)), scale)

            def take_t(phase, chunk, dst):
                acc_is_done(act, phase, Turn(chunk))
                for m in range(NT):
                    copy(dst[:, m], acc(phase, Turn(chunk), m), acc_bank(phase, Turn(chunk), m))

            take_f("sbqk", 0, SQK[:, 0:2, :], DH ** -0.5)
            split_ahead("sbqk", Turn(0))
            act.wait_ge(tiny_abs, 1)
            link(act.activation(TE, TE, ACT.Exp, scale=-1.0))
            act.activation(TE, TE, ACT.Ln, bias=1.0).then_inc(tiny_ln, 1)
            take_small("gTq0", GT[:, 0, 0, :], small("gTq0"))
            take_small("gTk0", GT[:, 0, 1, :], small("gTk0"))
            take_f("sbqk", 1, SQK[:, 2:4, :], DH ** -0.5)
            split_ahead("sbqk", Turn(1))
            act.wait_ge(tiny_sp, 1)
            act.activation(BETA, TS[:, :, 4:8], ACT.Exp, scale=-1.0)
            act.wait_ge(tiny_loaded, 16 * 3)
            act.activation(EA, EA, ACT.Exp).then_inc(tiny_exp, 1)
            for t in range(NT):
                for part in "qk":
                    small_is_taken(act, f"gT{part}{t}")
                act.activation(GSQ[:, t, :], flat(GT[:, t, 0:2, :]), ACT.Square).then_inc(heads_sq, 1)
            take_small("gTv0", GT[:, 0, 2, :], small("gTv0"))
            take_f("sbqk", 2, SQK[:, 4:6, :], 1.0)
            split_ahead("sbqk", Turn(2))
            small_is_taken(act, "gcol")
            act.activation(EGC, NC, ACT.Exp, scale=-1.0)
            act.activation(KD, KD, ACT.Exp).then_inc(rates_exp, 1)
            for t in range(NT):
                small_is_taken(act, f"grow{t}")
                act.activation(MA[:, t], MA[:, t], ACT.Exp).then_inc(decay_ready, 1)
                act.activation(MB[:, t], MB[:, t], ACT.Exp, scale=-1.0).then_inc(decay_ready, 1)
            take_f("sbqk", 3, SQK[:, 6:8, :], 1.0)
            split_ahead("sbqk", Turn(3))
            take_small("gFq0", QKF[:, 0:4, tok(0)], by_head(small("gFq0")))
            take_small("gFk0", QKF[:, 4:8, tok(0)], by_head(small("gFk0")))
            split_ahead("sbv", Turn(0))
            take_t("sbv", 0, SV)
            split_ahead("sbv", Turn(1))
            for h in range(HEADS):
                take_small(f"z{h}", Z[:, h, :], small(f"z{h}")[:, 0:384])
            split_ahead("foxqk", Turn(0))
            act.wait_ge(keep_abs, 1)
            link(act.activation(SP_[:, :, :], SP_[:, :, :], ACT.Exp, scale=-1.0))
            act.activation(SP_[:, :, :], SP_[:, :, :], ACT.Ln, bias=1.0).then_inc(keep_ln, 1)
            take_small("D2_0", MC[:, 0], by_head(small("D2_0")))
            take_small("D2t_0", ME[:, 0], by_head(small("D2t_0")))
            take_t("foxqk", 0, HT[:, :, 0:HW])
            split_ahead("foxqk", Turn(1))
            take_small("D4_0", MA[:, 0], by_head(small("D4_0")))
            split_ahead("foxqk", Turn(2))
            take_small("D4t_0", MB[:, 0], by_head(small("D4t_0")))
            take_t("foxqk", 1, HT[:, :, HW:2 * HW])
            split_ahead("foxqk", Turn(3))
            for t in range(NT):
                for c in range(2):
                    acc_is_taken(act, "foxqk", Turn(c), t)
                act.activation(XS[:, t, :], HT[:, t, :], ACT.Square).then_inc(heads_sq, 1)
            split_ahead("foxv", Turn(0))
            for h in range(HEADS):
                small_is_taken(act, f"rc{h}")
            act.activation(Z[:, :, :], Z[:, :, :], ACT.Exp).then_inc(stick_ready, 1)
            take_small("D8_0", MC[:, 0], by_head(small("D8_0")))
            take_t("foxv", 0, FV)
            split_ahead("foxv", Turn(1))
            for g in range(2):
                small_is_done(act, f"so{g}")
                copy(YH[:, 2 * g:2 * g + 2, :], by_head(small(f"so{g}"), SEQ), y_hi)
            act.wait_ge(heads_ready, 4)
            gates("gate_c", 0, G, 2)
            split_ahead("gate_c", Turn(0))
            take_small("T16_0", ME[:, 0], by_head(small("T16_0")))
            gates("gate_c", 1, G, 2)
            split_ahead("gate_c", Turn(1))
            take_small("fTq0", FQK[:, 0:4, tok(0)], by_head(small("fTq0")), col("fox_qnorm"))
            take_small("fTk0", FQK[:, 4:8, tok(0)], by_head(small("fTk0")), col("fox_knorm"))
            gates("gate_c", 2, G, 2)
            split_ahead("gate_c", Turn(2))
            take_small("Z16_0", MB[:, 0], by_head(small("Z16_0")))
            gates("gate_c", 3, G, 2)
            split_ahead("gate_c", Turn(3))
            split_ahead("out_c", Turn(0))
            act.wait_ge(row_max, 1)
            softmax_exp("fS0", FP0, by_head(small("fS0")), 0)
            act.wait_ge(row_max, 3)
            softmax_exp("fS1a", FP1[:, 0:2, :], by_head(small("fS1a"), SEQ), 4)
            softmax_exp("fS1b", FP1[:, 2:4, :], by_head(small("fS1b"), SEQ), 6)
            split_ahead("out_c", Turn(1))
            take_small("Z32_0", MB[:, 0], by_head(small("Z32_0")))
            for k in range(2):
                acc_is_taken(act, "out_c", Turn(1), k)
            gates("gate_a", 0, G, 0)
            split_ahead("gate_a", Turn(0))
            gates("gate_a", 1, G, 0)
            split_ahead("gate_a", Turn(1))
            take_small("fP0", FPT0[:, :, :], by_head(small("fP0")))
            take_small("fP1a", FPT1[:, 0], by_head(small("fP1a")))
            gates("gate_a", 2, G, 0)
            split_ahead("gate_a", Turn(2))
            for t in range(NT):
                small_is_done(act, f"fo{t}")
                copy(YH[:, :, tok(t)], by_head(small(f"fo{t}")), y_hi)
            take_small("Z64_0", MB[:, 0], by_head(small("Z64_0")))
            gates("gate_a", 3, G, 0)
            split_ahead("gate_a", Turn(3))
            split_ahead("out_a", Turn(0))
            take_small("vn0", GT[:, 1, 0, :], small("vn0"))
            split_ahead("out_a", Turn(1))
            take_small("S1", MA[:, 0], by_head(small("S1")))

            def gz_silu(j):
                acc_is_done(act, "gz", Turn(j))
                act.activation(GZS[:, 2 * j:2 * j + 2, :], acc("gz", Turn(j)).rearrange("p (n s) -> p n s", s=SEQ),
                               ACT.Silu).then_inc(acc_bank("gz", Turn(j)), 1)

            gz_silu(0)
            split_ahead("gz", Turn(0))
            gz_silu(1)
            split_ahead("gz", Turn(1))
            take_small("vn1", MA[:, 1], by_head(small("vn1")))
            for k in range(2):
                acc_is_taken(act, "out_a", Turn(1), k)
            gates("gate_b", 0, G, 1)
            split_ahead("gate_b", Turn(0))
            take_small("o0", DO[:, 0, :], small("o0"))
            for t in range(NT):
                small_is_taken(act, f"o{t}")
                act.activation(OSQ[:, t, :], DO[:, t, :], ACT.Square).then_inc(heads_sq, 1)
            pre_gain_load("norm_mem")
            act.dma_start(MEM[:, :, :], A["mem"][0].rearrange("(t p) d -> p t d", p=P)).then_inc(mem_loaded, 16)
            for j in range(1, 4):
                gates("gate_b", j, G, 1)
                split_ahead("gate_b", Turn(j))
                if j == 2:
                    for t in range(NT):
                        small_is_taken(act, f"yT{t}")
                        copy(YH[:, :, tok(t)], YB[:, :, tok(t)], y_hi)
            act.wait_ge(mem_loaded, 16)
            for t in range(NT):
                norm_square("norm_mem", t, MEM, MJUNK)
            for j in range(2):
                for k in range(2):
                    act.wait_ge(mixed_ready, 2 * j + k + 1)
                    copy(XH[:, 4 * j + 2 * k:4 * j + 2 * k + 2, :], MIX[:, 4 * j + 2 * k:4 * j + 2 * k + 2, :], mixed_hi)
                split_ahead("out_b", Turn(j))
                if j == 0:
                    for t in range(NT):
                        norm_split("norm_mem", t, MH)
                    pre_gain_load("norm_xq")
            act.wait_ge(mixed_lo, 4)
            act.dma_start(X[:, :, :], A["x"][0].rearrange("(t p) d -> p t d", p=P)).then_inc(x_again, 16)

            def new_square(phase, r, m):
                acc_is_taken(act, phase, Turn(0), 2 * m)
                acc_is_taken(act, phase, Turn(0), 2 * m + 1)
                norm_square(r, m, X, XS)

            def post_square(phase, m):
                tile_is_done(act, phase, m)
                act.activation(XS[:, m, :], flat(ACCP[:, 2 * m:2 * m + 2, :]), ACT.Square, scale=DM ** -0.5,
                               accum_out=PSS[phase][:, m:m + 1]).then_inc(post_sq, 1)

            def take_opened(phase, t):
                n = F_OPEN.get(phase, 0)
                for b in range((n + 1) // 2):
                    name, width = f"{phase}.{t}{b}", min(2, n - 2 * b) * 256
                    if t == 1 and b < 2:
                        split_ahead(phase, Turn(b))
                    if (t, b) != (1, 1):
                        take_small(name, OPENED[:, t, b * 512:b * 512 + width], small(name)[:, 0:width])

            def norm_behind(phase, r, behind):
                n = COUNT[phase]
                if n >= RING:
                    split_ahead(phase, Turn(n - 4))
                new_square(phase, r, 0)
                if n >= RING:
                    split_ahead(phase, Turn(n - 3))
                norm_split(r, 0, XH)
                split_ahead(phase, Turn(n - 2))
                new_square(phase, r, 1)
                norm_split(r, 1, XH)
                take_opened(behind, 0)
                split_ahead(phase, Turn(n - 1))
                take_opened(behind, 1)

            def post_norm_behind(phase, r, behind, between=None):
                n = COUNT[phase]
                post_square(phase, 0)
                split_ahead(phase, Turn(n - 4))
                new_square(phase, r, 0)
                split_ahead(phase, Turn(n - 3))
                norm_split(r, 0, XH)
                split_ahead(phase, Turn(n - 2), (0,))
                post_square(phase, 1)
                split_ahead(phase, Turn(n - 2), (1,))
                if between:
                    between(0)
                split_ahead(phase, Turn(n - 1), (0,))
                new_square(phase, r, 1)
                split_ahead(phase, Turn(n - 1), (1,))
                if between:
                    between(1)
                norm_split(r, 1, XH)
                take_opened(behind, 0)
                take_opened(behind, 1)

            norm_behind("w_out", "norm_xq", "mem_k")
            pre_gain_load("norm_ffn")
            take_t("mem_k", 0, MK)
            for t in range(NT):
                acc_is_taken(act, "mem_k", Turn(0), t)
                act.activation(MSQ[:, t, :], MK[:, t, :], ACT.Square).then_inc(heads_sq, 1)
            split_ahead("mem_k", Turn(0))
            split_ahead("mem_k", Turn(1))
            take_t("mem_q", 0, MQ)
            act.wait_ge(heads_ready, 8)
            for t in range(NT):
                acc_is_taken(act, "mem_q", Turn(0), t)
                act.activation(MSQ[:, t, :], MQ[:, t, :], ACT.Square).then_inc(heads_sq, 1)
            take_small("mkT0", MKT[:, :, tok(0)], by_head(small("mkT0")), col("mk_norm"))
            take_small("mqT0", MQT[:, :, tok(0)], by_head(small("mqT0")), col("mq_norm"))
            split_ahead("mem_q", Turn(0))
            for t in range(NT):
                for i, part in enumerate("ab"):
                    act.wait_ge(row_max, 3 + 2 * t + i + 1)
                    softmax_exp(f"mS{t}{part}", MPR[:, t, 2 * i:2 * i + 2, :], by_head(small(f"mS{t}{part}"), SEQ), 4 * t + 2 * i)
            split_ahead("mem_q", Turn(1))
            take_t("mem_v", 0, MV)
            for t in range(NT):
                take_small(f"mP{t}a", MPT[:, 0, :, tok(t)], by_head(small(f"mP{t}a")))
            split_ahead("mem_v", Turn(0))
            split_ahead("mem_v", Turn(1))
            for g in range(2):
                small_is_done(act, f"mo{g}")
                copy(YH[:, 2 * g:2 * g + 2, :], by_head(small(f"mo{g}"), SEQ), y_hi)
            norm_behind("mem_o", "norm_ffn", "up")
            act.wait_ge(block_done, FIRST["up"])
            act.dma_start(SGUW[:, :, :], A["sgu_w_2"][0].rearrange("g t s -> t g s")).then_inc(sgu_loaded, 16)
            act.dma_start(flat(BS[:, :, :]), A["sgu_b_2"][0].rearrange("g t -> (g t)").unsqueeze(0).broadcast_to([P, 4 * P])).then_inc(sgu_loaded, 16)
            post_gain_load("ffn1_post_g_2")
            pre_gain_load("ffn1_pre_g_2")

            def ffn_hi(t):
                copy(HH[:, tiles_of(t), :], UB[:, t.j % 2], h_hi)

            def up_step(t):
                u = t.j % 2
                for k, half in enumerate((UA, UB)):
                    b = t.part(k, 2)
                    acc_is_done(act, "up", b)
                    for i in range(2):
                        tile = k * FT + 2 * t.j + i
                        ins = act.activation(half[:, u, i, :], acc("up", b)[:, i * 256:(i + 1) * 256], ACT.Identity,
                                             scale=conv_tap(2, tile, t), bias=conv_bias(tile, t))
                    ins.then_inc((a_base, b_base)[k], 1)
                    if k == 1:
                        acc_is_taken(act, "up", t.part(0, 2))
                        act.activation(UA[:, u], UA[:, u], ACT.Silu).then_inc(a_act, 1)
                    split_behind("up", b)
                act.wait_ge(h_ready, t.count(lambda j: j + 1))
                ffn_hi(t)

            for j in range(2):
                up_step(Turn(j))
            repeat(act, 2, FT // 2, 2, up_step)

            def down_splits(phase):
                for j in range(COUNT[phase] - RING):
                    split_ahead(phase, Turn(j))

            down_splits("down")
            norm_behind("down", "norm_f1", "ffn1")
            pre_gain_load("mix_pre_g_2")

            def glu_steps(phase):
                def step(t):
                    a, b = t.part(0, 2), t.part(1, 2)
                    acc_is_done(act, phase, a)
                    act.activation(UA[:, t.j % 2], acc(phase, a).rearrange("p (n s) -> p n s", s=SEQ),
                                   ACT.Silu).then_inc(acc_bank(phase, a), 1)
                    split_behind(phase, a)
                    split_behind(phase, b)
                    acc_is_taken(act, phase, b)
                    ffn_hi(t)
                for j in range(2):
                    step(Turn(j))
                repeat(act, 2, FT // 2, 2, step)

            glu_steps("ffn1")
            down_splits("down1")
            post_norm_behind("down1", "norm_mix2", "mix_v")
            post_gain_load("mix_post_g_2")

            for chunk in range(2):
                split_ahead("mix_v", Turn(2 * chunk))
                acc_is_done(act, "mix_v", Turn(chunk))
                for m in range(NT):
                    act.activation(V2[:, m, chunk * 512:(chunk + 1) * 512], acc("mix_v", Turn(chunk), m),
                                   ACT.Gelu_apprx_tanh).then_inc(acc_bank("mix_v", Turn(chunk), m), 1)
                split_ahead("mix_v", Turn(2 * chunk + 1))
            for j in range(4):
                acc_is_done(act, "mix_u", Turn(j))
                act.activation(U2[:, 2 * j:2 * j + 2, :], acc("mix_u", Turn(j)).rearrange("p (n s) -> p n s", s=SEQ),
                               ACT.Gelu_apprx_tanh).then_inc(acc_bank("mix_u", Turn(j)), 1)
                split_ahead("mix_u", Turn(j))
                if j == 1:
                    for t in range(NT):
                        act.wait_ge(ln_mean, t + 1)
                        act.activation(XS[:, t, :], V2[:, t, :], ACT.Square, scale=DM ** -0.5, accum_out=LSS[:, t:t + 1]).then_inc(ln_sq, 1)
            for j in range(4):
                take_f("mix_c", j, C2[:, 2 * j:2 * j + 2, :], 1.0)
                split_ahead("mix_c", Turn(j))
                act.wait_ge(gated, j + 1)
                copy(HH[:, 2 * j:2 * j + 2, :], U2[:, 2 * j:2 * j + 2, :], gated_hi)
            act.wait_ge(gated_lo, 4)

            def branch_gates(phase, j, dst):
                acc_is_done(act, phase, Turn(j))
                act.activation(dst[:, 2 * j:2 * j + 2, :], acc(phase, Turn(j)).rearrange("p (n s) -> p n s", s=SEQ),
                               ACT.Sigmoid).then_inc(acc_bank(phase, Turn(j)), 1)
                split_ahead(phase, Turn(j))

            for j in range(4):
                branch_gates("mix_ga", j, SGA)
                act.wait_ge(pooled, j + 1)
                copy(HH[:, 8 + 2 * j:10 + 2 * j, :], C2[:, 2 * j:2 * j + 2, :], pooled_hi)
            for j in range(4):
                branch_gates("mix_gb", j, SGB)
            for g in range(4):
                acc_is_done(act, "pool", Turn(g))
                for i in range(2):
                    copy(HH[:, 8 + 2 * g + i, :], acc("pool", Turn(g))[:, i * 256:(i + 1) * 256], proj_hi,
                         col("pool_scale_2", 2 * g + i))
            split_ahead("pool", Turn(0))
            for j in range(4):
                split_ahead("mix_out", Turn(2 * j))
                split_ahead("mix_out", Turn(2 * j + 1))
                act.wait_ge(y2_ready, j + 1)
                copy(XH[:, 2 * j:2 * j + 2, :], SGA[:, 2 * j:2 * j + 2, :], y2_hi)
            pre_gain_load("ffn2_pre_g_2")
            post_norm_behind("mix_o", "norm_f2", "ffn2")
            post_gain_load("ffn2_post_g_2")
            pre_gain_load("ple_pre_g_2")
            act.dma_start(PR[:, :, :], A["p_2"][0, 0].rearrange("(t p) d -> p t d", p=P)).then_inc(p_loaded, 16)
            glu_steps("ffn2")
            small_is_done(act, "pT")
            copy(PH[:, :, :], by_head(small("pT"), SEQ), p_hi)
            down_splits("down2")

            def take_projection(m):
                for half in range(2):
                    name = f"ple.{m}{'ab'[half]}"
                    take_small(name, EP[:, m, half * 512:(half + 1) * 512], small(name))

            post_norm_behind("down2", "norm_ple", "ple_e", take_projection)
            post_gain_load("ple_post_g_2")
            split_ahead("ple_e", Turn(0))
            for chunk in range(2):
                for m in range(NT):
                    if chunk == 0:
                        acc_is_done(act, "ple_g", Turn(0))
                    else:
                        tile_is_done(act, "ple_g", m)
                    act.activation(PG[:, m, chunk * 512:(chunk + 1) * 512], acc("ple_g", Turn(chunk), m),
                                   ACT.Sigmoid).then_inc(acc_bank("ple_g", Turn(chunk), m), 1)

        @block.vector
        def _(dve):
            steps = [0]

            def link(ins):
                steps[0] += 1
                ins.then_inc(dve_step, 1)
                dve.wait_ge(dve_step, steps[0])

            def lo_half(n, half, hi_count):
                dve.wait_ge(hi_ready, hi_count)
                s, c = n % RING, half_of(half)
                dve.tensor_tensor(LO[:, s, c], RAW[:, n % RAWS, half, :], HI[:, s, c].bitcast(f32), ALU.subtract).then_inc(lo_ready[s], 1)

            def split(n):
                for half in range(2):
                    lo_half(n, half, 2 * n + half + 1)

            def split_ahead(phase, t, halves=range(2)):
                n = FIRST[phase] + t.j + RING
                if n < N_BLOCKS and n not in ON_POOL:
                    for half in halves:
                        lo_half(n, half, t.count(lambda j: 2 * (FIRST[phase] + j + RING) + half + 1))

            def split_behind(phase, t):
                if t.i is not None or t.j >= 2:
                    split_ahead(phase, t)

            def root_is_ready(name):
                dve.wait_ge(root_ready, ROOT_ORDER[name] + 1)
                return ROOT[name]

            def copy(dst, src, signal):
                dve.tensor_copy(dst, src).then_inc(signal, 1)

            def take_small(name, dst, src):
                small_is_done(dve, name)
                copy(dst, src, bank_of(name))

            def norm_scale(r, t, src, dst):
                dve.wait_ge(pre_gain_loaded, 16 * (NORMS.index(r) + 1))
                root = root_is_ready(f"{r}.{t}")
                for half in (slice(0, DM // 2), slice(DM // 2, DM)):
                    dve.scalar_tensor_tensor(out=dst[:, t, half], in0=src[:, t, half], scalar=root,
                                             in1=PRE_GAIN[:, half], op0=ALU.mult, op1=ALU.mult).then_inc(scaled, 1)

            def norm_split(r, t, hi, lo):
                for b in range(2):
                    name = f"{r}.{t}{b}"
                    dve.wait_ge(norm_hi, 4 * NORMS.index(r) + 2 * t + b + 1)
                    quarter = slice(4 * b, 4 * b + 4)
                    dve.tensor_tensor(lo[:, quarter, tok(t)], by_head(small(name)), hi[:, quarter, tok(t)].bitcast(f32),
                                      ALU.subtract).then_inc(bank_of(name), 1)

            def heads_norm(n, squares, width):
                heads = width // P
                for t in range(NT):
                    dve.wait_ge(heads_sq, 2 * n + t + 1)
                    dve.tensor_reduce(HSS[n][:, t * heads:(t + 1) * heads], by_head(squares[:, t, :]), AX, ALU.add).then_inc(heads_sums, 1)

            def heads_scale(n, rows_, heads):
                root = root_is_ready(f"heads{n}")
                for t in range(NT):
                    x = by_head(rows_(t))
                    dve.tensor_tensor(x, x, per_head(root[:, t * heads:(t + 1) * heads], P), ALU.mult).then_inc(heads_ready, 1)

            def y_split(n, names, view):
                for i, name in enumerate(names):
                    dve.wait_ge(y_hi, n + i + 1)
                    hi, lo, src = view(i)
                    dve.tensor_tensor(lo, src, hi.bitcast(f32), ALU.subtract).then_inc(bank_of(name), 1)

            for t in range(NT):
                dve.wait_ge(x_loaded[t], 16)
                norm_scale("norm_mix", t, X, XS)
            norm_split("norm_mix", 0, XH, XL)
            split(0)
            norm_split("norm_mix", 1, XH, XL)
            split(1)
            take_small("cols0", COL[0][:, :], small("cols0")[:, 0:COL_N[0]])
            small_is_done(dve, "cols1")
            dve.tensor_copy(FCONV[:, P:CONV_N], small("cols1")[:, COL_N[1]:COL_N[1] + CONV_TAIL])
            copy(COL[1][:, :], small("cols1")[:, 0:COL_N[1]], bank_of("cols1"))
            take_small("cols2", FCONV[:, 0:P], small("cols2")[:, 0:P])
            small_is_taken(dve, "cols0")
            link(dve.tensor_scalar(col("fox_qnorm"), col("fox_qnorm"), DH ** -0.5, None, ALU.mult))
            link(dve.tensor_scalar(col("mq_norm"), col("mq_norm"), DH ** -0.5, None, ALU.mult))

            for n in range(2, RING):
                split(n)
            dve.wait_ge(tiny_hi, 1)
            dve.tensor_tensor(TLO[:, :, :], TW[:, :, :], THI[:, :, :].bitcast(f32), ALU.subtract).then_inc(tiny_lo, 1)

            for j in range(6):
                dve.wait_ge(conv_base, 2 * j + 2)
                for i in range(2):
                    tile = 2 * j + i
                    u = acc("gdn", Turn(j))[:, i * 256:(i + 1) * 256]
                    for back in (1, 2, 3):
                        y = CONVF[:, tile, back:SEQ]
                        ins = dve.scalar_tensor_tensor(out=y, in0=u[:, 0:SEQ - back], scalar=col("gdn_conv", (3 - back) * 12 + tile),
                                                       in1=y, op0=ALU.mult, op1=ALU.add)
                        if i == 0 or back < 3:
                            link(ins)
                ins.then_inc(acc_bank("gdn", Turn(j)), 1)
                split_ahead("gdn", Turn(j))
            small_is_done(dve, "tiny")
            dve.wait_ge(masks_ready, 2)
            tiny = small("tiny")[:, 0:32].rearrange("p (t c) -> p t c", t=NT)[:, :, 0:12]
            dve.wait_ge(tiny_loaded, 16 * 3)
            dve.tensor_tensor(TY, tiny, every(BROW, NT), ALU.add).then_inc(bank_of("tiny"), 1)
            small_is_taken(dve, "tiny")
            link(dve.tensor_tensor(TY, TY, every(SGN, NT), ALU.mult))
            dve.scalar_tensor_tensor(out=TE, in0=TY, scalar=-1.0, in1=TY, op0=ALU.mult, op1=ALU.max).then_inc(tiny_abs, 1)
            split_ahead("sbqk", Turn(0))
            take_small("gTq1", GT[:, 1, 0, :], small("gTq1"))
            take_small("gTk1", GT[:, 1, 1, :], small("gTk1"))
            dve.wait_ge(tiny_ln, 1)
            dve.scalar_tensor_tensor(out=TS, in0=TY, scalar=0.0, in1=TE, op0=ALU.max, op1=ALU.add).then_inc(tiny_sp, 1)
            split_ahead("sbqk", Turn(1))
            dve.wait_ge(tiny_exp, 1)
            dve.tensor_tensor(NG, TS[:, :, 8:12], every(EA, NT), ALU.mult).then_inc(rates_ready, 1)
            take_small("gTv1", GT[:, 1, 2, :], small("gTv1"))
            heads_norm(0, GSQ, 2 * HW)
            rq = root_is_ready("heads0").rearrange("p (t h) -> p t h", t=NT)[:, :, 0:4]
            link(dve.tensor_scalar(rq, rq, DH ** -0.5, None, ALU.mult))
            heads_scale(0, lambda t: flat(GT[:, t, 0:2, :]), 8)
            small_is_done(dve, "gcol")
            link(dve.tensor_copy(NC, small("gcol")[:, 0:8].rearrange("p (t c) -> p t c", t=NT)))
            dve.tensor_tensor(KD, NC[:, 0, :], small("gcol")[:, 8:12], ALU.subtract).then_inc(bank_of("gcol"), 1)
            for t in range(NT):
                small_is_done(dve, f"grow{t}")
                for h in range(HEADS):
                    row = small(f"grow{t}")[:, h * P:(h + 1) * P]
                    dve.tensor_scalar(MA[:, t, h, :], row, NC[:, t, h:h + 1], 0.0, ALU.subtract, ALU.min)
                    ins = dve.tensor_scalar(MB[:, t, h, :], row, NC[:, t, h:h + 1], 0.0, ALU.subtract, ALU.max)
                ins.then_inc(bank_of(f"grow{t}"), 1)
            split_ahead("sbqk", Turn(2))
            split_ahead("sbqk", Turn(3))
            take_small("gFq1", QKF[:, 0:4, tok(1)], by_head(small("gFq1")))
            take_small("gFk1", QKF[:, 4:8, tok(1)], by_head(small("gFk1")))
            for t in range(NT):
                dve.wait_ge(decay_ready, 2 * t + 2)
                link(dve.tensor_tensor(MB[:, t], MB[:, t], every(TRI, HEADS), ALU.mult))
            split_ahead("sbv", Turn(0))
            for t in range(NT):
                small_is_done(dve, f"kk{t}")
                for h in range(HEADS):
                    ins = dve.scalar_tensor_tensor(out=DL[:, t, h, :], in0=small(f"kk{t}")[:, h * P:(h + 1) * P],
                                                   scalar=BETA[:, t, h:h + 1], in1=MA[:, t, h, :], op0=ALU.mult, op1=ALU.mult)
                ins.then_inc(bank_of(f"kk{t}"), 1)
            for t in range(NT):
                small_is_done(dve, f"kq{t}")
                dve.tensor_tensor(MAT[:, t], by_head(small(f"kq{t}")), MB[:, t], ALU.mult).then_inc(bank_of(f"kq{t}"), 1)
            split_ahead("sbv", Turn(1))
            for h in range(HEADS):
                small_is_taken(dve, f"z{h}")
            dve.scalar_tensor_tensor(out=SP_[:, :, :], in0=Z[:, :, :], scalar=-1.0, in1=Z[:, :, :], op0=ALU.mult, op1=ALU.max).then_inc(keep_abs, 1)

            def first_factor(t):
                name = f"Dt{t}"
                small_is_done(dve, name)
                dve.tensor_copy(MB[:, t], by_head(small(name)))
                dve.tensor_tensor(MP[:, t], every(IDENT[:, :], HEADS), by_head(small(name)), ALU.subtract).then_inc(bank_of(name), 1)

            for t in range(NT):
                first_factor(t)
            split_ahead("foxqk", Turn(0))
            take_small("D2_1", MC[:, 1], by_head(small("D2_1")))
            take_small("D2t_1", ME[:, 1], by_head(small("D2t_1")))
            dve.wait_ge(keep_ln, 1)
            link(dve.scalar_tensor_tensor(out=SP_[:, :, :], in0=Z[:, :, :], scalar=0.0, in1=SP_[:, :, :], op0=ALU.max, op1=ALU.add))
            link(dve.tensor_tensor(SP_[:, :, 0:P], SP_[:, :, 0:P], every(BEFORE[:, :], HEADS), ALU.mult))
            dve.tensor_tensor(SP_[:, :, SEQ:SEQ + P], SP_[:, :, SEQ:SEQ + P], every(BEFORE[:, :], HEADS), ALU.mult).then_inc(keep_ready, 1)
            split_ahead("foxqk", Turn(1))

            def factor(n, t):
                name = f"P{n}_{t}"
                small_is_done(dve, name)
                dve.tensor_tensor(MP[:, t], MP[:, t], by_head(small(name)), ALU.add).then_inc(bank_of(name), 1)

            for t in range(NT):
                factor(2, t)
            take_small("D4_1", MA[:, 1], by_head(small("D4_1")))
            split_ahead("foxqk", Turn(2))
            take_small("D4t_1", MB[:, 1], by_head(small("D4t_1")))

            def stick_arg(h):
                small_is_done(dve, f"rc{h}")
                dve.tensor_tensor(Z[:, h, :], Z[:, h, :], small(f"rc{h}")[:, 0:384], ALU.subtract).then_inc(bank_of(f"rc{h}"), 1)

            for h in range(2):
                stick_arg(h)
            split_ahead("foxqk", Turn(3))
            for h in range(2, 4):
                stick_arg(h)
            for t in range(NT):
                factor(4, t)
            heads_norm(1, XS, 2 * HW)
            heads_scale(1, lambda t: HT[:, t, :], 8)
            split_ahead("foxv", Turn(0))
            take_small("D8_1", MC[:, 1], by_head(small("D8_1")))
            split_ahead("foxv", Turn(1))
            for t in range(NT):
                factor(8, t)
            y_split(0, ("so0", "so1"), lambda g: (YH[:, 2 * g:2 * g + 2, :], YL[:, 2 * g:2 * g + 2, :], by_head(small(f"so{g}"), SEQ)))
            split_ahead("gate_c", Turn(0))
            take_small("T16_1", ME[:, 1], by_head(small("T16_1")))
            split_ahead("gate_c", Turn(1))
            for i, (part, gain) in enumerate((("q", "fox_qnorm"), ("k", "fox_knorm"))):
                name = f"fT{part}1"
                small_is_done(dve, name)
                dve.tensor_scalar(FQK[:, 4 * i:4 * i + 4, tok(1)], by_head(small(name)), col(gain), None, ALU.mult).then_inc(bank_of(name), 1)
            split_ahead("gate_c", Turn(2))
            take_small("Z16_1", MB[:, 1], by_head(small("Z16_1")))
            split_ahead("gate_c", Turn(3))

            def join(b, both=True):
                for t in range(NT):
                    name = f"Tt{b}_{t}"
                    small_is_done(dve, name)
                    dve.tensor_tensor(MP[:, t], MP[:, t], by_head(small(name)), ALU.subtract).then_inc(bank_of(name), 1)
                for t in range(NT if both else 0):
                    name = f"T{b}_{t}"
                    small_is_done(dve, name)
                    dve.tensor_tensor(ME[:, t], ME[:, t], by_head(small(name)), ALU.subtract).then_inc(bank_of(name), 1)

            def row_maxima(name, scores, first):
                small_is_done(dve, name)
                m = MX[:, first:first + scores.shape[1]]
                link(dve.tensor_reduce(m, scores, AX, ALU.max))
                dve.tensor_scalar(m, m, -1.0, None, ALU.mult).then_inc(row_max, 1)

            def normalise(names, rows_, first):
                for n in names:
                    small_is_taken(dve, n)
                s = RSUM[:, first:first + rows_.shape[1]]
                link(dve.reciprocal(s, s))
                dve.tensor_tensor(rows_, rows_, per_head(s, rows_.shape[2]), ALU.mult).then_inc(probs_ready, 1)

            def mix(g, j):
                phase = f"out_{g}"
                acc_is_done(dve, phase, Turn(j))
                for i in range(2 * j, 2 * j + 2):
                    acc_is_taken(dve, f"gate_{g}", Turn(i))
                for k in range(2):
                    tiles = slice(4 * j + 2 * k, 4 * j + 2 * k + 2)
                    src = acc(phase, Turn(j), k).rearrange("p (n s) -> p n s", s=SEQ)
                    dst = MIX if g == "c" else G
                    dve.tensor_tensor(dst[:, tiles, :], src, G[:, tiles, :], ALU.mult).then_inc(acc_bank(phase, Turn(j), k), 1)
                if g == "c":
                    return
                for k in range(2):
                    tiles = slice(4 * j + 2 * k, 4 * j + 2 * k + 2)
                    acc_is_taken(dve, phase, Turn(j), k)
                    ins = dve.tensor_tensor(MIX[:, tiles, :], MIX[:, tiles, :], G[:, tiles, :], ALU.add)
                    ins.then_inc(mixed_ready if g == "b" else dve_mix, 1)

            join(32)
            mix("c", 0)
            split_ahead("out_c", Turn(0))
            row_maxima("fS0", by_head(small("fS0")), 0)
            row_maxima("fS1a", by_head(small("fS1a"), SEQ), 4)
            row_maxima("fS1b", by_head(small("fS1b"), SEQ), 6)
            mix("c", 1)
            split_ahead("out_c", Turn(1))
            take_small("Z32_1", MB[:, 1], by_head(small("Z32_1")))
            normalise(("fS0",), FP0[:, :, :], 0)
            normalise(("fS1a", "fS1b"), FP1[:, :, :], 4)
            split_ahead("gate_a", Turn(0))
            join(64)
            dve.wait_ge(rates_exp, 1)
            dve.tensor_tensor(by_head(GT[:, 0, 0, :]), by_head(GT[:, 0, 2, :]), per_head(BETA[:, 0, :], P), ALU.mult).then_inc(rhs_ready, 1)
            dve.tensor_tensor(by_head(GT[:, 0, 1, :]), by_head(GT[:, 0, 1, :]), per_head(KD, P), ALU.mult).then_inc(rhs_ready, 1)
            split_ahead("gate_a", Turn(1))
            take_small("fP1b", FPT1[:, 1], by_head(small("fP1b")))
            split_ahead("gate_a", Turn(2))
            y_split(2, ("fo0", "fo1"), lambda t: (YH[:, :, tok(t)], YL[:, :, tok(t)], by_head(small(f"fo{t}"))))
            take_small("Z64_1", MB[:, 1], by_head(small("Z64_1")))
            split_ahead("gate_a", Turn(3))
            join(128, both=False)
            mix("a", 0)
            split_ahead("out_a", Turn(0))
            mix("a", 1)
            split_ahead("out_a", Turn(1))
            split_ahead("gz", Turn(0))
            small_is_done(dve, "kS")
            dve.tensor_tensor(MB[:, 0], by_head(small("kS")), per_head(EGC[:, 1, :], P), ALU.mult).then_inc(bank_of("kS"), 1)
            small_is_done(dve, "qS")
            dve.tensor_tensor(MB[:, 1], by_head(small("qS")), per_head(EGC[:, 1, :], P), ALU.mult).then_inc(bank_of("qS"), 1)
            small_is_taken(dve, "kS")
            link(dve.tensor_tensor(MB[:, 0], by_head(GT[:, 1, 2, :]), MB[:, 0], ALU.subtract))
            dve.tensor_tensor(by_head(GT[:, 1, 2, :]), MB[:, 0], per_head(BETA[:, 1, :], P), ALU.mult).then_inc(rhs_ready, 1)
            split_ahead("gz", Turn(1))
            split_ahead("gate_b", Turn(0))
            small_is_done(dve, "o1")
            small_is_taken(dve, "qS")
            dve.tensor_tensor(by_head(DO[:, 1, :]), by_head(small("o1")), MB[:, 1], ALU.add).then_inc(bank_of("o1"), 1)
            heads_norm(2, OSQ, HW)
            heads_scale(2, lambda t: DO[:, t, :], 4)
            split_ahead("gate_b", Turn(1))
            split_ahead("gate_b", Turn(2))
            for j in range(2):
                acc_is_taken(dve, "gz", Turn(j))
            for t in range(NT):
                name = f"yT{t}"
                small_is_done(dve, name)
                dve.scalar_tensor_tensor(out=YB[:, :, tok(t)], in0=by_head(small(name)), scalar=col("gdn_onorm"),
                                         in1=GZS[:, :, tok(t)], op0=ALU.mult, op1=ALU.mult).then_inc(bank_of(name), 1)
            for t in range(NT):
                dve.wait_ge(y_hi, 4 + t + 1)
                dve.tensor_tensor(YL[:, :, tok(t)], YB[:, :, tok(t)], YH[:, :, tok(t)].bitcast(f32), ALU.subtract).then_inc(y_lo, 1)
            split_ahead("gate_b", Turn(3))
            for t in range(NT):
                norm_scale("norm_mem", t, MEM, MEM)
            for j in range(2):
                dve.wait_ge(dve_mix, 4)
                mix("b", j)
                for k in range(2):
                    i = 2 * j + k
                    dve.wait_ge(mixed_hi, i + 1)
                    dve.tensor_tensor(XL[:, 2 * i:2 * i + 2, :], MIX[:, 2 * i:2 * i + 2, :], XH[:, 2 * i:2 * i + 2, :].bitcast(f32),
                                      ALU.subtract).then_inc(mixed_lo, 1)
                split_ahead("out_b", Turn(j))
                if j == 0:
                    for t in range(NT):
                        norm_split("norm_mem", t, MH, MLO)

            def add_residual(phase, m):
                tile_is_done(dve, phase, m)
                for k in range(2):
                    part = X[:, m, k * 512:(k + 1) * 512]
                    dve.tensor_tensor(part, part, acc(phase, Turn(0), 2 * m + k), ALU.add).then_inc(acc_bank(phase, Turn(0), 2 * m + k), 1)
                acc_is_taken(dve, phase, Turn(0), 2 * m)
                acc_is_taken(dve, phase, Turn(0), 2 * m + 1)

            def opening_splits(phase):
                if phase in F_OPEN:
                    split_ahead(phase, Turn(0))
                    width = (F_OPEN[phase] - 2) * 256
                    take_small(f"{phase}.11", OPENED[:, 1, 512:512 + width], small(f"{phase}.11")[:, 0:width])
                    split_ahead(phase, Turn(1))

            def norm_behind(phase, r, behind):
                n = COUNT[phase]
                if n >= RING:
                    split_ahead(phase, Turn(n - 4))
                add_residual(phase, 0)
                norm_scale(r, 0, X, XS)
                if n >= RING:
                    split_ahead(phase, Turn(n - 3))
                norm_split(r, 0, XH, XL)
                add_residual(phase, 1)
                split_ahead(phase, Turn(n - 2))
                norm_scale(r, 1, X, XS)
                norm_split(r, 1, XH, XL)
                split_ahead(phase, Turn(n - 1))
                opening_splits(behind)

            dve.wait_ge(x_again, 16)
            norm_behind("w_out", "norm_xq", "mem_k")
            heads_norm(3, MSQ, HW)
            heads_scale(3, lambda t: MK[:, t, :], 4)
            split_ahead("mem_k", Turn(0))

            def take_scaled(name, dst, gain):
                small_is_done(dve, name)
                dve.tensor_scalar(dst, by_head(small(name)), col(gain), None, ALU.mult).then_inc(bank_of(name), 1)

            heads_norm(4, MSQ, HW)
            heads_scale(4, lambda t: MQ[:, t, :], 4)
            take_scaled("mkT1", MKT[:, :, tok(1)], "mk_norm")
            split_ahead("mem_k", Turn(1))
            take_scaled("mqT1", MQT[:, :, tok(1)], "mq_norm")
            for t in range(NT):
                for i, part in enumerate("ab"):
                    row_maxima(f"mS{t}{part}", by_head(small(f"mS{t}{part}"), SEQ), 4 * t + 2 * i)
            for t in range(NT):
                for i, part in enumerate("ab"):
                    normalise((f"mS{t}{part}",), MPR[:, t, 2 * i:2 * i + 2, :], 4 * t + 2 * i)
            for t in range(NT):
                take_small(f"mP{t}b", MPT[:, 1, :, tok(t)], by_head(small(f"mP{t}b")))
            y_split(6, ("mo0", "mo1"), lambda g: (YH[:, 2 * g:2 * g + 2, :], YL[:, 2 * g:2 * g + 2, :], by_head(small(f"mo{g}"), SEQ)))
            split_ahead("mem_v", Turn(1))
            norm_behind("mem_o", "norm_ffn", "up")

            def hidden_lo(t, pairs):
                dve.wait_ge(h_hi, t.count(lambda j: pairs + j + 1))
                dve.tensor_tensor(HL[:, tiles_of(t), :], UB[:, t.j % 2], HH[:, tiles_of(t), :].bitcast(f32),
                                  ALU.subtract).then_inc(h_lo, 1)

            def up_step(t):
                u = t.j % 2
                for k, half in enumerate((UA, UB)):
                    b = t.part(k, 2)
                    dve.wait_ge((a_base, b_base)[k], t.count(lambda j: j + 1))
                    for back in (1, 2):
                        for i in range(2):
                            if back == 2:
                                dve.wait_ge(tap_done, t.count(lambda j: 4 * j + 2 * k + i + 1))
                            y = half[:, u, i, back:SEQ]
                            ins = dve.scalar_tensor_tensor(out=y, in0=acc("up", b)[:, i * 256:i * 256 + SEQ - back],
                                                           scalar=conv_tap(2 - back, k * FT + 2 * t.j + i, t), in1=y,
                                                           op0=ALU.mult, op1=ALU.add)
                            if back == 1:
                                ins.then_inc(tap_done, 1)
                    ins.then_inc(acc_bank("up", b), 1)
                    if k == 1:
                        dve.wait_ge(a_act, t.count(lambda j: j + 1))
                        acc_is_taken(dve, "up", b)
                        dve.tensor_tensor(UB[:, u], UB[:, u], UA[:, u], ALU.mult).then_inc(h_ready, 1)
                    split_behind("up", b)
                hidden_lo(t, 0)

            for j in range(2):
                up_step(Turn(j))
            repeat(dve, 2, FT // 2, 2, up_step)

            def down_splits(phase):
                for j in range(COUNT[phase] - RING):
                    split_ahead(phase, Turn(j))

            down_splits("down")
            norm_behind("down", "norm_f1", "ffn1")

            def glu_steps(phase, pairs):
                def step(t):
                    a, b = t.part(0, 2), t.part(1, 2)
                    split_behind(phase, a)
                    acc_is_done(dve, phase, b)
                    acc_is_taken(dve, phase, a)
                    dve.tensor_tensor(UB[:, t.j % 2], acc(phase, b).rearrange("p (n s) -> p n s", s=SEQ), UA[:, t.j % 2],
                                      ALU.mult).then_inc(acc_bank(phase, b), 1)
                    split_behind(phase, b)
                    hidden_lo(t, pairs)
                for j in range(2):
                    step(Turn(j))
                repeat(dve, 2, FT // 2, 2, step)

            def post_norm(n, phase, factor, m):
                root = root_is_ready(f"{phase}.{m}")
                dve.wait_ge(post_gain_loaded, 16 * (n + 1))
                dve.scalar_tensor_tensor(out=XS[:, m, :], in0=flat(ACCP[:, 2 * m:2 * m + 2, :]), scalar=root,
                                         in1=POST_GAIN[:, :], op0=ALU.mult, op1=ALU.mult).then_inc(acc_bank(phase, Turn(0), 2 * m), 1)
                acc_is_taken(dve, phase, Turn(0), 2 * m)
                dve.scalar_tensor_tensor(out=X[:, m, :], in0=XS[:, m, :], scalar=factor, in1=X[:, m, :],
                                         op0=ALU.mult, op1=ALU.add).then_inc(acc_bank(phase, Turn(0), 2 * m + 1), 1)
                acc_is_taken(dve, phase, Turn(0), 2 * m + 1)

            def post_norm_behind(n, phase, r, factor, behind):
                blocks = COUNT[phase]
                post_norm(n, phase, factor, 0)
                split_ahead(phase, Turn(blocks - 4))
                norm_scale(r, 0, X, XS)
                split_ahead(phase, Turn(blocks - 3), (0,))
                norm_split(r, 0, XH, XL)
                split_ahead(phase, Turn(blocks - 3), (1,))
                split_ahead(phase, Turn(blocks - 2), (0,))
                post_norm(n, phase, factor, 1)
                split_ahead(phase, Turn(blocks - 1), (0,))
                norm_scale(r, 1, X, XS)
                split_ahead(phase, Turn(blocks - 1), (1,))
                norm_split(r, 1, XH, XL)
                opening_splits(behind)

            glu_steps("ffn1", FT // 2)
            down_splits("down1")
            post_norm_behind(0, "down1", "norm_mix2", 0.5, "mix_v")

            for j in range(4):
                split_ahead("mix_v", Turn(j))
            small_is_done(dve, "sguw")
            dve.tensor_tensor(WST[:, :, :], by_head(small("sguw")), every(TRI, 4), ALU.mult).then_inc(bank_of("sguw"), 1)
            split_ahead("mix_u", Turn(0))
            for t in range(NT):
                for chunk in range(2):
                    acc_is_taken(dve, "mix_v", Turn(chunk), t)
                link(dve.tensor_reduce(MEAN[:, t:t + 1], V2[:, t, :], AX, ALU.add))
                link(dve.tensor_scalar(MEAN[:, t:t + 1], MEAN[:, t:t + 1], 1.0 / DM, None, ALU.mult))
                dve.tensor_scalar(V2[:, t, :], V2[:, t, :], MEAN[:, t:t + 1], None, ALU.subtract).then_inc(ln_mean, 1)
            split_ahead("mix_u", Turn(1))
            root = root_is_ready("layer")
            for t in range(NT):
                dve.tensor_scalar(V2[:, t, :], V2[:, t, :], root[:, t:t + 1], None, ALU.mult).then_inc(ln_ready, 1)
            split_ahead("mix_u", Turn(2))
            split_ahead("mix_u", Turn(3))
            dve.wait_ge(sgu_loaded, 32)
            for g in range(4):
                split_ahead("mix_c", Turn(g))
                name = f"sgu{g}"
                small_is_done(dve, name)
                for i in range(2):
                    d = 2 * g + i
                    ins = dve.scalar_tensor_tensor(out=by_head(G[:, d, :]), in0=by_head(small(name)[:, i * SEQ:(i + 1) * SEQ]),
                                                   scalar=col("sgu_norm_g_2", d), in1=every(BS[:, g, :], NT),
                                                   op0=ALU.mult, op1=ALU.add)
                ins.then_inc(bank_of(name), 1)
                small_is_taken(dve, name)
                acc_is_taken(dve, "mix_u", Turn(g))
                pair = slice(2 * g, 2 * g + 2)
                dve.tensor_tensor(U2[:, pair, :], U2[:, pair, :], G[:, pair, :], ALU.mult).then_inc(gated, 1)
                dve.wait_ge(gated_hi, g + 1)
                dve.tensor_tensor(HL[:, pair, :], U2[:, pair, :], HH[:, pair, :].bitcast(f32), ALU.subtract).then_inc(gated_lo, 1)
            for g, (sums, size) in enumerate(zip((S2A[:, :, :], S4[:, 0:2, :], S8[:, 0:2, :], S16[:, :, :]), POOL_WINDOWS)):
                split_ahead("mix_ga", Turn(g))
                dve.wait_ge(windows_ready, (2, 3, 4, 5)[g])
                link(dve.tensor_tensor(sums[:, :, 0:16], sums[:, :, 0:16], every(INV16[:, g, :], 2), ALU.mult))
                pair, dst = slice(2 * g, 2 * g + 2), slice(8 + 2 * g, 10 + 2 * g)
                dve.scalar_tensor_tensor(out=C2[:, pair, :], in0=sums, scalar=1.0 / size, in1=C2[:, pair, :],
                                         op0=ALU.mult, op1=ALU.subtract).then_inc(pooled, 1)
                dve.wait_ge(pooled_hi, g + 1)
                dve.tensor_tensor(HL[:, dst, :], C2[:, pair, :], HH[:, dst, :].bitcast(f32), ALU.subtract).then_inc(pooled_lo, 1)
            for j in range(4):
                split_ahead("mix_gb", Turn(j))
            for g in range(4):
                dve.wait_ge(proj_hi, 2 * g + 2)
                for i in range(2):
                    d = 2 * g + i
                    ins = dve.scalar_tensor_tensor(out=HL[:, 8 + d, :], in0=acc("pool", Turn(g))[:, i * 256:(i + 1) * 256],
                                                   scalar=col("pool_scale_2", d), in1=HH[:, 8 + d, :].bitcast(f32),
                                                   op0=ALU.mult, op1=ALU.subtract)
                ins.then_inc(acc_bank("pool", Turn(g)), 1)
            split_ahead("pool", Turn(0))
            for j in range(4):
                pair = slice(2 * j, 2 * j + 2)
                for k, (gate, dst) in enumerate((("mix_ga", SGA), ("mix_gb", SGB))):
                    t = Turn(2 * j + k)
                    acc_is_taken(dve, gate, Turn(j))
                    acc_is_done(dve, "mix_out", t)
                    dve.tensor_tensor(dst[:, pair, :], acc("mix_out", t).rearrange("p (n s) -> p n s", s=SEQ), dst[:, pair, :],
                                      ALU.mult).then_inc(acc_bank("mix_out", t), 1)
                    split_ahead("mix_out", t)
                for k in range(2):
                    acc_is_taken(dve, "mix_out", Turn(2 * j + k))
                dve.tensor_tensor(SGA[:, pair, :], SGA[:, pair, :], SGB[:, pair, :], ALU.add).then_inc(y2_ready, 1)
                dve.wait_ge(y2_hi, j + 1)
                dve.tensor_tensor(XL[:, pair, :], SGA[:, pair, :], XH[:, pair, :].bitcast(f32), ALU.subtract).then_inc(y2_lo, 1)
            post_norm_behind(1, "mix_o", "norm_f2", 1.0, "ffn2")

            glu_steps("ffn2", 2 * (FT // 2))
            dve.wait_ge(p_hi, 1)
            dve.tensor_tensor(PL[:, :, :], by_head(small("pT"), SEQ), PH[:, :, :].bitcast(f32), ALU.subtract).then_inc(bank_of("pT"), 1)
            down_splits("down2")
            post_norm_behind(2, "down2", "norm_ple", 0.5, "ple_e")
            split_ahead("ple_e", Turn(0))

            def gated_half(t, half):
                part = slice(half * 512, (half + 1) * 512)
                small_is_taken(dve, f"ple.{t}{'ab'[half]}")
                acc_is_taken(dve, "ple_g", Turn(half), t)
                link(dve.tensor_tensor(PG[:, t, part], PG[:, t, part], EP[:, t, part], ALU.mult))
                dve.tensor_tensor_reduce(out=EP[:, t, part], in0=PG[:, t, part], in1=PG[:, t, part], scale=1.0 / DM, scalar=0.0,
                                         op0=ALU.mult, op1=ALU.add,
                                         accum_out=POST[:, 2 * t + half:2 * t + half + 1]).then_inc(last_sq, 1)

            def gained_half(t, half):
                part = slice(half * 512, (half + 1) * 512)
                link(dve.tensor_tensor(PG[:, t, part], PG[:, t, part], POST_GAIN[:, part], ALU.mult))

            def add_gated(t):
                root = root_is_ready(f"last.{t}")
                for half in range(2):
                    part = slice(half * 512, (half + 1) * 512)
                    dve.scalar_tensor_tensor(out=X[:, t, part], in0=PG[:, t, part], scalar=root, in1=X[:, t, part],
                                             op0=ALU.mult, op1=ALU.add).then_inc(out_ready, 1)

            for t in range(NT):
                gated_half(t, 0)
            dve.wait_ge(post_gain_loaded, 16 * 4)
            for t in range(NT):
                gained_half(t, 0)
            gated_half(0, 1)
            gained_half(0, 1)
            gated_half(1, 1)
            add_gated(0)
            gained_half(1, 1)
            add_gated(1)


def kernel(**inputs):
    import numpy as np
    import concourse.bacc as bacc
    from concourse.bass_utils import run_bass_kernel_spmd

    nc = bacc.Bacc("TRN2", target_bir_lowering=False, num_devices=1)
    arrays, args = {}, {}
    for name, value in inputs.items():
        a = np.ascontiguousarray(value)
        arrays[f"in_{name}_dram"] = a
        args[name] = nc.dram_tensor(f"in_{name}_dram", a.shape, mybir.dt.from_np(a.dtype), kind="ExternalInput").ap()
    out = nc.dram_tensor("out_0_dram", (1, SEQ, DM), mybir.dt.float32, kind="ExternalOutput").ap()
    build(nc, args, out)
    r = run_bass_kernel_spmd(nc, [arrays], core_ids=[0])
    return r.results[0]["out_0_dram"]
```
